# Optimizing a Trainium2 kernel written in Bass

```python
import jax, jax.numpy as jnp
from jax import lax
import numpy as np
import math
import jax
import jax.numpy as jnp

D_MODEL = 1024
BATCH = 1
SEQ = 256
DEPTH = 2

HEAD_DIM = 64
MIX_WIDTH = D_MODEL
FOX_HEADS = MIX_WIDTH // (4 * HEAD_DIM)
MOBA_HEADS = MIX_WIDTH // (4 * HEAD_DIM)
RWKV_HEADS = MIX_WIDTH // (2 * HEAD_DIM)
FOX_WIDTH = FOX_HEADS * HEAD_DIM
MOBA_WIDTH = MOBA_HEADS * HEAD_DIM
RWKV_WIDTH = RWKV_HEADS * HEAD_DIM
RWKV_DECAY_LORA = 64
RWKV_ICLR_LORA = 64
RWKV_GATE_LORA = 160
RWKV_GN_EPS = 64e-5
FOX_IN = 3 * FOX_WIDTH + FOX_HEADS
MOBA_IN = 3 * MOBA_WIDTH
RWKV_IN = 3 * RWKV_WIDTH + RWKV_DECAY_LORA + RWKV_ICLR_LORA + RWKV_GATE_LORA
IN_WIDTH = FOX_IN + MOBA_IN + RWKV_IN
FOX_QBLOCK = 128
MOBA_BLOCK = 256
MOBA_TOPK = 3
MOBA_QCHUNK = 32
ROPE_THETA = 500000.0
ROPE_DIM = HEAD_DIM // 4
FFN_DIM = 2816
MEM_LEN = 256
XATTN_HEADS = 4
XATTN_HEAD_DIM = 128
XATTN_WIDTH = XATTN_HEADS * XATTN_HEAD_DIM
NORM_EPS = 1e-6


def rms_norm(t, g):
    tf = t.astype(jnp.float32)
    y = tf * lax.rsqrt(jnp.mean(tf * tf, axis=-1, keepdims=True) + NORM_EPS)
    return (y * g).astype(t.dtype)

def swiglu(h, w_in, w_out):
    gate, up = jnp.split(h @ w_in, 2, axis=-1)
    return (jax.nn.silu(gate) * up) @ w_out

def split_heads(t, n_heads):
    B, S, _ = t.shape
    return t.reshape(B, S, n_heads, HEAD_DIM).transpose(0, 2, 1, 3)

def merge_heads(t):
    B, H, S, d = t.shape
    return t.transpose(0, 2, 1, 3).reshape(B, S, H * d)

def rope_tables(positions):
    inv_freq = ROPE_THETA ** (-jnp.arange(0, ROPE_DIM, 2, dtype=jnp.float32) / ROPE_DIM)
    ang = positions.astype(jnp.float32)[..., None] * inv_freq
    return jnp.cos(ang), jnp.sin(ang)

def apply_partial_rope(t, cos, sin):
    half = ROPE_DIM // 2
    x1, x2, rest = t[..., :half], t[..., half:ROPE_DIM], t[..., ROPE_DIM:]
    c, s = cos[:, None], sin[:, None]
    out = jnp.concatenate([x1 * c - x2 * s, x2 * c + x1 * s, rest.astype(jnp.float32)], axis=-1)
    return out.astype(t.dtype)

def forgetting_attention(q, k, v, log_f):
    B, H, S, d = q.shape
    c = jnp.cumsum(log_f, axis=-1)
    n_qb = S // FOX_QBLOCK
    q_blocks = q.reshape(B, H, n_qb, FOX_QBLOCK, d).transpose(2, 0, 1, 3, 4)
    c_blocks = c.reshape(B, H, n_qb, FOX_QBLOCK).transpose(2, 0, 1, 3)
    k_pos = jnp.arange(S)
    scale = d ** -0.5

    def block(args):
        i, q_i, c_i = args
        s = jnp.einsum('bhqd,bhkd->bhqk', q_i, k).astype(jnp.float32) * scale
        s = s + c_i[..., None] - c[:, :, None, :]
        q_pos = i * FOX_QBLOCK + jnp.arange(FOX_QBLOCK)
        s = jnp.where(k_pos[None, :] <= q_pos[:, None], s, -jnp.inf)
        p = jax.nn.softmax(s, axis=-1).astype(v.dtype)
        return jnp.einsum('bhqk,bhkd->bhqd', p, v)

    out = lax.map(block, (jnp.arange(n_qb), q_blocks, c_blocks))
    return out.transpose(1, 2, 0, 3, 4).reshape(B, H, S, d)

def fox_mixer(z, f_bias, q_gain, k_gain):
    q, k, v, f = jnp.split(z, [FOX_WIDTH, 2 * FOX_WIDTH, 3 * FOX_WIDTH], axis=-1)
    q = rms_norm(split_heads(q, FOX_HEADS), q_gain)
    k = rms_norm(split_heads(k, FOX_HEADS), k_gain)
    v = split_heads(v, FOX_HEADS)
    log_f = jax.nn.log_sigmoid(f.astype(jnp.float32) + f_bias).transpose(0, 2, 1)
    return merge_heads(forgetting_attention(q, k, v, log_f))

def moba_attention(q, k, v):
    B, H, S, d = q.shape
    s_pad = -(-S // MOBA_BLOCK) * MOBA_BLOCK
    pad = ((0, 0), (0, 0), (0, s_pad - S), (0, 0))
    k_pad = jnp.pad(k, pad)
    v_pad = jnp.pad(v, pad)
    n_blk = s_pad // MOBA_BLOCK
    top_k = min(MOBA_TOPK, n_blk)
    k_blk = k_pad.reshape(B, H, n_blk, MOBA_BLOCK, d)
    v_blk = v_pad.reshape(B, H, n_blk, MOBA_BLOCK, d)
    k_mean = jnp.mean(k_blk.astype(jnp.float32), axis=3)
    n_chunk = S // MOBA_QCHUNK
    q_chunks = q.reshape(B, H, n_chunk, MOBA_QCHUNK, d).transpose(2, 0, 1, 3, 4)
    b_idx = jnp.arange(B)[:, None, None, None]
    h_idx = jnp.arange(H)[None, :, None, None]
    blk_ids = jnp.arange(n_blk)
    scale = d ** -0.5

    def chunk(args):
        i, q_i = args
        q_start = i * MOBA_QCHUNK
        q_blk = q_start // MOBA_BLOCK
        gate = jnp.einsum('bhqd,bhnd->bhqn', q_i.astype(jnp.float32), k_mean)
        gate = jnp.where(blk_ids < q_blk, gate, -jnp.inf)
        _, sel = lax.top_k(gate, top_k)
        valid = sel < q_blk
        k_sel = k_blk[b_idx, h_idx, sel]
        v_sel = v_blk[b_idx, h_idx, sel]
        s_sel = jnp.einsum('bhqd,bhqnkd->bhqnk', q_i, k_sel).astype(jnp.float32) * scale
        s_sel = jnp.where(valid[..., None], s_sel, -jnp.inf)
        s_sel = s_sel.reshape(B, H, MOBA_QCHUNK, top_k * MOBA_BLOCK)
        blk_start = q_blk * MOBA_BLOCK
        k_own = lax.dynamic_slice_in_dim(k_pad, blk_start, MOBA_BLOCK, axis=2)
        v_own = lax.dynamic_slice_in_dim(v_pad, blk_start, MOBA_BLOCK, axis=2)
        s_own = jnp.einsum('bhqd,bhkd->bhqk', q_i, k_own).astype(jnp.float32) * scale
        q_pos = q_start + jnp.arange(MOBA_QCHUNK)
        k_pos = blk_start + jnp.arange(MOBA_BLOCK)
        s_own = jnp.where(k_pos[None, :] <= q_pos[:, None], s_own, -jnp.inf)
        p = jax.nn.softmax(jnp.concatenate([s_sel, s_own], axis=-1), axis=-1).astype(v.dtype)
        p_sel = p[..., :top_k * MOBA_BLOCK].reshape(B, H, MOBA_QCHUNK, top_k, MOBA_BLOCK)
        p_own = p[..., top_k * MOBA_BLOCK:]
        return (jnp.einsum('bhqnk,bhqnkd->bhqd', p_sel, v_sel)
                + jnp.einsum('bhqk,bhkd->bhqd', p_own, v_own))

    out = lax.map(chunk, (jnp.arange(n_chunk), q_chunks))
    return out.transpose(1, 2, 0, 3, 4).reshape(B, H, S, d)

def moba_mixer(z, cos, sin, q_gain, k_gain):
    q, k, v = jnp.split(z, [MOBA_WIDTH, 2 * MOBA_WIDTH], axis=-1)
    q = apply_partial_rope(rms_norm(split_heads(q, MOBA_HEADS), q_gain), cos, sin)
    k = apply_partial_rope(rms_norm(split_heads(k, MOBA_HEADS), k_gain), cos, sin)
    v = split_heads(v, MOBA_HEADS)
    return merge_heads(moba_attention(q, k, v))

def rwkv7_mixer(z, mu, w0, w2, a0, a2, g2, k_k, k_a, r_k, ln_w, ln_b):
    B, S, _ = z.shape
    zf = z.astype(jnp.float32)
    z_prev = jnp.pad(zf, ((0, 0), (1, 0), (0, 0)))[:, :S]
    zf = zf + (z_prev - zf) * mu
    W = RWKV_WIDTH
    r, k, v, w_lo, a_lo, g_lo = jnp.split(
        zf, [W, 2 * W, 3 * W, 3 * W + RWKV_DECAY_LORA, 3 * W + RWKV_DECAY_LORA + RWKV_ICLR_LORA], axis=-1)
    w_raw = w0 + jnp.tanh(w_lo) @ w2
    decay = jnp.exp(-jnp.exp(-jax.nn.softplus(-w_raw) - 0.5))
    a = jax.nn.sigmoid(a0 + a_lo @ a2)
    g = jax.nn.sigmoid(g_lo) @ g2
    kk = k * k_k
    k = k * (1.0 + (a - 1.0) * k_a)

    def hd(t):
        return t.reshape(B, S, RWKV_HEADS, HEAD_DIM)

    r, k, v, decay, a, kk = hd(r), hd(k), hd(v), hd(decay), hd(a), hd(kk)
    kk = kk / jnp.maximum(jnp.sqrt(jnp.sum(kk * kk, axis=-1, keepdims=True)), 1e-12)

    def step(state, inp):
        r_t, w_t, k_t, v_t, kk_t, a_t = inp
        sa = jnp.einsum('bhij,bhj->bhi', state, -kk_t)
        state = (state * w_t[:, :, None, :] + sa[..., None] * (kk_t * a_t)[:, :, None, :]
                 + v_t[..., None] * k_t[:, :, None, :])
        return state, jnp.einsum('bhij,bhj->bhi', state, r_t)

    xs = tuple(t.transpose(1, 0, 2, 3) for t in (r, decay, k, v, kk, a))
    state0 = jnp.zeros((B, RWKV_HEADS, HEAD_DIM, HEAD_DIM), jnp.float32)
    _, ys = lax.scan(step, state0, xs)
    y = ys.transpose(1, 0, 2, 3)
    mean = jnp.mean(y, axis=-1, keepdims=True)
    var = jnp.mean(jnp.square(y - mean), axis=-1, keepdims=True)
    y = ((y - mean) * lax.rsqrt(var + RWKV_GN_EPS)).reshape(B, S, W) * ln_w + ln_b
    bonus = (jnp.sum(r * k * r_k, axis=-1, keepdims=True) * v).reshape(B, S, W)
    return ((y + bonus) * g).astype(z.dtype)

def memory_cross_attention(h, m, w_q, w_kv, q_gain, k_gain, w_o):
    B, S, _ = h.shape
    M = m.shape[1]
    q = rms_norm((h @ w_q).reshape(B, S, XATTN_HEADS, XATTN_HEAD_DIM), q_gain)
    kv = (m @ w_kv).reshape(B, M, 2, XATTN_HEADS, XATTN_HEAD_DIM)
    k = rms_norm(kv[:, :, 0], k_gain)
    v = kv[:, :, 1]
    s = jnp.einsum('bqhd,bkhd->bhqk', q, k).astype(jnp.float32) * (XATTN_HEAD_DIM ** -0.5)
    p = jax.nn.softmax(s, axis=-1).astype(v.dtype)
    o = jnp.einsum('bhqk,bkhd->bqhd', p, v).reshape(B, S, XATTN_WIDTH)
    return o @ w_o

def first_inputs(seed: int = 0) -> dict:
    key = jax.random.key(seed)
    ks = iter(jax.random.split(key, 64))
    L, D = DEPTH, D_MODEL

    def nrm(shape, scale):
        return jax.random.normal(next(ks), shape, jnp.float32) * scale

    def gain(shape):
        return 1.0 + nrm(shape, 0.02)

    x = nrm((BATCH, SEQ, D), 1.0)
    mem = nrm((BATCH, MEM_LEN, D), 1.0)
    offset = jax.random.randint(next(ks), (BATCH, 1), 0, SEQ, dtype=jnp.int32)
    positions = (offset + jnp.arange(SEQ, dtype=jnp.int32)[None, :]).astype(jnp.int32)
    return {
        'x': x, 'mem': mem, 'positions': positions,
        'ffn1_norm': gain((L, D)),
        'ffn1_w_in': nrm((L, D, 2 * FFN_DIM), D ** -0.5),
        'ffn1_w_out': nrm((L, FFN_DIM, D), FFN_DIM ** -0.5),
        'mix_norm': gain((L, D)),
        'mix_w_in': nrm((L, D, IN_WIDTH), D ** -0.5),
        'mix_w_out': nrm((L, MIX_WIDTH, D), MIX_WIDTH ** -0.5),
        'fox_f_bias': 3.0 + nrm((L, FOX_HEADS), 0.5),
        'fox_q_gain': gain((L, HEAD_DIM)),
        'fox_k_gain': gain((L, HEAD_DIM)),
        'moba_q_gain': gain((L, HEAD_DIM)),
        'moba_k_gain': gain((L, HEAD_DIM)),
        'rwkv_mu': jax.random.uniform(next(ks), (L, RWKV_IN), jnp.float32, 0.0, 1.0),
        'rwkv_w0': nrm((L, RWKV_WIDTH), 1.0) - 1.0,
        'rwkv_w2': nrm((L, RWKV_DECAY_LORA, RWKV_WIDTH), RWKV_DECAY_LORA ** -0.5),
        'rwkv_a0': nrm((L, RWKV_WIDTH), 0.5),
        'rwkv_a2': nrm((L, RWKV_ICLR_LORA, RWKV_WIDTH), RWKV_ICLR_LORA ** -0.5),
        'rwkv_g2': nrm((L, RWKV_GATE_LORA, RWKV_WIDTH), RWKV_GATE_LORA ** -0.5),
        'rwkv_k_k': 0.85 + nrm((L, RWKV_WIDTH), 0.05),
        'rwkv_k_a': 1.0 + nrm((L, RWKV_WIDTH), 0.05),
        'rwkv_r_k': nrm((L, RWKV_HEADS, HEAD_DIM), 0.1),
        'rwkv_ln_w': gain((L, RWKV_WIDTH)),
        'rwkv_ln_b': nrm((L, RWKV_WIDTH), 0.02),
        'xattn_norm': gain((L, D)),
        'xattn_mem_norm': gain((L, D)),
        'xattn_w_q': nrm((L, D, XATTN_WIDTH), D ** -0.5),
        'xattn_w_kv': nrm((L, D, 2 * XATTN_WIDTH), D ** -0.5),
        'xattn_q_gain': gain((L, XATTN_HEAD_DIM)),
        'xattn_k_gain': gain((L, XATTN_HEAD_DIM)),
        'xattn_w_out': nrm((L, XATTN_WIDTH, D), XATTN_WIDTH ** -0.5),
        'ffn2_norm': gain((L, D)),
        'ffn2_w_in': nrm((L, D, 2 * FFN_DIM), D ** -0.5),
        'ffn2_w_out': nrm((L, FFN_DIM, D), FFN_DIM ** -0.5),
    }

def first_block(x, mem, positions, ffn1_norm, ffn1_w_in, ffn1_w_out, mix_norm, mix_w_in, mix_w_out,
              fox_f_bias, fox_q_gain, fox_k_gain, moba_q_gain, moba_k_gain,
              rwkv_mu, rwkv_w0, rwkv_w2, rwkv_a0, rwkv_a2, rwkv_g2, rwkv_k_k, rwkv_k_a, rwkv_r_k,
              rwkv_ln_w, rwkv_ln_b, xattn_norm, xattn_mem_norm, xattn_w_q, xattn_w_kv,
              xattn_q_gain, xattn_k_gain, xattn_w_out, ffn2_norm, ffn2_w_in, ffn2_w_out):
    cos, sin = rope_tables(positions)
    for l in range(DEPTH):
        x = x + 0.5 * swiglu(rms_norm(x, ffn1_norm[l]), ffn1_w_in[l], ffn1_w_out[l]).astype(x.dtype)
        z = rms_norm(x, mix_norm[l]) @ mix_w_in[l]
        z_fox, z_moba, z_rwkv = jnp.split(z, [FOX_IN, FOX_IN + MOBA_IN], axis=-1)
        y_fox = fox_mixer(z_fox, fox_f_bias[l], fox_q_gain[l], fox_k_gain[l])
        y_rwkv = rwkv7_mixer(z_rwkv, rwkv_mu[l], rwkv_w0[l], rwkv_w2[l], rwkv_a0[l], rwkv_a2[l],
                             rwkv_g2[l], rwkv_k_k[l], rwkv_k_a[l], rwkv_r_k[l], rwkv_ln_w[l], rwkv_ln_b[l])
        y_moba = moba_mixer(z_moba, cos, sin, moba_q_gain[l], moba_k_gain[l])
        y = jnp.concatenate([y_fox, y_rwkv, y_moba], axis=-1) @ mix_w_out[l]
        x = x + y.astype(x.dtype)
        x = x + memory_cross_attention(rms_norm(x, xattn_norm[l]), rms_norm(mem, xattn_mem_norm[l]),
                                       xattn_w_q[l], xattn_w_kv[l], xattn_q_gain[l], xattn_k_gain[l],
                                       xattn_w_out[l]).astype(x.dtype)
        x = x + 0.5 * swiglu(rms_norm(x, ffn2_norm[l]), ffn2_w_in[l], ffn2_w_out[l]).astype(x.dtype)
    return x


DEPTH_2 = 1

CTX_LEN = 256
GRID_W = 64

ATTN_HEADS = 8
ATTN_KV_HEADS = 2
ATTN_GROUP = ATTN_HEADS // ATTN_KV_HEADS
HEAD_DIM_2 = 128
ROPE_AXIS_DIM = HEAD_DIM_2 // 2
ROPE_THETA_2 = 10000.0
Q_BLOCK = 128

GDN_HEADS = 8
GDN_DK = 128
GDN_DV = 128
GDN_CHUNK = 64
SHORT_CONV = 3

D_FF = 2816
FFN_CONV = 3


ATTN_Q_W = ATTN_HEADS * HEAD_DIM_2
ATTN_KV_W = ATTN_KV_HEADS * HEAD_DIM_2
GDN_QK_W = GDN_HEADS * GDN_DK
GDN_V_W = GDN_HEADS * GDN_DV
GDN_CONV_W = 2 * GDN_QK_W + GDN_V_W
IN_SPLITS = (ATTN_KV_W, ATTN_KV_W, GDN_CONV_W, 2 * GDN_HEADS, 2 * GDN_HEADS, ATTN_Q_W, GDN_V_W, 2 * D_MODEL)
CTX_COLS = 2 * ATTN_KV_W + GDN_CONV_W + 4 * GDN_HEADS
IN_COLS = CTX_COLS + ATTN_Q_W + GDN_V_W + 2 * D_MODEL


def rms_norm_2(x, gain=None):
    x32 = x.astype(jnp.float32)
    y = x32 * lax.rsqrt(jnp.mean(x32 * x32, axis=-1, keepdims=True) + NORM_EPS)
    if gain is not None:
        y = y * gain.astype(jnp.float32)
    return y.astype(x.dtype)

def l2_normalize(x):
    return x * lax.rsqrt(jnp.sum(x * x, axis=-1, keepdims=True) + NORM_EPS)

def modulate(h, shift, scale):
    return h * (1.0 + scale) + shift

def split_cols(p):
    parts, off = [], 0
    for size in IN_SPLITS:
        if off >= p.shape[-1]:
            break
        parts.append(p[..., off:off + size])
        off += size
    return parts

def dwconv_centred(x, w, b=None):
    width = w.shape[0]
    pad = width // 2
    n = x.shape[1]
    xp = jnp.pad(x, ((0, 0), (pad, pad), (0, 0)))
    y = xp[:, 0:n] * w[0]
    for j in range(1, width):
        y = y + xp[:, j:j + n] * w[j]
    return y if b is None else y + b

def axial_rope_tables(n):
    rows = n // GRID_W
    row_ids = jnp.broadcast_to(jnp.arange(rows, dtype=jnp.float32)[:, None], (rows, GRID_W)).reshape(n)
    col_ids = jnp.broadcast_to(jnp.arange(GRID_W, dtype=jnp.float32)[None, :], (rows, GRID_W)).reshape(n)
    inv_freq = ROPE_THETA_2 ** (-jnp.arange(0, ROPE_AXIS_DIM, 2, dtype=jnp.float32) / ROPE_AXIS_DIM)
    ang = jnp.concatenate([row_ids[:, None] * inv_freq, col_ids[:, None] * inv_freq], axis=-1)
    ang = ang.reshape(n, 2, ROPE_AXIS_DIM // 2)
    return jnp.cos(ang), jnp.sin(ang)

def apply_axial_rope(x, cos, sin):
    x32 = x.astype(jnp.float32).reshape(*x.shape[:-1], 2, 2, ROPE_AXIS_DIM // 2)
    x1, x2 = x32[..., 0, :], x32[..., 1, :]
    cos = cos[None, :, None]
    sin = sin[None, :, None]
    out = jnp.stack([x1 * cos - x2 * sin, x2 * cos + x1 * sin], axis=-2)
    return out.reshape(x.shape).astype(x.dtype)

def sdpa_block(q, k, v):
    s = jnp.einsum('bqhgd,bkhd->bhgqk', q, k).astype(jnp.float32) * (HEAD_DIM_2 ** -0.5)
    p = jax.nn.softmax(s, axis=-1).astype(v.dtype)
    return jnp.einsum('bhgqk,bkhd->bqhgd', p, v)

def latent_attention(q, k_all, v_all):
    b, n = q.shape[:2]
    nb = n // Q_BLOCK
    qb = jnp.moveaxis(q.reshape(b, nb, Q_BLOCK, *q.shape[2:]), 1, 0)
    o = lax.map(lambda q_blk: sdpa_block(q_blk, k_all, v_all), qb)
    return jnp.moveaxis(o, 0, 1).reshape(b, n, ATTN_Q_W)

def gdn_chunked(q, k, v, log_a, beta, s0, with_output):
    b, h, n, dk = q.shape
    dv = v.shape[-1]
    nc = n // GDN_CHUNK
    q = q.reshape(b, h, nc, GDN_CHUNK, dk)
    k = k.reshape(b, h, nc, GDN_CHUNK, dk)
    v = v.reshape(b, h, nc, GDN_CHUNK, dv)
    log_a = log_a.reshape(b, h, nc, GDN_CHUNK)
    beta = beta.reshape(b, h, nc, GDN_CHUNK)
    gam = jnp.cumsum(log_a, axis=-1)
    idx = jnp.arange(GDN_CHUNK)
    strict = idx[:, None] > idx[None, :]
    incl = idx[:, None] >= idx[None, :]
    dec = jnp.exp(jnp.where(incl, gam[..., :, None] - gam[..., None, :], -jnp.inf))
    kk = jnp.einsum('bhncd,bhnsd->bhncs', k, k)
    a_mat = jnp.where(strict, beta[..., :, None] * dec * kk, 0.0) + jnp.eye(GDN_CHUNK, dtype=jnp.float32)
    rhs = jnp.concatenate([beta[..., None] * v, (beta * jnp.exp(gam))[..., None] * k], axis=-1)
    uw = lax.linalg.triangular_solve(a_mat, rhs, left_side=True, lower=True, unit_diagonal=True)
    u, w = uw[..., :dv], uw[..., dv:]
    k_dec = k * jnp.exp(gam[..., -1:] - gam)[..., None]
    g_last = jnp.exp(gam[..., -1])
    xs = [u, w, k_dec, g_last]
    if with_output:
        q_dec = q * jnp.exp(gam)[..., None]
        p = dec * jnp.einsum('bhncd,bhnsd->bhncs', q, k)
        xs = xs + [q_dec, p]
    xs = tuple(jnp.moveaxis(t, 2, 0) for t in xs)

    def step(s, inp):
        u_c, w_c, kd_c, gl_c = inp[:4]
        delta = u_c - jnp.einsum('bhcd,bhde->bhce', w_c, s)
        s_new = gl_c[..., None, None] * s + jnp.einsum('bhcd,bhce->bhde', kd_c, delta)
        if with_output:
            qd_c, p_c = inp[4], inp[5]
            o = jnp.einsum('bhcd,bhde->bhce', qd_c, s) + jnp.einsum('bhcs,bhse->bhce', p_c, delta)
            return s_new, o
        return s_new, None

    s_fin, o = lax.scan(step, s0, xs)
    if with_output:
        o = jnp.moveaxis(o, 0, 2).reshape(b, h, n, dv)
    return o, s_fin

def gdn_prepare(qkv, db, da, conv_w, a_log, dt_bias):
    b, n, _ = qkv.shape
    qkv = jax.nn.silu(dwconv_centred(qkv, conv_w)).astype(jnp.float32)
    q, k, v = jnp.split(qkv, [GDN_QK_W, 2 * GDN_QK_W], axis=-1)
    q = l2_normalize(q.reshape(b, n, GDN_HEADS, GDN_DK)) * (GDN_DK ** -0.5)
    k = l2_normalize(k.reshape(b, n, GDN_HEADS, GDN_DK))
    v = v.reshape(b, n, GDN_HEADS, GDN_DV)
    q, k, v = (t.transpose(0, 2, 1, 3) for t in (q, k, v))
    beta = jax.nn.sigmoid(db.astype(jnp.float32)).reshape(b, n, 2, GDN_HEADS).transpose(2, 0, 3, 1)
    da = da.astype(jnp.float32).reshape(b, n, 2, GDN_HEADS).transpose(2, 0, 3, 1)
    log_a = -jnp.exp(a_log.astype(jnp.float32))[:, None, :, None] * jax.nn.softplus(
        da + dt_bias.astype(jnp.float32)[:, None, :, None])
    return q, k, v, log_a, beta

def gdn_bidirectional(ctx_in, lat_in, with_ctx_output):
    qc, kc, vc, lac, bc = ctx_in
    ql, kl, vl, lal, bl = lat_in
    s0 = jnp.zeros((ql.shape[0], GDN_HEADS, GDN_DK, GDN_DV), jnp.float32)
    o_lat, o_ctx = None, None
    for d in range(2):
        rev = (lambda t: jnp.flip(t, axis=2)) if d == 1 else (lambda t: t)
        oc, sc = gdn_chunked(rev(qc), rev(kc), rev(vc), rev(lac[d]), rev(bc[d]), s0, with_ctx_output)
        ol, _ = gdn_chunked(rev(ql), rev(kl), rev(vl), rev(lal[d]), rev(bl[d]), sc, True)
        o_lat = rev(ol) if o_lat is None else o_lat + rev(ol)
        if with_ctx_output:
            o_ctx = rev(oc) if o_ctx is None else o_ctx + rev(oc)
    return o_lat, o_ctx

def gdn_output(o, z, norm_w):
    b, n = z.shape[:2]
    o = rms_norm_2(o.transpose(0, 2, 1, 3), norm_w)
    y = o * jax.nn.silu(z.astype(jnp.float32).reshape(b, n, GDN_HEADS, GDN_DV))
    return y.reshape(b, n, GDN_V_W).astype(z.dtype)

def merge_branches(attn, gdn, gates, w_pa, w_pd, w_out):
    g_a, g_d = jnp.split(gates, 2, axis=-1)
    y = jax.nn.sigmoid(g_a) * (attn @ w_pa) + jax.nn.sigmoid(g_d) * (gdn @ w_pd)
    return y @ w_out

def conv_ffn(h, w_up, conv_w, conv_b, w_down):
    u = dwconv_centred(h @ w_up, conv_w, conv_b)
    g, val = jnp.split(u, 2, axis=-1)
    return (jax.nn.silu(g) * val) @ w_down

def hybrid_layer(x, ctx, c, c_ctx, w_mod, b_mod, w_in, q_norm_w, k_norm_w, conv_qkv_w, a_log, dt_bias,
                 gdn_norm_w, w_pa, w_pd, w_out, w_up, ffn_conv_w, ffn_conv_b, w_down, update_ctx):
    b, n, _ = x.shape
    cl = ctx.shape[1]
    mod_lat = jax.nn.silu(c) @ w_mod + b_mod
    mod_ctx = jax.nn.silu(c_ctx) @ w_mod + b_mod
    sh1, sc1, g1, sh2, sc2, g2 = [m[:, None, :] for m in jnp.split(mod_lat, 6, axis=-1)]
    csh1, csc1, cg1, csh2, csc2, cg2 = jnp.split(mod_ctx, 6, axis=-1)

    hx = modulate(rms_norm_2(x), sh1, sc1)
    hc = modulate(rms_norm_2(ctx), csh1, csc1)
    ak_x, av_x, qkv_x, db_x, da_x, aq_x, z_x, gate_x = split_cols(hx @ w_in)
    ak_c, av_c, qkv_c, db_c, da_c, *rest_c = split_cols(hc @ (w_in if update_ctx else w_in[:, :CTX_COLS]))

    cos, sin = axial_rope_tables(n)
    q_x = apply_axial_rope(rms_norm_2(aq_x.reshape(b, n, ATTN_HEADS, HEAD_DIM_2), q_norm_w), cos, sin)
    q_x = q_x.reshape(b, n, ATTN_KV_HEADS, ATTN_GROUP, HEAD_DIM_2)
    k_x = apply_axial_rope(rms_norm_2(ak_x.reshape(b, n, ATTN_KV_HEADS, HEAD_DIM_2), k_norm_w), cos, sin)
    v_x = av_x.reshape(b, n, ATTN_KV_HEADS, HEAD_DIM_2)
    k_c = rms_norm_2(ak_c.reshape(b, cl, ATTN_KV_HEADS, HEAD_DIM_2), k_norm_w)
    v_c = av_c.reshape(b, cl, ATTN_KV_HEADS, HEAD_DIM_2)
    attn_x = latent_attention(q_x, jnp.concatenate([k_c, k_x], axis=1), jnp.concatenate([v_c, v_x], axis=1))

    gdn_x_in = gdn_prepare(qkv_x, db_x, da_x, conv_qkv_w, a_log, dt_bias)
    gdn_c_in = gdn_prepare(qkv_c, db_c, da_c, conv_qkv_w, a_log, dt_bias)
    o_x, o_c = gdn_bidirectional(gdn_c_in, gdn_x_in, update_ctx)
    gdn_x = gdn_output(o_x, z_x, gdn_norm_w)

    x = x + g1 * merge_branches(attn_x, gdn_x, gate_x, w_pa, w_pd, w_out)
    x = x + g2 * conv_ffn(modulate(rms_norm_2(x), sh2, sc2), w_up, ffn_conv_w, ffn_conv_b, w_down)

    if update_ctx:
        aq_c, z_c, gate_c = rest_c
        q_c = rms_norm_2(aq_c.reshape(b, cl, ATTN_HEADS, HEAD_DIM_2), q_norm_w)
        q_c = q_c.reshape(b, cl, ATTN_KV_HEADS, ATTN_GROUP, HEAD_DIM_2)
        attn_c = sdpa_block(q_c, k_c, v_c).reshape(b, cl, ATTN_Q_W)
        gdn_c = gdn_output(o_c, z_c, gdn_norm_w)
        ctx = ctx + cg1 * merge_branches(attn_c, gdn_c, gate_c, w_pa, w_pd, w_out)
        ctx = ctx + cg2 * conv_ffn(modulate(rms_norm_2(ctx), csh2, csc2), w_up, ffn_conv_w, ffn_conv_b, w_down)
    return x, ctx

def second_inputs(seed: int = 0) -> dict:
    key = jax.random.key(seed)
    ks = jax.random.split(key, 22)
    f32 = jnp.float32

    def dense(k, shape, fan_in, s=1.0):
        return s * (fan_in ** -0.5) * jax.random.normal(k, shape, f32)

    dt = jnp.exp(jax.random.uniform(ks[10], (DEPTH_2, 2, GDN_HEADS), f32,
                                    minval=math.log(1e-3), maxval=math.log(1e-1)))
    return {
        'x': jax.random.normal(ks[0], (BATCH, SEQ, D_MODEL), f32),
        'c': jax.random.normal(ks[1], (BATCH, D_MODEL), f32),
        'ctx': jax.random.normal(ks[2], (BATCH, CTX_LEN, D_MODEL), f32),
        'c_ctx': jax.random.normal(ks[3], (D_MODEL,), f32),
        'w_mod': dense(ks[4], (DEPTH_2, D_MODEL, 6 * D_MODEL), D_MODEL, 0.5),
        'b_mod': 0.02 * jax.random.normal(ks[5], (DEPTH_2, 6 * D_MODEL), f32),
        'w_in': dense(ks[6], (DEPTH_2, D_MODEL, IN_COLS), D_MODEL),
        'q_norm_w': 1.0 + 0.05 * jax.random.normal(ks[7], (DEPTH_2, HEAD_DIM_2), f32),
        'k_norm_w': 1.0 + 0.05 * jax.random.normal(ks[8], (DEPTH_2, HEAD_DIM_2), f32),
        'conv_qkv_w': dense(ks[9], (DEPTH_2, SHORT_CONV, GDN_CONV_W), SHORT_CONV),
        'a_log': jnp.log(jax.random.uniform(ks[11], (DEPTH_2, 2, GDN_HEADS), f32, minval=1.0, maxval=16.0)),
        'dt_bias': dt + jnp.log(-jnp.expm1(-dt)),
        'gdn_norm_w': 1.0 + 0.05 * jax.random.normal(ks[12], (DEPTH_2, GDN_DV), f32),
        'w_pa': dense(ks[13], (DEPTH_2, ATTN_Q_W, D_MODEL), ATTN_Q_W),
        'w_pd': dense(ks[14], (DEPTH_2, GDN_V_W, D_MODEL), GDN_V_W),
        'w_out': dense(ks[15], (DEPTH_2, D_MODEL, D_MODEL), D_MODEL),
        'w_up': dense(ks[16], (DEPTH_2, D_MODEL, 2 * D_FF), D_MODEL),
        'ffn_conv_w': dense(ks[17], (DEPTH_2, FFN_CONV, 2 * D_FF), FFN_CONV),
        'ffn_conv_b': 0.02 * jax.random.normal(ks[18], (DEPTH_2, 2 * D_FF), f32),
        'w_down': dense(ks[19], (DEPTH_2, D_FF, D_MODEL), D_FF),
        'final_norm_w': 1.0 + 0.05 * jax.random.normal(ks[20], (D_MODEL,), f32),
    }

def second_block(x, c, ctx, c_ctx, w_mod, b_mod, w_in, q_norm_w, k_norm_w, conv_qkv_w, a_log, dt_bias,
              gdn_norm_w, w_pa, w_pd, w_out, w_up, ffn_conv_w, ffn_conv_b, w_down, final_norm_w):
    for layer in range(DEPTH_2):
        x, ctx = hybrid_layer(
            x, ctx, c, c_ctx, w_mod[layer], b_mod[layer], w_in[layer], q_norm_w[layer], k_norm_w[layer],
            conv_qkv_w[layer], a_log[layer], dt_bias[layer], gdn_norm_w[layer], w_pa[layer], w_pd[layer],
            w_out[layer], w_up[layer], ffn_conv_w[layer], ffn_conv_b[layer], w_down[layer],
            update_ctx=layer < DEPTH_2 - 1)
    return rms_norm_2(x, final_norm_w)


def setup_inputs(seed=0):
    out = dict(first_inputs(seed))
    for name, value in second_inputs(seed + 1).items():
        if name != "x":
            out[name + "_2"] = value
    return out


def reference(
    x, mem, positions, ffn1_norm, ffn1_w_in, ffn1_w_out, mix_norm, mix_w_in, mix_w_out,
    fox_f_bias, fox_q_gain, fox_k_gain, moba_q_gain, moba_k_gain, rwkv_mu, rwkv_w0, rwkv_w2,
    rwkv_a0, rwkv_a2, rwkv_g2, rwkv_k_k, rwkv_k_a, rwkv_r_k, rwkv_ln_w, rwkv_ln_b, xattn_norm,
    xattn_mem_norm, xattn_w_q, xattn_w_kv, xattn_q_gain, xattn_k_gain, xattn_w_out, ffn2_norm,
    ffn2_w_in, ffn2_w_out, c_2, ctx_2, c_ctx_2, w_mod_2, b_mod_2, w_in_2, q_norm_w_2,
    k_norm_w_2, conv_qkv_w_2, a_log_2, dt_bias_2, gdn_norm_w_2, w_pa_2, w_pd_2, w_out_2, w_up_2,
    ffn_conv_w_2, ffn_conv_b_2, w_down_2, final_norm_w_2,
):
    x = first_block(
        x, mem, positions, ffn1_norm, ffn1_w_in, ffn1_w_out, mix_norm, mix_w_in, mix_w_out,
        fox_f_bias, fox_q_gain, fox_k_gain, moba_q_gain, moba_k_gain, rwkv_mu, rwkv_w0, rwkv_w2,
        rwkv_a0, rwkv_a2, rwkv_g2, rwkv_k_k, rwkv_k_a, rwkv_r_k, rwkv_ln_w, rwkv_ln_b,
        xattn_norm, xattn_mem_norm, xattn_w_q, xattn_w_kv, xattn_q_gain, xattn_k_gain,
        xattn_w_out, ffn2_norm, ffn2_w_in, ffn2_w_out,
    )
    return second_block(
        x, c_2, ctx_2, c_ctx_2, w_mod_2, b_mod_2, w_in_2, q_norm_w_2, k_norm_w_2, conv_qkv_w_2,
        a_log_2, dt_bias_2, gdn_norm_w_2, w_pa_2, w_pd_2, w_out_2, w_up_2, ffn_conv_w_2,
        ffn_conv_b_2, w_down_2, final_norm_w_2,
    )


_drawn_inputs = setup_inputs


def setup_inputs(seed=0):
    import zlib

    import numpy as np

    out = dict(_drawn_inputs(seed))
    spreads = {}
    factors = {'ffn1_norm': 3.985,
     'fox_q_gain': 8.0,
     'fox_k_gain': 8.0,
     'moba_q_gain': 8.0,
     'moba_k_gain': 8.0,
     'rwkv_k_k': 6.419,
     'rwkv_ln_w': 5.803,
     'rwkv_ln_b': 4.765,
     'xattn_norm': 8.0,
     'xattn_mem_norm': 8.0,
     'xattn_q_gain': 8.0,
     'xattn_k_gain': 8.0,
     'ffn2_norm': 4.916,
     'ctx_2': 38.347,
     'c_ctx_2': 20.232,
     'b_mod_2': 14.194,
     'q_norm_w_2': 64.0,
     'k_norm_w_2': 64.0,
     'a_log_2': 10.749,
     'gdn_norm_w_2': 64.0,
     'ffn_conv_b_2': 64.0,
     'dt_bias_2': 3.998,
     'w_pa_2': 4.898,
     'w_up_2': 4.197,
     'ffn_conv_w_2': 4.157,
     'w_down_2': 4.152}
    for name, (base, spread) in spreads.items():
        noise = np.random.default_rng([zlib.crc32(name.encode()), seed]).standard_normal(out[name].shape)
        drawn = base * np.exp(spread * noise) if base else spread * noise
        out[name] = jnp.asarray(drawn.astype(out[name].dtype))
    for name, factor in factors.items():
        out[name] = (out[name] * factor).astype(out[name].dtype)
    return out
```

```python
import numpy as np
from contextlib import ExitStack
import concourse.bass as bass
from concourse import mybir

F32 = mybir.dt.float32
I32 = mybir.dt.int32
ALU = mybir.AluOpType
ACT = mybir.ActivationFunctionType
AX = mybir.AxisListType

P = 128
D = 1024
KD = D // P
T = 256
TT = T // P
LAYERS = 2
FFN = 2816
FK = FFN // P
HALF = 256
RING = 3
EPS = 1e-6
GN_EPS = 64e-5
DECAY = float(np.exp(-0.5))
CH = 64
NEG = -1.0e30
LEVELS = 7

FOX_IN = 3 * 256 + 4
MOBA_IN = 3 * 256
RW0 = FOX_IN + MOBA_IN
CTX_COLS = 512 + 3072 + 32


class Counted:

    def __init__(self, sem):
        self.sem = sem
        self.n = 0

    def on(self, ins, by=1):
        ins.then_inc(self.sem, by)
        self.n += by
        return self.n

    def after(self, eng, ins):
        self.on(ins)
        eng.wait_ge(self.sem, self.n)

    def hold(self, eng):
        if self.n:
            eng.wait_ge(self.sem, self.n)



FIRST_ONLY = ("headsum", "rot", "chunkmask", "gate", "causal", "freq", "gneps")
SECOND_ONLY = ("axial", "levels_back", "future", "past", "axcos", "axsin", "fwd", "bwd")


def constant_tables():
    i = np.arange(P)
    row, col = i[:, None], i[None, :]
    same = (row // CH) == (col // CH)
    parts = {}
    parts["ident"] = row == col
    parts["ones"] = np.ones((P, P))
    parts["headsum"] = same
    rot = np.zeros((P, P))
    for h in (0, 64):
        for j in range(8):
            rot[h + 8 + j, h + j] = -1.0
            rot[h + j, h + 8 + j] = 1.0
    parts["rot"] = rot
    axial = np.zeros((P, P))
    for a in (0, 64):
        for j in range(32):
            axial[a + 32 + j, a + j] = -1.0
            axial[a + j, a + 32 + j] = 1.0
    parts["axial"] = axial
    lev = []
    for l in range(LEVELS):
        join = (row >> (l + 1)) == (col >> (l + 1))
        lev.append(join & (((col >> l) & 1) == 1) & (((row >> l) & 1) == 0))
    parts["levels"] = np.concatenate(lev, 1)
    parts["levels_back"] = np.concatenate([m.T for m in lev], 1)
    strict, incl = same & (row < col), same & (row <= col)
    parts["chunkmask"] = np.concatenate([strict, incl, strict, incl], 1)
    gate = np.ones((P, 4 * T))
    gate[:, ::CH] = 0.0
    parts["gate"] = gate
    parts["nomask"] = np.zeros((P, 512))
    causal = np.where(row >= col, 0.0, NEG)
    parts["causal"] = np.concatenate([np.zeros((P, P)), causal], 1)
    parts["future"] = np.where(row <= col, 0.0, NEG)
    parts["past"] = np.where(row >= col, 0.0, NEG)
    rows, cols = np.arange(T) // 64, np.arange(T) % 64
    inv = (np.float32(10000.0) ** (-np.arange(0, 64, 2, dtype=np.float32) / np.float32(64))).astype(np.float32)
    ang = np.concatenate([rows[None, :].astype(np.float32) * inv[:, None]] * 2
                         + [cols[None, :].astype(np.float32) * inv[:, None]] * 2, 0).astype(np.float32)
    parts["axcos"], parts["axsin"] = np.cos(ang), np.sin(ang)
    inv1 = (np.float32(500000.0) ** (-np.arange(0, 16, 2, dtype=np.float32) / np.float32(16))).astype(np.float32)
    freq = np.zeros((P, 1), np.float32)
    for h in (0, 64):
        freq[h:h + 16, 0] = np.concatenate([inv1, inv1])
    parts["freq"] = freq
    parts["eps"] = np.full((P, 1), EPS)
    parts["gneps"] = np.full((P, 1), GN_EPS)
    parts["fwd"] = row < 8
    parts["bwd"] = row >= 8
    at, tiles = {}, []
    for part in range(3):
        columns, off = [], 0
        for name, a in parts.items():
            if part == (1 if name in FIRST_ONLY else 2 if name in SECOND_ONLY else 0):
                a = np.asarray(a, np.float32)
                at[name] = (part, off, a.shape[1])
                columns.append(a)
                off += a.shape[1]
        tiles.append(np.ascontiguousarray(np.concatenate(columns, 1)))
    return at, tiles


CONST_AT, CONSTS = constant_tables()

PARAM_ROWS = {}


def _rows():
    at = 0
    for name, n in (("ffn1_norm", 8), ("mix_norm", 8), ("xattn_norm", 8), ("xattn_mem_norm", 8),
                    ("ffn2_norm", 8), ("mu_rkv", 12), ("mu_wa", 1), ("mu_g", 2), ("w0", 4), ("a0", 4),
                    ("k_k", 4), ("k_a", 4), ("r_k", 4), ("ln_w", 4), ("ln_b", 4), ("fox_q", 1), ("fox_k", 1),
                    ("moba_q", 1), ("moba_k", 1), ("xq", 1), ("xk", 1), ("f_bias", 1)):
        PARAM_ROWS[name] = at
        at += n
    return at


N_PARAM_ROWS = _rows()


class Kernel:

    def __init__(self, nc, a, out):
        self.nc, self.a, self.out = nc, a, out
        self.ctx = ExitStack()
        self.names = 0

    def sb(self, name, shape, dt=F32, ctx=None):
        self.names += 1
        return (ctx or self.ctx).enter_context(self.nc.sbuf_tensor(f"{name}_{self.names}", shape, dt))

    def open(self):
        nc, ctx = self.nc, self.ctx
        self.sems = {}
        self.bank = [ctx.enter_context(nc.psum_tensor(f"bank{i}", [P, 512], F32)) for i in range(8)]
        self.consts = [self.sb("const", [P, CONSTS[0].shape[1]]), None, None]
        self.ring = [self.sb(f"ring{i}", [P, KD * HALF]) for i in range(RING)]
        self.x = self.sb("x", [P, KD, T])
        self.h = self.sb("h", [P, KD, T])
        self.prm = self.sb("prm", [P, P])
        self.sem_ctx = ctx
        self.loaded = [Counted(self.sem(f"slab_loaded{i}")) for i in range(RING)]
        self.done = Counted(self.sem("slab_done"))
        self.pe_own = Counted(self.sem("pe_own"))
        self.act_own = Counted(self.sem("act_own"))
        self.dve_own = Counted(self.sem("dve_own"))
        self.pool_own = Counted(self.sem("pool_own"))
        self.sem_ctx = ExitStack()

    def c(self, name, rows=slice(0, P), first=0, n=None):
        part, off, width = CONST_AT[name]
        return self.consts[part][rows, off + first:off + first + (width - first if n is None else n)]

    def sem(self, name):
        if name not in self.sems:
            self.sems[name] = self.sem_ctx.enter_context(self.nc.semaphore(name))
        return self.sems[name]

    def forget(self):
        keep = {s.sem.name: s.sem for s in self.lasting()}
        self.sem_ctx.close()
        self.sem_ctx = ExitStack()
        self.sems = keep

    def lasting(self):
        return self.loaded + [self.done, self.pe_own, self.act_own, self.dve_own, self.pool_own]

    def clear(self, keep=()):
        ids = sorted(s.num for s in self.sems.values() if s.num not in keep)
        runs = []
        for i in ids:
            if runs and runs[-1][1] == i:
                runs[-1][1] = i + 1
            else:
                runs.append([i, i + 1])
        with self.nc.Block(no_gpsimd_drain=True) as block:
            @block.sync
            def _(sync):
                for first, end in runs:
                    sync.sem_clear(range(first, end))

    def restart(self):
        self.clear()
        for s in self.lasting():
            s.n = 0

    def restart_stages(self):
        self.clear({s.sem.num for s in self.loaded + [self.done]})
        self.split_until = {}
        for s in (self.pe_own, self.act_own, self.dve_own, self.pool_own):
            s.n = 0

    def plan(self, slabs):
        self.slabs, self.issued, self.eaten = slabs, 0, 0
        self.split_until = {}
        self.landed = []
        total = [0] * RING
        for n, pieces in enumerate(slabs):
            total[n % RING] += 16 * len(pieces)
            self.landed.append(total[n % RING])

    def load_slabs(self, sync, upto):
        for n in range(self.issued, min(upto, len(self.slabs))):
            if n - RING in self.split_until:
                sync.wait_ge(*self.split_until[n - RING])
            elif n >= RING:
                sync.wait_ge(self.done.sem, n - RING + 1)
            for src, rows, start, groups, cols in self.slabs[n]:
                dst = self.ring[n % RING][0:rows, start:start + groups * cols]
                sync.dma_start(dst.rearrange("p (k n) -> p k n", k=groups), src)\
                    .then_inc(self.loaded[n % RING].sem, 16)
            self.issued = n + 1

    def next_slab(self, pe):
        n = self.eaten
        self.eaten += 1
        pe.wait_ge(self.loaded[n % RING].sem, self.landed[n])
        return self.ring[n % RING]

    def slab_done(self, last):
        last.then_inc(self.done.sem, 1)

    def wait_slabs(self, eng, n):
        eng.wait_ge(self.done.sem, n)



def groups_of(w, k0, groups, c0, cols):
    return w[:, k0 * P:(k0 + groups) * P, c0:c0 + cols].rearrange("a (k p) n -> p (a k) n", p=P)


def whole(w, c0, cols=HALF):
    return [(groups_of(w, 0, KD, c0, cols), P, 0, KD, cols)]


def view(place, groups=KD, cols=HALF, start=0, rows=P):
    return place[0:rows, start:start + groups * cols].rearrange("p (k n) -> p k n", k=groups)


def feature_major(K, pe, bank, w, act, kd, cols, tokens=T, at=0):
    for j in range(0, cols, P):
        m = min(P, cols - j)
        for k in range(kd):
            last = pe.matmul(bank[0:m, at:at + tokens], w[:, k, j:j + m], act[:, k, 0:tokens],
                             start=(k == 0), stop=(k == kd - 1))
        at += tokens
    return last


def token_major(K, pe, bank, w, act, kd, cols, tiles=(0, 1)):
    for i, tt in enumerate(tiles):
        for k in range(kd):
            last = pe.matmul(bank[:, i * cols:(i + 1) * cols], act[:, k, tt * P:(tt + 1) * P],
                             w[:, k, 0:cols], start=(k == 0), stop=(k == kd - 1))
    return last


F32R = mybir.dt.float32r


class Split:

    PLACES = 3

    def __init__(self, K, ctx, tag, n0, count):
        self.K, self.n0, self.count, self.issued = K, n0, count, 0
        self.hi = [K.sb(f"slab_hi{i}", [P, KD * HALF], F32R, ctx=ctx) for i in range(self.PLACES)]
        self.lo = [K.sb(f"slab_lo{i}", [P, KD * HALF], F32R, ctx=ctx) for i in range(self.PLACES)]
        self.hi_ready, self.lo_ready = K.sem(tag + "_slab_hi"), K.sem(tag + "_slab_lo")
        for i in range(count):
            K.split_until[n0 + i] = (self.lo_ready, i + 1)

    def used(self, i):
        return sum(groups * cols for _, _, _, groups, cols in self.K.slabs[self.n0 + i])

    def act(self, act, upto):
        K = self.K
        for i in range(self.issued, min(upto, self.count)):
            n, w = self.n0 + i, self.used(i)
            act.wait_ge(K.loaded[n % RING].sem, K.landed[n])
            if i >= self.PLACES:
                K.wait_slabs(act, n - self.PLACES + 1)
            act.copy(self.hi[i % self.PLACES][:, 0:w], K.ring[n % RING][:, 0:w]).then_inc(self.hi_ready, 1)
            self.issued = i + 1

    def pool(self, pool):
        K = self.K
        for i in range(self.count):
            w, place = self.used(i), K.ring[(self.n0 + i) % RING]
            pool.wait_ge(self.hi_ready, i + 1)
            pool.tensor_tensor(self.lo[i % self.PLACES][:, 0:w], place[:, 0:w],
                               self.hi[i % self.PLACES][:, 0:w].bitcast(F32), ALU.subtract).then_inc(self.lo_ready, 1)

    def next_slab(self, pe):
        K = self.K
        i = K.eaten - self.n0
        K.eaten += 1
        pe.wait_ge(self.lo_ready, i + 1)
        return self.hi[i % self.PLACES], self.lo[i % self.PLACES]

    def next_view(self, pe, groups=KD, cols=HALF):
        return self.view(self.next_slab(pe), groups, cols)

    @staticmethod
    def view(places, groups=KD, cols=HALF, start=0):
        return [view(place, groups, cols, start) for place in places]


def product3(pe, out, w, act, start, stop):
    pe.matmul(out, w[0], act[0], start=start, stop=False)
    pe.matmul(out, w[0], act[1], start=False, stop=False)
    return pe.matmul(out, w[1], act[0], start=False, stop=stop)


def feature_major3(pe, bank, w, act, kd, cols, at=0, first=None):
    for j in range(0, cols, P):
        for k in range(kd):
            if first is not None and j == 0:
                first(k)
            last = product3(pe, bank[:, at:at + T], [p[:, k, j:j + P] for p in w], [p[:, k, :] for p in act],
                            k == 0, k == kd - 1)
        at += T
    return last


def token_major3(pe, bank, w, act, kd, cols, tiles=(0, 1)):
    for i, tt in enumerate(tiles):
        for k in range(kd):
            last = product3(pe, bank[:, i * cols:(i + 1) * cols], [p[:, k, tt * P:(tt + 1) * P] for p in act],
                            [p[:, k, 0:cols] for p in w], k == 0, k == kd - 1)
    return last


class Parts:

    def __init__(self, K, ctx, tag, groups):
        self.hi = K.sb(tag + "_hi", [P, groups, T], F32R, ctx=ctx)
        self.lo = K.sb(tag + "_lo", [P, groups, T], F32R, ctx=ctx)
        self.hi_ready, self.lo_ready = K.sem(tag + "_hi_ready"), K.sem(tag + "_lo_ready")
        self.splits = 0

    def act(self, act, t, source):
        act.copy(self.hi[:, t, :], source).then_inc(self.hi_ready, 1)

    def dve(self, dve, t, source):
        self.splits += 1
        dve.wait_ge(self.hi_ready, self.splits)
        dve.tensor_tensor(self.lo[:, t, :], source, self.hi[:, t, :].bitcast(F32), ALU.subtract)\
            .then_inc(self.lo_ready, 1)


def pair_of(i):
    return slice(2 * i, 2 * i + 2)


class Norm:

    def __init__(self, K, ctx, tag, x, h, gain, bank, shift=None, parts=None, sq=None):
        self.K, self.x, self.h, self.gain, self.bank = K, x, h, gain, bank
        self.shift, self.parts = shift, parts
        self.sq = h if sq is None else sq
        self.rstd = K.sb("rstd", [P, T], ctx=ctx)
        self.squared = K.sem(tag + "_squared")
        self.summed = K.sem(tag + "_summed")
        self.rstd_ready = K.sem(tag + "_rstd_ready")
        self.h_ready = K.sem(tag + "_h_ready")

    def act(self, act, between=None):
        K = self.K
        for i in range(4):
            act.activation(self.sq[:, 2 * i:2 * i + 2, :], self.x[:, 2 * i:2 * i + 2, :], ACT.Square)\
                .then_inc(self.squared, 1)
        if between is not None:
            between()
        act.wait_ge(self.summed, 1)
        K.act_own.after(act, act.activation(self.rstd[:, :], self.bank[:, 0:T], ACT.Ln,
                                            bias=K.c("eps"), scale=1.0 / D))
        act.activation(self.rstd[:, :], self.rstd[:, :], ACT.Exp, scale=-0.5).then_inc(self.rstd_ready, 1)
        if self.parts is not None:
            for i in range(KD // 2):
                act.wait_ge(self.h_ready, 2 * i + 2)
                self.parts.act(act, pair_of(i), self.h[:, pair_of(i), :])

    def pe(self, pe):
        for k in range(KD):
            if k % 2 == 0:
                pe.wait_ge(self.squared, k // 2 + 1)
            last = pe.matmul(self.bank[:, 0:T], self.K.c("ones"), self.sq[:, k, :], start=(k == 0), stop=(k == KD - 1))
        last.then_inc(self.summed, 1)

    def dve(self, dve):
        K = self.K
        dve.wait_ge(self.rstd_ready, 1)
        for k in range(KD):
            ins = dve.scalar_tensor_tensor(self.h[:, k, :], self.x[:, k, :], self.gain[:, k:k + 1], self.rstd[:, :],
                                           ALU.mult, ALU.mult)
            if self.shift is not None:
                K.dve_own.after(dve, ins)
                ins = dve.tensor_scalar(self.h[:, k, :], self.h[:, k, :], self.shift[:, k:k + 1], None, ALU.add)
            ins.then_inc(self.h_ready, 1)
        if self.parts is not None:
            for i in range(KD // 2):
                self.parts.dve(dve, pair_of(i), self.h[:, pair_of(i), :])


def ffn_out_pe(K, pe, split, hidden, x_updated):
    for jj in range(4):
        if jj >= 2:
            pe.wait_ge(x_updated, 2 * (jj - 1))
        for k0 in (0, 8, 16):
            g = min(KD, FK - k0)
            w = split.next_view(pe, groups=g)
            for j in range(2):
                for k in range(g):
                    if jj == j == 0:
                        pe.wait_ge(hidden.lo_ready, (k0 + k) // 2 + 1)
                    last = product3(pe, K.bank[2 * (jj % 2) + j][:, 0:T], [p[:, k, j * P:(j + 1) * P] for p in w],
                                    (hidden.hi[:, k0 + k, :], hidden.lo[:, k0 + k, :]), k0 + k == 0, k0 + k == FK - 1)
            K.slab_done(last)


def ffn_stage(K, tag, gain):
    nc = K.nc
    n0 = K.eaten
    N = FK // 2
    with ExitStack() as ctx:
        hidden = Parts(K, ctx, tag + "_hidden", FK)
        whole_hidden = K.sb("hidden", [P, 2, 2 * T], ctx=ctx)
        gate = K.sb("gate", [P, 2, 2 * T], ctx=ctx)
        parts = Parts(K, ctx, tag + "_h", KD)
        norm = Norm(K, ctx, tag, K.x, K.h, gain, K.bank[4], parts=parts)
        split = Split(K, ctx, tag, n0, FK + 12)
        silu_ready, product_ready = K.sem(tag + "_silu_ready"), K.sem(tag + "_product_ready")
        x_updated = K.sem(tag + "_x_updated")
        flat = lambda x: x.rearrange("p a t -> p (a t)")
        with nc.Block(no_gpsimd_drain=True) as block:
            @block.sync
            def _(sync):
                K.load_slabs(sync, n0 + FK + 12 + RING)

            @block.gpsimd
            def _(pool):
                split.pool(pool)

            @block.scalar
            def _(act):
                norm.act(act, between=lambda: split.act(act, 2))
                for i in range(N):
                    split.act(act, 2 * i + 4)
                    K.wait_slabs(act, n0 + 2 * i + 1)
                    if i >= 2:
                        act.wait_ge(product_ready, i - 1)
                    act.activation(gate[:, i % 2, :], K.bank[2 * (i % 2)][:, :], ACT.Silu).then_inc(silu_ready, 1)
                    split.act(act, 2 * i + 5)
                    act.wait_ge(product_ready, i + 1)
                    act.copy(flat(hidden.hi[:, pair_of(i), :]), whole_hidden[:, i % 2, :]).then_inc(hidden.hi_ready, 1)
                split.act(act, FK + 12)

            @block.tensor
            def _(pe):
                norm.pe(pe)
                for i in range(N):
                    for part in range(2):
                        w = split.next_view(pe)
                        if i >= 2:
                            pe.wait_ge(product_ready, i - 1)
                        K.slab_done(feature_major3(pe, K.bank[2 * (i % 2) + part], w, (parts.hi, parts.lo), KD, HALF,
                                                   first=(lambda k: pe.wait_ge(parts.lo_ready, k // 2 + 1))
                                                   if i == part == 0 else None))
                pe.wait_ge(product_ready, N)
                ffn_out_pe(K, pe, split, hidden, x_updated)

            @block.vector
            def _(dve):
                norm.dve(dve)
                for i in range(N + 1):
                    if i < N:
                        dve.wait_ge(silu_ready, i + 1)
                        K.wait_slabs(dve, n0 + 2 * i + 2)
                        if i >= 2:
                            dve.wait_ge(hidden.lo_ready, i - 1)
                        dve.tensor_tensor(whole_hidden[:, i % 2, :], gate[:, i % 2, :],
                                          K.bank[2 * (i % 2) + 1][:, :], ALU.mult).then_inc(product_ready, 1)
                    if i >= 1:
                        hidden.dve(dve, pair_of(i - 1),
                                   whole_hidden[:, (i - 1) % 2, :].rearrange("p (a t) -> p a t", a=2))
                for jj in range(4):
                    K.wait_slabs(dve, n0 + FK + 3 * (jj + 1))
                    for j in range(2):
                        k = 2 * jj + j
                        dve.scalar_tensor_tensor(K.x[:, k, :], K.bank[2 * (jj % 2) + j][:, 0:T], 0.5, K.x[:, k, :],
                                                 ALU.mult, ALU.add).then_inc(x_updated, 1)


def ffn_slabs(w_in, w_out):
    slabs = []
    for i in range(FK // 2):
        slabs += [whole(w_in, i * HALF), whole(w_in, FFN + i * HALF)]
    for jj in range(4):
        for k0 in (0, 8, 16):
            g = min(KD, FK - k0)
            slabs.append([(groups_of(w_out, k0, g, jj * HALF, HALF), P, 0, g, HALF)])
    return slabs


def load_feature_major(K, block_ctx, tag, src, dst, banks, queue="sync"):
    rows = K.sb(tag + "_rows", [P, TT, D], ctx=block_ctx)
    arrived, turned, copied = K.sem(tag + "_arrived"), K.sem(tag + "_turned"), K.sem(tag + "_copied")

    def start(eng):
        eng.dma_start(rows[:, :, :], src.rearrange("(t p) d -> p t d", p=P)).then_inc(arrived, 16)

    def pe_part(pe):
        pe.wait_ge(arrived, 16)
        for i in range(4):
            bank = K.bank[banks[i % len(banks)]]
            if i >= len(banks):
                pe.wait_ge(copied, i - len(banks) + 1)
            for j in range(2):
                for tt in range(TT):
                    last = pe.transpose(bank[:, j * T + tt * P:j * T + (tt + 1) * P],
                                        rows[:, tt, (2 * i + j) * P:(2 * i + j + 1) * P], K.c("ident"))
            last.then_inc(turned, 1)

    def act_part(act):
        for i in range(4):
            act.wait_ge(turned, i + 1)
            act.copy(dst[:, 2 * i:2 * i + 2, :].rearrange("p a t -> p (a t)"), K.bank[banks[i % len(banks)]][:, :])\
                .then_inc(copied, 1)
    return start, pe_part, act_part, copied


def prologue(K):
    nc, a = K.nc, K.a
    first = K.first
    K.consts[1] = K.sb("const1", [P, CONSTS[1].shape[1]], ctx=first)
    K.mem = K.sb("mem", [P, KD, T], ctx=first)
    K.cos = K.sb("cos", [P, T], ctx=first)
    K.sin = K.sb("sin", [P, T], ctx=first)
    with ExitStack() as ctx:
        pos_i = K.sb("pos_i", [1, T], I32, ctx=ctx)
        pos = K.sb("pos", [1, T], ctx=ctx)
        ang = K.sb("ang", [P, T], ctx=ctx)
        turns = K.sb("turns", [P, T], ctx=ctx)
        quarter = K.sb("quarter", [P, T], ctx=ctx)
        over = K.sb("over", [P, T], ctx=ctx)
        consts_in, pos_in = K.sem("consts_in"), K.sem("pos_in")
        pos_ready, pos_spread, angles_ready = K.sem("pos_ready"), K.sem("pos_spread"), K.sem("angles_ready")
        x_start, x_pe, x_act, x_copied = load_feature_major(K, ctx, "x", a["x"][0], K.x, (0, 1))
        mem_in = K.sb("mem_in", [P, KD, T], ctx=ctx)
        m_start, m_pe, m_act, m_copied = load_feature_major(K, ctx, "mem", a["mem"][0], mem_in, (2, 3))
        norm = Norm(K, ctx, "mem", mem_in, K.mem, K.c("ones")[:, 0:KD], K.bank[4])
        with nc.Block(no_gpsimd_drain=True) as block:
            @block.sync
            def _(sync):
                for i in range(2):
                    sync.dma_start(K.consts[i][:, :], a[f"consts{i}"]).then_inc(consts_in, 16)
                x_start(sync)
                m_start(sync)
                sync.dma_start(pos_i[:, :], a["positions"]).then_inc(pos_in, 16)

            @block.scalar
            def _(act):
                act.wait_ge(consts_in, 32)
                x_act(act)
                m_act(act)
                act.wait_ge(m_copied, 4)
                norm.act(act)
                act.wait_ge(angles_ready, 1)
                act.activation(K.sin[:, :], ang[:, :], ACT.Sin)
                act.activation(K.cos[:, :], quarter[:, :], ACT.Sin)

            @block.tensor
            def _(pe):
                pe.wait_ge(consts_in, 32)
                x_pe(pe)
                m_pe(pe)
                norm.pe(pe)
                pe.wait_ge(pos_ready, 1)
                pe.matmul(K.bank[5][:, 0:T], K.c("ones", slice(0, 1)), pos[:, :], start=True, stop=True)\
                    .then_inc(pos_spread, 1)

            @block.vector
            def _(dve):
                own = K.dve_own
                dve.wait_ge(consts_in, 32)
                dve.wait_ge(pos_in, 16)
                dve.tensor_copy(pos[:, :], pos_i[:, :]).then_inc(pos_ready, 1)
                norm.dve(dve)
                dve.wait_ge(pos_spread, 1)
                own.after(dve, dve.tensor_scalar(ang[:, :], K.bank[5][:, 0:T], K.c("freq"), None, ALU.mult))
                own.after(dve, dve.tensor_scalar(turns[:, :], ang[:, :], float(1 / (2 * np.pi)), 12582912.0,
                                                 ALU.mult, ALU.add))
                own.after(dve, dve.tensor_scalar(turns[:, :], turns[:, :], 12582912.0, None, ALU.subtract))
                for part in (6.28125, 2029.0 / 2 ** 20, 2 * np.pi - 6.28125 - 2029.0 / 2 ** 20):
                    own.after(dve, dve.scalar_tensor_tensor(ang[:, :], turns[:, :], -float(part), ang[:, :],
                                                            ALU.mult, ALU.add))
                own.after(dve, dve.tensor_scalar(quarter[:, :], ang[:, :], float(np.pi / 2), None, ALU.add))
                own.after(dve, dve.tensor_scalar(over[:, :], quarter[:, :], float(np.pi), float(2 * np.pi),
                                                 ALU.is_gt, ALU.mult))
                own.after(dve, dve.tensor_tensor(quarter[:, :], quarter[:, :], over[:, :], ALU.subtract))
                own.after(dve, dve.tensor_scalar(quarter[:, :], quarter[:, :], 3.1415925, -3.1415925, ALU.min, ALU.max))
                dve.tensor_scalar(ang[:, :], ang[:, :], 3.1415925, -3.1415925, ALU.min, ALU.max)\
                    .then_inc(angles_ready, 1)


def load_params(K, l):
    nc, a = K.nc, K.a
    with ExitStack() as ctx:
        rows = K.sb("param_rows", [P, P], ctx=ctx)
        cleared, arrived, turned = K.sem("prm_cleared"), K.sem("prm_arrived"), K.sem("prm_turned")

        def layer(name):
            return a[name][bass.ds(l, 1), :]
        pieces = []
        for name, key, n in (("ffn1_norm", "ffn1_norm", 8), ("mix_norm", "mix_norm", 8), ("xattn_norm", "xattn_norm", 8),
                             ("xattn_mem_norm", "xattn_mem_norm", 8), ("ffn2_norm", "ffn2_norm", 8),
                             ("w0", "rwkv_w0", 4), ("a0", "rwkv_a0", 4), ("k_k", "rwkv_k_k", 4), ("k_a", "rwkv_k_a", 4),
                             ("ln_w", "rwkv_ln_w", 4), ("ln_b", "rwkv_ln_b", 4), ("xq", "xattn_q_gain", 1),
                             ("xk", "xattn_k_gain", 1)):
            r = PARAM_ROWS[name]
            pieces.append((rows[r:r + n, :], layer(key).rearrange("a (r c) -> (a r) c", c=P)))
        r = PARAM_ROWS["mu_rkv"]
        pieces.append((rows[r:r + 12, :], layer("rwkv_mu")[:, 0:1536].rearrange("a (r c) -> (a r) c", c=P)))
        r = PARAM_ROWS["mu_wa"]
        pieces.append((rows[r:r + 2, :], layer("rwkv_mu")[:, 1536:1792].rearrange("a (r c) -> (a r) c", c=P)))
        pieces.append((rows[r + 2:r + 3, 0:32], layer("rwkv_mu")[:, 1792:1824]))
        r = PARAM_ROWS["r_k"]
        pieces.append((rows[r:r + 4, :], a["rwkv_r_k"][bass.ds(l, 1), :, :].rearrange("a (r h) d -> (a r) (h d)", h=2)))
        for name, key in (("fox_q", "fox_q_gain"), ("fox_k", "fox_k_gain"), ("moba_q", "moba_q_gain"),
                          ("moba_k", "moba_k_gain")):
            r = PARAM_ROWS[name]
            pieces += [(rows[r:r + 1, 0:64], layer(key)), (rows[r:r + 1, 64:128], layer(key))]
        r = PARAM_ROWS["f_bias"]
        pieces.append((rows[r:r + 1, 0:4], layer("fox_f_bias")))
        with nc.Block(no_gpsimd_drain=True) as block:
            @block.vector
            def _(dve):
                dve.memset(rows[:, :], 0.0).then_inc(cleared, 1)
                dve.wait_ge(turned, 1)
                dve.tensor_copy(K.prm[:, :], K.bank[7][:, 0:P])

            @block.sync
            def _(sync):
                sync.wait_ge(cleared, 1)
                for dst, src in pieces:
                    sync.dma_start(dst, src).then_inc(arrived, 16)
                K.load_slabs(sync, RING)

            @block.tensor
            def _(pe):
                pe.wait_ge(arrived, 16 * len(pieces))
                pe.transpose(K.bank[7][:, 0:P], rows[:, :], K.c("ident")).then_inc(turned, 1)


def epilogue(K, gain=None):
    nc = K.nc
    with ExitStack() as ctx:
        rows = K.sb("out_rows", [P, TT, D], ctx=ctx)
        turned, copied, stored = K.sem("out_turned"), K.sem("out_copied"), K.sem("out_stored")
        with nc.Block() as block:
            @block.tensor
            def _(pe):
                for i in range(4):
                    for j in range(4):
                        last = pe.transpose(K.bank[i][:, j * P:(j + 1) * P],
                                            K.h[:, 4 * (i % 2) + j, (i // 2) * P:(i // 2 + 1) * P], K.c("ident"))
                    last.then_inc(turned, 1)

            @block.scalar
            def _(act):
                for i in range(4):
                    act.wait_ge(turned, i + 1)
                    act.copy(rows[:, i // 2, (i % 2) * 512:(i % 2 + 1) * 512], K.bank[i][:, :]).then_inc(copied, 1)

            @block.sync
            def _(sync):
                for t in range(TT):
                    sync.wait_ge(copied, 2 * t + 2)
                    sync.dma_start(K.out[0, t * P:(t + 1) * P, :], rows[:, t, :]).then_inc(stored, 16)
                sync.wait_ge(stored, 16 * TT)


def layer_slabs(K, l):
    def w(name):
        return K.a[name][bass.ds(l, 1), :, :]
    mix = w("mix_w_in")
    slabs = ffn_slabs(w("ffn1_w_in"), w("ffn1_w_out"))
    slabs += mix_slabs(K, mix, l)
    slabs += [whole(w("mix_w_out"), i * HALF) for i in range(4)]
    slabs += xattn_slabs(K, l)
    slabs += ffn_slabs(w("ffn2_w_in"), w("ffn2_w_out"))
    return slabs



MIX_ORDER = ([("wa", RW0 + 1536, 128), ("g", RW0 + 1664, 160)]
             + [("k", RW0 + 512 + i * HALF, HALF) for i in range(2)]
             + [("r", RW0 + i * HALF, HALF) for i in range(2)]
             + [("v", RW0 + 1024 + i * HALF, HALF) for i in range(2)]
             + [("fox_q", 0, HALF), ("fox_k", 256, HALF), ("fox_v", 512, HALF)]
             + [("moba_q", FOX_IN, HALF), ("moba_k", FOX_IN + 256, HALF), ("moba_v", FOX_IN + 512, HALF)])


def mix_slabs(K, w, l):
    slabs = []
    for name, c0, cols in MIX_ORDER:
        pieces = [(groups_of(w, 0, KD, c0, cols), P, 0, KD, cols)]
        if name == "wa":
            pieces.append((groups_of(w, 0, KD, 768, 4), P, KD * 128, KD, 4))
        slabs.append(pieces)
    return slabs


def mixer(K, l):
    with ExitStack() as ctx:
        s = K.mx = {}
        s["y"] = K.sb("y", [P, KD, T], ctx=ctx)
        s["qk"] = K.sb("qk", [P, 8, T], ctx=ctx)
        s["v"] = K.sb("vtok", [P, TT, 512], ctx=ctx)
        s["f"] = K.sb("f", [4, T], ctx=ctx)
        with ExitStack() as rctx:
            s["ar"] = K.sb("ar", [P, 4, TT, 2, P], ctx=rctx)
            for n in ("kt", "bt", "bv", "g"):
                s[n] = K.sb(n, [P, 4, T], ctx=rctx)
            for n in ("ktok", "btok", "vtok_r"):
                s[n] = K.sb(n, [P, TT, 512], ctx=rctx)
            s["es"] = K.sb("es", [P, 4, 4], ctx=rctx)
            project_stage(K, l)
            rwkv_stage(K)
        attention_stage(K)
        mix_out_stage(K)


def project_stage(K, l):
    nc, s = K.nc, K.mx
    n0 = K.eaten
    n_slabs = len(MIX_ORDER)
    with ExitStack() as ctx:
        t3 = lambda name: K.sb(name, [P, 4, T], ctx=ctx)
        z = K.sb("z", [P, 12, T + 1], ctx=ctx)
        zs = K.sb("zs", [P, 3, T + 1], ctx=ctx)
        diff = K.sb("diff", [P, 2, T], ctx=ctx)
        kk, sq, nrm, rate, lw, cum = t3("kk"), t3("sq"), t3("nrm"), t3("rate"), t3("lw"), t3("cum")
        dd, d3, kp = t3("dd"), t3("d3"), t3("kp")
        w2a2 = K.sb("w2a2", [P, 512], ctx=ctx)
        g2 = K.sb("g2", [P, 2, 512], ctx=ctx)
        om = K.sb("om", [P, 4], ctx=ctx)
        norm = Norm(K, ctx, "mix", K.x, K.h, K.col("mix_norm", KD), K.bank[4],
                    sq=K.sb("squares", [P, KD, T], ctx=ctx))
        e1, e3, e2 = norm.sq[:, 0:4, :], norm.sq[:, 4:8, :], sq
        lora_in, z_ready, mixed = K.sem("lora_in"), K.sem("z_ready"), K.sem("mixed")
        ranks_ready, lora_ready, lora_read = K.sem("ranks_ready"), K.sem("lora_ready"), K.sem("lora_read")
        kk_ready, kk_squared, kk_summed, kk_norm = K.sem("kk_ready"), K.sem("kk_squared"), K.sem("kk_summed"), K.sem("kk_norm")
        decay_diff, decays_ready = K.sem("decay_diff"), K.sem("decays_ready")
        bonus_in, bonus_summed, bonus_read = K.sem("bonus_in"), K.sem("bonus_summed"), K.sem("bonus_read")
        turn_in, turned, turn_copied = K.sem("turn_in"), K.sem("turned"), K.sem("turn_copied")
        z_cleared = K.sem("z_cleared")

        def bank4(b):
            return K.bank[b][:, :].rearrange("p (a t) -> p a t", a=2)

        with nc.Block(no_gpsimd_drain=True) as block:
            @block.sync
            def _(sync):
                sync.dma_start(w2a2[0:64, :], K.a["rwkv_w2"][bass.ds(l, 1), :, :].rearrange("a k n -> (a k) n"))\
                    .then_inc(lora_in, 16)
                sync.dma_start(w2a2[64:128, :], K.a["rwkv_a2"][bass.ds(l, 1), :, :].rearrange("a k n -> (a k) n"))\
                    .then_inc(lora_in, 16)
                sync.dma_start(g2[:, 0, :], K.a["rwkv_g2"][bass.ds(l, 1), 0:128, :].rearrange("a k n -> (a k) n"))\
                    .then_inc(lora_in, 16)
                sync.dma_start(g2[0:32, 1, :], K.a["rwkv_g2"][bass.ds(l, 1), 128:160, :].rearrange("a k n -> (a k) n"))\
                    .then_inc(lora_in, 16)
                K.load_slabs(sync, n0 + n_slabs + RING)

            def evacuate(act, n):
                name = MIX_ORDER[n][0]
                K.wait_slabs(act, n0 + n + 1)
                b = K.bank[n % 4]
                if name == "wa":
                    act.copy(s["f"][:, :], b[0:4, T:2 * T])
                    ins = act.copy(zs[:, 0, 1:], b[:, 0:T])
                elif name == "g":
                    act.copy(zs[:, 1, 1:], b[:, 0:T])
                    ins = act.copy(zs[0:32, 2, 1:], b[0:32, T:2 * T])
                elif name in ("r", "k", "v"):
                    i = {"k": 2, "r": 4, "v": 6}[name]
                    t = {"r": 0, "k": 4, "v": 8}[name] + 2 * (n - i)
                    ins = act.copy(z[:, t:t + 2, 1:], bank4(n % 4))
                elif name.endswith("_v"):
                    c = 0 if name == "fox_v" else HALF
                    ins = act.copy(s["v"][:, :, c:c + HALF], bank4(n % 4))
                else:
                    t = {"fox_q": 0, "fox_k": 2, "moba_q": 4, "moba_k": 6}[name]
                    ins = act.copy(s["qk"][:, t:t + 2, :], bank4(n % 4))
                ins.then_inc(z_ready, 1)

            @block.scalar
            def _(act):
                norm.act(act)
                for n in range(8):
                    evacuate(act, n)
                act.wait_ge(mixed, 2)
                act.activation(zs[0:64, 0, 1:], zs[0:64, 0, 1:], ACT.Tanh)
                act.activation(zs[:, 1, 1:], zs[:, 1, 1:], ACT.Sigmoid)
                act.activation(zs[0:32, 2, 1:], zs[0:32, 2, 1:], ACT.Sigmoid).then_inc(ranks_ready, 1)
                for n in range(8, 11):
                    evacuate(act, n)
                act.wait_ge(lora_ready, 1)
                for t in range(4):
                    act.activation(lw[:, t, :], K.bank[4 + t // 2][:, (t % 2) * T:(t % 2 + 1) * T], ACT.Sigmoid,
                                   bias=K.col("w0", 4)[:, t:t + 1])
                for t in range(4):
                    last = act.activation(rate[:, t, :], K.bank[6 + t // 2][:, (t % 2) * T:(t % 2 + 1) * T], ACT.Sigmoid,
                                          bias=K.col("a0", 4)[:, t:t + 1])
                last.then_inc(lora_read, 1)
                act.wait_ge(kk_ready, 1)
                act.activation(sq[:, :, :], kk[:, :, :], ACT.Square).then_inc(kk_squared, 1)
                for n in range(11, 14):
                    evacuate(act, n)
                act.wait_ge(lora_ready, 2)
                for i in range(2):
                    last = act.copy(s["g"][:, 2 * i:2 * i + 2, :], bank4(4 + i))
                last.then_inc(lora_read, 1)
                act.wait_ge(kk_summed, 1)
                for i in range(2):
                    last = act.activation(nrm[:, 2 * i:2 * i + 2, :], bank4(6 + i), ACT.Sqrt)
                last.then_inc(kk_norm, 1)
                act.wait_ge(decay_diff, 1)
                act.activation(e1[:, :, :], dd[:, :, :], ACT.Exp)
                act.activation(e2[:, :, :], dd[:, :, :], ACT.Exp, scale=-1.0)
                act.activation(e3[:, :, :], d3[:, :, :], ACT.Exp)
                act.activation(s["es"][:, :, 0:3], s["es"][:, :, 0:3], ACT.Exp).then_inc(decays_ready, 1)
                for i, dst in enumerate(("vtok_r", "vtok_r", "ktok", "ktok", "btok", "btok")):
                    act.wait_ge(turned, i + 1)
                    act.copy(s[dst][:, i % 2, :], K.bank[i % 4][:, :]).then_inc(turn_copied, 1)

            @block.tensor
            def _(pe):
                norm.pe(pe)
                pe.wait_ge(norm.h_ready, KD)

                def project(n):
                    name, _, cols = MIX_ORDER[n]
                    place = K.next_slab(pe)
                    if n >= 4:
                        pe.wait_ge(z_ready, n - 3)
                    if name.endswith("_v"):
                        last = token_major(K, pe, K.bank[n % 4], view(place), K.h, KD, HALF)
                    else:
                        last = feature_major(K, pe, K.bank[n % 4], view(place, cols=cols), K.h, KD, cols)
                    if name == "wa":
                        last = feature_major(K, pe, K.bank[n % 4], view(place, cols=4, start=KD * 128), K.h, KD, 4, at=T)
                    K.slab_done(last)
                for n in range(11):
                    project(n)
                pe.wait_ge(lora_in, 64)
                pe.wait_ge(ranks_ready, 1)
                for half, banks in ((slice(0, 64), 4), (slice(64, 128), 6)):
                    for t in range(4):
                        last = pe.matmul(K.bank[banks + t // 2][:, (t % 2) * T:(t % 2 + 1) * T],
                                         w2a2[half, t * P:(t + 1) * P], zs[half, 0, 1:], start=True, stop=True)
                last.then_inc(lora_ready, 1)
                for n in range(11, 14):
                    project(n)
                pe.wait_ge(lora_read, 1)
                for t in range(4):
                    o = K.bank[4 + t // 2][:, (t % 2) * T:(t % 2 + 1) * T]
                    pe.matmul(o, g2[:, 0, t * P:(t + 1) * P], zs[:, 1, 1:], start=True, stop=False)
                    last = pe.matmul(o, g2[0:32, 1, t * P:(t + 1) * P], zs[0:32, 2, 1:], start=False, stop=True)
                last.then_inc(lora_ready, 1)
                pe.wait_ge(kk_squared, 1)
                for i in range(2):
                    last = pe.matmul(K.bank[6 + i][:, :], K.c("headsum"),
                                     sq[:, 2 * i:2 * i + 2, :].rearrange("p a t -> p (a t)"), start=True, stop=True)
                last.then_inc(kk_summed, 1)
                pe.wait_ge(lora_read, 2)
                pe.wait_ge(bonus_in, 1)
                for i in range(2):
                    last = pe.matmul(K.bank[4 + i][:, :], K.c("headsum"),
                                     dd[:, 2 * i:2 * i + 2, :].rearrange("p a t -> p (a t)"), start=True, stop=True)
                last.then_inc(bonus_summed, 1)
                pe.wait_ge(z_ready, 14)
                for i in range(6):
                    if i >= 4:
                        pe.wait_ge(turn_copied, i - 3)
                    pe.wait_ge(turn_in, i // 2)
                    for t in range(4):
                        tok = slice((i % 2) * P, (i % 2 + 1) * P)
                        src = (z[:, 8 + t, 1:][:, tok], s["kt"][:, t, tok], s["bt"][:, t, tok])[i // 2]
                        last = pe.transpose(K.bank[i % 4][:, t * P:(t + 1) * P], src, K.c("ident"))
                    last.then_inc(turned, 1)

            @block.vector
            def _(dve):
                own = K.dve_own
                dve.memset(z[:, :, 0:1], 0.0)
                own.after(dve, dve.memset(zs[:, :, 0:1], 0.0))
                norm.dve(dve)
                for n in range(8):
                    dve.wait_ge(z_ready, n + 1)
                    if n:
                        dve.wait_ge(mixed, n)
                    name = MIX_ORDER[n][0]
                    if name in ("wa", "g"):
                        tiles = [(zs, 0, P, K.col("mu_wa"))] if name == "wa" else \
                            [(zs, 1, P, K.col("mu_g")), (zs, 2, 32, K.prm[:, PARAM_ROWS["mu_g"] + 1:PARAM_ROWS["mu_g"] + 2])]
                    else:
                        t0 = {"r": 0, "k": 4, "v": 8}[name] + 2 * (n - {"k": 2, "r": 4, "v": 6}[name])
                        tiles = [(z, t0 + j, P, K.col("mu_rkv", 12)[:, t0 + j:t0 + j + 1]) for j in range(2)]
                    for j, (zz, t, m, mu) in enumerate(tiles):
                        last = dve.tensor_tensor(diff[0:m, j, :], zz[0:m, t, 0:T], zz[0:m, t, 1:T + 1], ALU.subtract)
                    own.after(dve, last)
                    for j, (zz, t, m, mu) in enumerate(tiles):
                        last = dve.scalar_tensor_tensor(zz[0:m, t, 1:], diff[0:m, j, :], mu[0:m, :], zz[0:m, t, 1:],
                                                        ALU.mult, ALU.add)
                    last.then_inc(mixed, 1)
                dve.wait_ge(mixed, 8)
                r, k, v = z[:, 0:4, 1:], z[:, 4:8, 1:], z[:, 8:12, 1:]
                for t in range(4):
                    last = dve.tensor_scalar(kk[:, t, :], k[:, t, :], K.col("k_k", 4)[:, t:t + 1], None, ALU.mult)
                last.then_inc(kk_ready, 1)
                own.after(dve, dve.tensor_scalar(om[:, :], K.col("k_a", 4), -1.0, 1.0, ALU.mult, ALU.add))
                dve.wait_ge(lora_read, 1)
                for t in range(4):
                    last = dve.tensor_scalar(kp[:, t, :], rate[:, t, :], K.col("k_a", 4)[:, t:t + 1], om[:, t:t + 1],
                                             ALU.mult, ALU.add)
                own.after(dve, last)
                own.after(dve, dve.tensor_tensor(kp[:, :, :], kp[:, :, :], k, ALU.mult))
                for t in range(4):
                    last = dve.scalar_tensor_tensor(dd[:, t, :], r[:, t, :], K.col("r_k", 4)[:, t:t + 1], kp[:, t, :],
                                                    ALU.mult, ALU.mult)
                last.then_inc(bonus_in, 1)
                flat = lambda x: x[:, :, :].rearrange("p a t -> p (a t)")
                own.after(dve, dve.tensor_scalar(flat(lw), flat(lw), -DECAY, None, ALU.mult))
                own.after(dve, dve.tensor_tensor_scan(flat(cum), K.c("gate"), flat(lw), 0.0, ALU.mult, ALU.add))
                chunks = lambda x: flat(x).rearrange("p (g c) -> p g c", c=CH)
                mid = chunks(cum)[:, :, CH // 2 - 1:CH // 2]
                c4 = cum[:, :, :].rearrange("p a (g c) -> p a g c", c=CH)
                end4, mid4 = c4[:, :, :, CH - 1], c4[:, :, :, CH // 2 - 1]
                own.after(dve, dve.tensor_tensor(s["es"][:, :, 0:3], end4[:, :, 0:3], mid4[:, :, 0:3], ALU.subtract))
                own.after(dve, dve.tensor_tensor(s["es"][:, :, 0:3], s["es"][:, :, 0:3], mid4[:, :, 1:4], ALU.add))
                dve.wait_ge(bonus_summed, 1)
                own.after(dve, dve.tensor_tensor(chunks(dd), chunks(cum), mid.to_broadcast([P, 16, CH]), ALU.subtract))
                dve.tensor_tensor(flat(d3), flat(dd), flat(lw), ALU.subtract).then_inc(decay_diff, 1)
                for i in range(2):
                    last = dve.tensor_tensor(s["bv"][:, 2 * i:2 * i + 2, :], bank4(4 + i), v[:, 2 * i:2 * i + 2, :],
                                             ALU.mult)
                dve.wait_ge(kk_norm, 1)
                own.after(dve, dve.tensor_scalar(flat(nrm), flat(nrm), 1e-12, None, ALU.max))
                own.after(dve, dve.reciprocal(flat(nrm), flat(nrm)))
                own.after(dve, dve.tensor_tensor(flat(kk), flat(kk), flat(nrm), ALU.mult))
                own.after(dve, dve.tensor_tensor(flat(rate), flat(rate), flat(kk), ALU.mult))
                dve.wait_ge(decays_ready, 1)
                dve.tensor_tensor(flat(s["kt"]), flat(kp), flat(e2), ALU.mult).then_inc(turn_in, 1)
                dve.tensor_tensor(flat(s["bt"]), flat(rate), flat(e2), ALU.mult).then_inc(turn_in, 1)
                for tt in range(TT):
                    tok = slice(tt * P, (tt + 1) * P)
                    dve.tensor_tensor(s["ar"][:, :, tt, 0, :], kk[:, :, tok], e3[:, :, tok], ALU.mult)
                    dve.tensor_tensor(s["ar"][:, :, tt, 1, :], r[:, :, tok], e1[:, :, tok], ALU.mult)


class Inverse:

    def __init__(self, K, ctx, tag, groups, levels, masks, lt, xt, before):
        self.K, self.groups, self.levels, self.masks = K, groups, levels, masks
        self.lt, self.xt, self.before = lt, xt, before
        f = lambda name: [K.sb(f"{name}{i}", [P, 4, P], ctx=ctx) for i in range(2)]
        self.X, self.T1 = f("inv_x"), f("inv_t")
        self.mask = [[K.sb(f"inv_m{s}{j}", [P, 4, P], ctx=ctx) for j in range(2)] for s in range(2)]
        self.m_ready, self.t_ready = K.sem(tag + "_part_ready"), K.sem(tag + "_first_ready")
        self.t_copied, self.uv_ready = K.sem(tag + "_first_copied"), K.sem(tag + "_second_ready")
        self.x_ready = K.sem(tag + "_x_ready")
        self.steps = [(pair * 2 + s, l) for pair in range(groups // 2) for l in range(levels) for s in range(2)]
        self.index = {st: i for i, st in enumerate(self.steps)}
        self.update = {st: i for i, st in enumerate([st for st in self.steps if st[1] > 0])}

    def final(self, g):
        return self.update[(g, self.levels - 1)] + 1

    def pool(self, pool):
        K = self.K
        for i, (g, l) in enumerate(self.steps):
            s = g % 2
            m = self.mask[s][l % 2]
            if l == 0:
                self.before(pool, g)
            prev = [j for j in range(i) if self.steps[j][0] % 2 == s and self.steps[j][1] % 2 == l % 2]
            if prev:
                pool.wait_ge(self.t_ready, prev[-1] + 1)
            level = K.c(self.masks, first=l * P, n=P).unsqueeze(1).to_broadcast([P, 4, P])
            ins = pool.tensor_tensor(m[:, :, :], self.lt(g), level, ALU.mult)
            if l == 0:
                K.pool_own.after(pool, ins)
                ident = K.c("ident").unsqueeze(1).to_broadcast([P, 4, P])
                ins = pool.tensor_tensor(self.xt(g), ident, m[:, :, :], ALU.subtract)
            ins.then_inc(self.m_ready, 1)

    def pe(self, pe, extra=None):
        K = self.K
        for i0 in range(0, len(self.steps), 2):
            for i in (i0, i0 + 1):
                g, l = self.steps[i]
                s = g % 2
                bank = K.bank[2 + 3 * s]
                pe.wait_ge(self.m_ready, i + 1)
                if l == 0:
                    for q in range(4):
                        last = pe.transpose(bank[:, q * P:(q + 1) * P], self.xt(g)[:, q, :], K.c("ident"))
                else:
                    if l == 1:
                        pe.wait_ge(self.t_copied, self.index[(g, 0)] + 1)
                    else:
                        pe.wait_ge(self.x_ready, self.update[(g, l - 1)] + 1)
                    for q in range(4):
                        last = pe.matmul(bank[:, q * P:(q + 1) * P], self.mask[s][l % 2][:, q, :], self.X[s][:, q, :],
                                         start=True, stop=True)
                last.then_inc(self.t_ready, 1)
            if self.steps[i0][1] == 0:
                continue
            for i in (i0, i0 + 1):
                g, l = self.steps[i]
                s = g % 2
                pe.wait_ge(self.t_copied, i + 1)
                if l == 1 and g >= 2:
                    pe.wait_ge(self.x_ready, self.final(g - 2))
                if l < self.levels - 1:
                    for q in range(4):
                        pe.matmul(K.bank[3 + 3 * s][:, q * P:(q + 1) * P], self.xt(g)[:, q, :], self.T1[s][:, q, :],
                                  start=True, stop=True)
                for q in range(4):
                    last = pe.matmul(K.bank[4 + 3 * s][:, q * P:(q + 1) * P], self.T1[s][:, q, :], self.xt(g)[:, q, :],
                                     start=True, stop=True)
                last.then_inc(self.uv_ready, 1)

    def act(self, act):
        K = self.K
        for i, (g, l) in enumerate(self.steps):
            s = g % 2
            act.wait_ge(self.t_ready, i + 1)
            dst = self.X[s] if l == 0 else self.T1[s]
            act.copy(dst[:, :, :].rearrange("p a t -> p (a t)"), K.bank[2 + 3 * s][:, :]).then_inc(self.t_copied, 1)

    def dve(self, dve):
        K = self.K
        for (g, l) in self.steps:
            if l == 0:
                continue
            s = g % 2
            dve.wait_ge(self.uv_ready, self.update[(g, l)] + 1)
            if l < self.levels - 1:
                dve.tensor_tensor(self.X[s][:, :, :], self.X[s][:, :, :],
                                  K.bank[3 + 3 * s][:, :].rearrange("p (a t) -> p a t", a=4), ALU.subtract)
            dve.tensor_tensor(self.xt(g), self.xt(g), K.bank[4 + 3 * s][:, :].rearrange("p (a t) -> p a t", a=4),
                              ALU.subtract).then_inc(self.x_ready, 1)


def rwkv_stage(K):
    nc, s = K.nc, K.mx
    with ExitStack() as ctx:
        lt = K.sb("lt", [P, 16, 4, P], ctx=ctx)
        xt = K.sb("xt", [P, 16, P], ctx=ctx)
        unit = lambda t, tt, hh: 4 * t + 2 * tt + hh
        intra_ready, intra_read = K.sem("intra_ready"), K.sem("intra_read")
        with ExitStack() as ictx:
            inv = Inverse(K, ictx, "rinv", 4, 6, "levels", lambda g: lt[:, 4 * g:4 * g + 4, 0, :],
                          lambda g: xt[:, 4 * g:4 * g + 4, :], lambda eng, g: eng.wait_ge(intra_read, 4 * g + 4))
            with nc.Block(no_gpsimd_drain=True) as block:
                @block.tensor
                def _(pe):
                    for t in range(4):
                        for tt in range(TT):
                            for hh in range(2):
                                u = unit(t, tt, hh)
                                if u >= 2:
                                    pe.wait_ge(intra_read, u - 1)
                                half = slice(64 * hh, 64 * hh + 64)
                                rhs = s["ar"][half, t, tt, :, :].rearrange("p a t -> p (a t)")
                                for j, n in enumerate(("bt", "kt")):
                                    last = pe.matmul(K.bank[hh][:, j * T:(j + 1) * T],
                                                     s[n][half, t, tt * P:(tt + 1) * P], rhs, start=True, stop=True)
                                last.then_inc(intra_ready, 1)
                    inv.pe(pe)

                @block.vector
                def _(dve):
                    for u in range(16):
                        dve.wait_ge(intra_ready, u + 1)
                        dve.tensor_tensor(lt[:, u, :, :].rearrange("p a t -> p (a t)"), K.bank[u % 2][:, :],
                                          K.c("chunkmask"), ALU.mult).then_inc(intra_read, 1)
                    inv.dve(dve)

                @block.scalar
                def _(act):
                    inv.act(act)

                @block.gpsimd
                def _(pool):
                    inv.pool(pool)
        rwkv_scan(K, lt, xt, unit)


def rwkv_scan(K, lt, xt, unit):
    nc, s = K.nc, K.mx
    with ExitStack() as ctx:
        state = K.sb("state", [P, 4, P], ctx=ctx)
        tmp = K.sb("state_next", [P, 4, P], ctx=ctx)
        rhs = K.sb("rhs", [P, 512], ctx=ctx)
        sa = K.sb("sa", [P, TT, 512], ctx=ctx)
        y = K.sb("ysb", [P, 4, T], ctx=ctx)
        sq = K.sb("ysq", [P, 4, T], ctx=ctx)
        s_ready, rhs_ready, rhs_copied = K.sem("s_ready"), K.sem("rhs_ready"), K.sem("rhs_copied")
        sa_ready, sa_copied, st_ready = K.sem("sa_ready"), K.sem("sa_copied"), K.sem("st_ready")
        y_ready, y_copied, mean_ready = K.sem("y_ready"), K.sem("y_copied"), K.sem("mean_ready")
        centred, squared, var_ready, rstd_ready = K.sem("centred"), K.sem("y_squared"), K.sem("var_ready"), K.sem("y_rstd")
        flat = lambda x: x[:, :, :].rearrange("p a t -> p (a t)")
        bank4 = lambda b: K.bank[b][:, :].rearrange("p (a t) -> p a t", a=2)
        with nc.Block(no_gpsimd_drain=True) as block:
            @block.tensor
            def _(pe):
                for tt in range(TT):
                    Y = K.bank[3 + tt]
                    for t in range(4):
                        for hh in range(2):
                            col = slice(t * P + 64 * hh, t * P + 64 * hh + 64)
                            pe.matmul(Y[64 * hh:64 * hh + 64, t * P:(t + 1) * P], s["vtok_r"][:, tt, col],
                                      lt[:, unit(t, tt, hh), 3, :], start=(t == 0), stop=False, skip_group_check=True)
                    for p in range(2):
                        c = 2 * tt + p
                        rows, tok = slice(64 * p, 64 * p + 64), slice(64 * p, 64 * p + 64)
                        pe.wait_ge(s_ready, c + 1)
                        for t in range(4):
                            pe.matmul(K.bank[0][rows, t * P:(t + 1) * P], s["ar"][:, t, tt, 0, tok], state[:, t, :],
                                      start=True, stop=False)
                            for hh in range(2):
                                col = slice(t * P + 64 * hh, t * P + 64 * hh + 64)
                                last = pe.matmul(K.bank[0][rows, col], lt[rows, unit(t, tt, hh), 2, tok],
                                                 s["vtok_r"][rows, tt, col], start=False, stop=(hh == 1))
                        last.then_inc(rhs_ready, 1)
                        for t in range(4):
                            pe.matmul(Y[:, t * P + 64 * p:t * P + 64 * p + 64], state[:, t, :], s["ar"][:, t, tt, 1, tok],
                                      start=False, stop=False, skip_group_check=True)
                        pe.wait_ge(rhs_copied, c + 1)
                        for t in range(4):
                            for hh in range(2):
                                col = slice(t * P + 64 * hh, t * P + 64 * hh + 64)
                                last = pe.matmul(K.bank[1][rows, col], xt[rows, unit(t, tt, hh), tok], rhs[rows, col],
                                                 start=True, stop=True)
                        last.then_inc(sa_ready, 1)
                        pe.wait_ge(sa_copied, c + 1)
                        if c < 3:
                            for t in range(4):
                                col = slice(t * P, (t + 1) * P)
                                pe.matmul(K.bank[2][:, col], s["ktok"][rows, tt, col], s["vtok_r"][rows, tt, col],
                                          start=True, stop=False)
                                last = pe.matmul(K.bank[2][:, col], s["btok"][rows, tt, col], sa[rows, tt, col],
                                                 start=False, stop=True)
                            last.then_inc(st_ready, 1)
                    for t in range(4):
                        for hh in range(2):
                            col = slice(t * P + 64 * hh, t * P + 64 * hh + 64)
                            last = pe.matmul(Y[64 * hh:64 * hh + 64, t * P:(t + 1) * P], sa[:, tt, col],
                                             lt[:, unit(t, tt, hh), 1, :], start=False, stop=True, skip_group_check=True)
                    last.then_inc(y_ready, 1)
                pe.wait_ge(y_copied, 2)
                for i in range(2):
                    last = pe.matmul(K.bank[i][:, :], K.c("headsum"), flat(y)[:, i * 512:(i + 1) * 512],
                                     start=True, stop=True)
                last.then_inc(mean_ready, 1)
                pe.wait_ge(squared, 1)
                for i in range(2):
                    last = pe.matmul(K.bank[5 + i][:, :], K.c("headsum"), flat(sq)[:, i * 512:(i + 1) * 512],
                                     start=True, stop=True)
                last.then_inc(var_ready, 1)

            @block.vector
            def _(dve):
                own = K.dve_own
                dve.memset(state[:, :, :], 0.0).then_inc(s_ready, 1)
                for c in range(4):
                    tt, p = c // 2, c % 2
                    rows = slice(64 * p, 64 * p + 64)
                    dve.wait_ge(rhs_ready, c + 1)
                    dve.tensor_scalar(rhs[rows, :], K.bank[0][rows, :], -1.0, None, ALU.mult).then_inc(rhs_copied, 1)
                    dve.wait_ge(sa_ready, c + 1)
                    dve.tensor_copy(sa[rows, tt, :], K.bank[1][rows, :]).then_inc(sa_copied, 1)
                    if c < 3:
                        dve.wait_ge(st_ready, c + 1)
                        own.after(dve, dve.tensor_tensor(flat(tmp), K.bank[2][:, :], flat(state), ALU.add))
                        for t in range(4):
                            last = dve.scalar_tensor_tensor(state[:, t, :], tmp[:, t, :], s["es"][:, t, c:c + 1],
                                                            K.c("headsum"), ALU.mult, ALU.mult)
                        last.then_inc(s_ready, 1)
                dve.wait_ge(mean_ready, 1)
                for i in range(2):
                    last = dve.scalar_tensor_tensor(flat(y)[:, i * 512:(i + 1) * 512], K.bank[i][:, :], -1.0 / 64,
                                                    flat(y)[:, i * 512:(i + 1) * 512], ALU.mult, ALU.add)
                last.then_inc(centred, 1)
                dve.wait_ge(rstd_ready, 1)
                own.after(dve, dve.tensor_tensor(flat(y), flat(y), flat(sq), ALU.mult))
                for t in range(4):
                    last = dve.tensor_scalar(y[:, t, :], y[:, t, :], K.col("ln_w", 4)[:, t:t + 1],
                                             K.col("ln_b", 4)[:, t:t + 1], ALU.mult, ALU.add)
                own.after(dve, last)
                own.after(dve, dve.tensor_tensor(flat(y), flat(y), flat(s["bv"]), ALU.add))
                dve.tensor_tensor(s["y"][:, 2:6, :], y[:, :, :], s["g"][:, :, :], ALU.mult)

            @block.scalar
            def _(act):
                for tt in range(TT):
                    act.wait_ge(y_ready, tt + 1)
                    act.copy(y[:, :, tt * P:(tt + 1) * P], K.bank[3 + tt][:, :].rearrange("p (a t) -> p a t", a=4))\
                        .then_inc(y_copied, 1)
                act.wait_ge(centred, 1)
                act.activation(flat(sq), flat(y), ACT.Square).then_inc(squared, 1)
                act.wait_ge(var_ready, 1)
                for i in range(2):
                    last = act.activation(sq[:, 2 * i:2 * i + 2, :], bank4(5 + i), ACT.Ln, bias=K.c("gneps"), scale=1.0 / 64)
                K.act_own.after(act, last)
                act.activation(flat(sq), flat(sq), ACT.Exp, scale=-0.5).then_inc(rstd_ready, 1)



class Attention:

    def __init__(self, K, ctx, tag, units, banks, keys):
        self.K, self.units, self.banks = K, units, banks
        two = lambda name, n: [K.sb(f"{name}{i}", [P, n], ctx=ctx) for i in range(2)]
        self.scores, self.probs, self.normed, self.turned = (two(n, keys) for n in ("at_s", "at_p", "at_n", "at_t"))
        self.top, self.sum = two("at_max", 2), two("at_sum", 2)
        self.scores_ready = K.sem(f"{tag}_scores_ready")
        self.top_ready = K.sem(f"{tag}_top_ready")
        self.exp_done = K.sem(f"{tag}_exp_done")
        self.probs_ready = K.sem(f"{tag}_probs_ready")
        self.turn_ready = K.sem(f"{tag}_turn_ready")
        self.turn_copied = K.sem(f"{tag}_turn_copied")
        self.out_ready = K.sem(f"{tag}_out_ready")
        self.out_copied = K.sem(f"{tag}_out_copied")

    def pe(self, pe):
        U, K = self.units, self.K
        for i in range(len(U) + 2):
            if i < len(U):
                u, bank = U[i], K.bank[self.banks[i % 2]]
                if i >= 2:
                    pe.wait_ge(self.top_ready, i - 1)
                n = u["keys"]
                prods = [(u["q"], k, c) for k, c in u["k"]] + [(a, b, slice(0, n)) for a, b in u.get("bias", ())]
                regions = len(u["k"])
                for j, (a, b, c) in enumerate(prods):
                    last = pe.matmul(bank[:, c], a, b, start=(j < regions), stop=(j == len(prods) - 1 or len(prods) == regions))
                last.then_inc(self.scores_ready, 1)
            j = i - 1
            if 0 <= j < len(U):
                bank = K.bank[self.banks[2 + j % 2]]
                pe.wait_ge(self.probs_ready, j + 1)
                if j >= 2:
                    pe.wait_ge(self.turn_copied, j - 1)
                for c in range(U[j]["keys"] // P):
                    last = pe.transpose(bank[:, c * P:(c + 1) * P], self.normed[j % 2][:, c * P:(c + 1) * P], K.c("ident"))
                last.then_inc(self.turn_ready, 1)
            m = i - 2
            if m >= 0:
                u, bank = U[m], K.bank[self.banks[4 + m % 2]]
                pe.wait_ge(self.turn_copied, m + 1)
                if m >= 2:
                    pe.wait_ge(self.out_copied, m - 1)
                rows = u["rows"]
                nk = u["keys"] // P
                for c in range(nk):
                    last = pe.matmul(bank[rows, 0:P], u["v"][c], self.turned[m % 2][:, c * P:(c + 1) * P],
                                     start=(c == 0), stop=(c == nk - 1))
                last.then_inc(self.out_ready, 1)

    def dve(self, dve):
        U, K = self.units, self.K
        for i in range(len(U) + 1):
            if i < len(U):
                n = U[i]["keys"]
                s, top = self.scores[i % 2][:, 0:n], self.top[i % 2]
                dve.wait_ge(self.scores_ready, i + 1)
                if i >= 2:
                    dve.wait_ge(self.exp_done, i - 1)
                K.dve_own.after(dve, dve.tensor_tensor_reduce(
                    out=s, in0=K.bank[self.banks[i % 2]][:, 0:n], in1=U[i]["mask"], scale=1.0, scalar=-3.0e38,
                    op0=ALU.add, op1=ALU.max, accum_out=top[:, 0:1]))
                dve.tensor_scalar(top[:, 1:2], top[:, 0:1], -1.0, None, ALU.mult).then_inc(self.top_ready, 1)
            j = i - 1
            if j >= 0:
                n = U[j]["keys"]
                dve.wait_ge(self.exp_done, j + 1)
                K.dve_own.after(dve, dve.reciprocal(self.sum[j % 2][:, 1:2], self.sum[j % 2][:, 0:1]))
                if j >= 2:
                    dve.wait_ge(self.turn_ready, j - 1)
                dve.tensor_scalar(self.normed[j % 2][:, 0:n], self.probs[j % 2][:, 0:n], self.sum[j % 2][:, 1:2],
                                  None, ALU.mult).then_inc(self.probs_ready, 1)

    def act(self, act):
        U, K = self.units, self.K
        for i in range(len(U) + 2):
            if i < len(U):
                n = U[i]["keys"]
                act.wait_ge(self.top_ready, i + 1)
                if i >= 2:
                    act.wait_ge(self.probs_ready, i - 1)
                act.activation(self.probs[i % 2][:, 0:n], self.scores[i % 2][:, 0:n], ACT.Exp,
                               bias=self.top[i % 2][:, 1:2], accum_out=self.sum[i % 2][:, 0:1]).then_inc(self.exp_done, 1)
            j = i - 1
            if 0 <= j < len(U):
                n = U[j]["keys"]
                act.wait_ge(self.turn_ready, j + 1)
                if j >= 2:
                    act.wait_ge(self.out_ready, j - 1)
                act.copy(self.turned[j % 2][:, 0:n], K.bank[self.banks[2 + j % 2]][:, 0:n]).then_inc(self.turn_copied, 1)
            m = i - 2
            if m >= 0:
                act.wait_ge(self.out_ready, m + 1)
                act.copy(U[m]["out"], K.bank[self.banks[4 + m % 2]][U[m]["rows"], 0:P]).then_inc(self.out_copied, 1)


LOG1P = [1.0 / (2 * k + 1) for k in range(9)]


def softplus_small(dve, own, e, s, s2, q, out):
    own.after(dve, dve.tensor_scalar(s2, e, 2.0, None, ALU.add))
    own.after(dve, dve.reciprocal(s2, s2))
    own.after(dve, dve.tensor_tensor(s, e, s2, ALU.mult))
    own.after(dve, dve.tensor_tensor(s2, s, s, ALU.mult))
    own.after(dve, dve.tensor_scalar(q, s2, LOG1P[8], None, ALU.mult))
    for c in LOG1P[7:0:-1]:
        own.after(dve, dve.scalar_tensor_tensor(q, q, c, s2, ALU.add, ALU.mult))
    own.after(dve, dve.scalar_tensor_tensor(q, q, 1.0, s, ALU.add, ALU.mult))
    return dve.tensor_scalar(out, q, 2.0, None, ALU.mult)


def attention_stage(K):
    nc, s = K.nc, K.mx
    qk, v, f, y = s["qk"], s["v"], s["f"], s["y"]
    with ExitStack() as ctx:
        sq = K.sb("qksq", [P, 8, T], ctx=ctx)
        gains = K.sb("gains", [P, 2], ctx=ctx)
        rot = K.sb("rotd", [P, 2, T], ctx=ctx)
        fx, fs, fs2, fq, fc, fneg, fe = (K.sb(n, [4, T], ctx=ctx) for n in ("fx", "fs", "fs2", "fq", "fc", "fneg", "fe"))
        squared, summed, rstd_ready = K.sem("qk_squared"), K.sem("qk_summed"), K.sem("qk_rstd")
        normed, rotated, roped = K.sem("qk_normed"), K.sem("qk_rotated"), K.sem("qk_roped")
        fabs_ready, fexp_ready, fsum_ready = K.sem("f_abs"), K.sem("f_exp"), K.sem("f_sum")
        units = []
        for kind in range(2):
            for h in range(4):
                rows = slice(64 * (h % 2), 64 * (h % 2) + 64)
                for i in range(TT):
                    n = P * (i + 1)
                    u = {"keys": n, "rows": rows,
                         "q": qk[rows, 4 * kind + h // 2, i * P:(i + 1) * P],
                         "k": [(qk[rows, 4 * kind + 2 + h // 2, 0:n], slice(0, n))],
                         "mask": K.c("causal")[:, P - i * P:2 * P],
                         "v": [v[:, c, 256 * kind + 64 * h:256 * kind + 64 * h + 64] for c in range(i + 1)],
                         "out": y[rows, 6 * kind + h // 2, i * P:(i + 1) * P]}
                    if kind == 0:
                        one = K.c("ident", slice(0, 4), first=h, n=1)
                        u["bias"] = [(fc[:, i * P:(i + 1) * P], one.to_broadcast([4, n])),
                                     (one.to_broadcast([4, P]), fneg[:, 0:n])]
                    units.append(u)
        att = Attention(K, ctx, "mix_at", units, (0, 1, 2, 3, 4, 5), T)
        with nc.Block(no_gpsimd_drain=True) as block:
            @block.tensor
            def _(pe):
                for i in range(4):
                    pe.wait_ge(squared, i + 1)
                    pe.matmul(K.bank[i][:, :], K.c("headsum"), sq[:, 2 * i:2 * i + 2, :].rearrange("p a t -> p (a t)"),
                              start=True, stop=True).then_inc(summed, 1)
                for i in range(2):
                    pe.wait_ge(normed, 8)
                    pe.matmul(K.bank[6 + i][:, :], K.c("rot"),
                              qk[:, 4 + 2 * i:6 + 2 * i, :].rearrange("p a t -> p (a t)"), start=True, stop=True)\
                        .then_inc(rotated, 1)
                pe.wait_ge(fsum_ready, 1)
                pe.wait_ge(roped, 2)
                att.pe(pe)

            @block.scalar
            def _(act):
                for i in range(4):
                    act.activation(sq[:, 2 * i:2 * i + 2, :], qk[:, 2 * i:2 * i + 2, :], ACT.Square).then_inc(squared, 1)
                act.wait_ge(fabs_ready, 1)
                act.activation(fe[:, :], fe[:, :], ACT.Exp).then_inc(fexp_ready, 1)
                for i in range(4):
                    act.wait_ge(summed, i + 1)
                    last = act.activation(sq[:, 2 * i:2 * i + 2, :], K.bank[i][:, :].rearrange("p (a t) -> p a t", a=2),
                                          ACT.Ln, bias=K.c("eps"), scale=1.0 / 64)
                K.act_own.after(act, last)
                act.activation(sq[:, :, :], sq[:, :, :], ACT.Exp, scale=-0.5).then_inc(rstd_ready, 1)
                att.act(act)

            @block.vector
            def _(dve):
                own = K.dve_own
                dve.tensor_scalar(gains[:, 0:1], K.col("fox_q"), 0.125, None, ALU.mult)
                own.after(dve, dve.tensor_scalar(gains[:, 1:2], K.col("moba_q"), 0.125, None, ALU.mult))
                own.after(dve, dve.tensor_scalar(fx[:, :], f[:, :], K.col("f_bias")[0:4, :], None, ALU.add))
                dve.scalar_tensor_tensor(fe[:, :], fx[:, :], -1.0, fx[:, :], ALU.mult, ALU.min).then_inc(fabs_ready, 1)
                dve.wait_ge(fexp_ready, 1)
                own.after(dve, softplus_small(dve, own, fe[:, :], fs[:, :], fs2[:, :], fq[:, :], fs[:, :]))
                own.after(dve, dve.scalar_tensor_tensor(fx[:, :], fx[:, :], 0.0, fs[:, :], ALU.min, ALU.subtract))
                own.after(dve, dve.tensor_tensor_scan(fc[:, :], fx[:, :], K.c("nomask")[0:4, 0:T], 0.0, ALU.add, ALU.add))
                dve.tensor_scalar(fneg[:, :], fc[:, :], -1.0, None, ALU.mult).then_inc(fsum_ready, 1)
                dve.wait_ge(rstd_ready, 1)
                for t in range(8):
                    gain = (gains[:, 0:1], K.col("fox_k"), gains[:, 1:2], K.col("moba_k"))[t // 2]
                    dve.scalar_tensor_tensor(qk[:, t, :], qk[:, t, :], gain, sq[:, t, :], ALU.mult, ALU.mult)\
                        .then_inc(normed, 1)
                cos = K.cos[:, :].unsqueeze(1).to_broadcast([P, 2, T])
                sin = K.sin[:, :].unsqueeze(1).to_broadcast([P, 2, T])
                for i in range(2):
                    t = slice(4 + 2 * i, 6 + 2 * i)
                    dve.wait_ge(rotated, i + 1)
                    if i:
                        dve.wait_ge(roped, i)
                    own.after(dve, dve.tensor_tensor(rot[:, :, :], K.bank[6 + i][:, :].rearrange("p (a t) -> p a t", a=2),
                                                     sin, ALU.mult))
                    own.after(dve, dve.tensor_tensor(qk[:, t, :], qk[:, t, :], cos, ALU.mult))
                    dve.tensor_tensor(qk[:, t, :], qk[:, t, :], rot[:, :, :], ALU.add).then_inc(roped, 1)
                att.dve(dve)


def mix_out_stage(K):
    nc, y = K.nc, K.mx["y"]
    n0 = K.eaten
    x_updated = K.sem("mix_x_updated")
    with ExitStack() as ctx:
        parts = Parts(K, ctx, "mix_y", KD)
        split = Split(K, ctx, "mix", n0, 4)
        with nc.Block(no_gpsimd_drain=True) as block:
            @block.sync
            def _(sync):
                K.load_slabs(sync, n0 + 4 + RING)

            @block.gpsimd
            def _(pool):
                split.pool(pool)

            @block.scalar
            def _(act):
                split.act(act, 1)
                for i in range(4):
                    parts.act(act, pair_of(i), y[:, pair_of(i), :])
                split.act(act, 4)

            @block.tensor
            def _(pe):
                for i in range(4):
                    w = split.next_view(pe)
                    K.slab_done(feature_major3(pe, K.bank[i], w, (parts.hi, parts.lo), KD, HALF,
                                               first=(lambda k: pe.wait_ge(parts.lo_ready, k // 2 + 1)) if i == 0 else None))

            @block.vector
            def _(dve):
                for i in range(4):
                    parts.dve(dve, pair_of(i), y[:, pair_of(i), :])
                for i in range(4):
                    K.wait_slabs(dve, n0 + i + 1)
                    dve.tensor_tensor(K.x[:, 2 * i:2 * i + 2, :], K.bank[i][:, :].rearrange("p (a t) -> p a t", a=2),
                                      K.x[:, 2 * i:2 * i + 2, :], ALU.add).then_inc(x_updated, 1)


def xattn_slabs(K, l):
    w = lambda n: K.a[n][bass.ds(l, 1), :, :]
    slabs = [whole(w("xattn_w_kv"), i * HALF) for i in range(4)]
    slabs += [whole(w("xattn_w_q"), i * HALF) for i in range(2)]
    slabs += [[(groups_of(w("xattn_w_out"), 0, 4, i * 512, 512), P, 0, 4, 512)] for i in range(2)]
    return slabs


def xattn_stage(K, l):
    nc = K.nc
    n0 = K.eaten
    with ExitStack() as ctx:
        hm = K.sb("hm", [P, KD, T], ctx=ctx)
        qk = K.sb("xqk", [P, 8, T], ctx=ctx)
        v = K.sb("xv", [P, TT, 512], ctx=ctx)
        o = K.sb("xo", [P, 4, T], ctx=ctx)
        sq = K.sb("xsq", [P, 8, T], ctx=ctx)
        gain = K.sb("xgain", [P, 1], ctx=ctx)
        norm = Norm(K, ctx, "xat", K.x, K.h, K.col("xattn_norm", KD), K.bank[6],
                    parts=Parts(K, ctx, "xh", KD))
        m_parts, o_parts = Parts(K, ctx, "xm", KD), Parts(K, ctx, "xo", 4)
        split = Split(K, ctx, "xat", n0, 8)
        mem_ready, z_ready, squared = K.sem("mem_ready"), K.sem("xz_ready"), K.sem("xqk_squared")
        summed, rstd_ready, normed = K.sem("xqk_summed"), K.sem("xqk_rstd"), K.sem("xqk_normed")
        x_updated = K.sem("xat_x_updated")
        units = []
        for h in range(4):
            for i in range(TT):
                units.append({"keys": T, "rows": slice(0, P), "q": qk[:, 4 + h, i * P:(i + 1) * P],
                              "k": [(qk[:, h, :], slice(0, T))], "mask": K.c("nomask")[:, 0:T],
                              "v": [v[:, c, h * P:(h + 1) * P] for c in range(TT)],
                              "out": o[:, h, i * P:(i + 1) * P]})
        att = Attention(K, ctx, "xat", units, (0, 1, 2, 3, 4, 5), T)
        with nc.Block(no_gpsimd_drain=True) as block:
            @block.sync
            def _(sync):
                K.load_slabs(sync, n0 + 8 + RING)

            @block.gpsimd
            def _(pool):
                split.pool(pool)

            @block.tensor
            def _(pe):
                norm.pe(pe)
                m, h = ((p.hi, p.lo) for p in (m_parts, norm.parts))
                for n in range(6):
                    w = split.next_view(pe)
                    if n == 4:
                        pe.wait_ge(norm.parts.lo_ready, 4)
                    if n >= 4:
                        pe.wait_ge(z_ready, n - 3)
                    if n in (2, 3):
                        last = token_major3(pe, K.bank[n % 4], w, m, KD, HALF)
                    else:
                        last = feature_major3(pe, K.bank[n % 4], w, m if n < 4 else h, KD, HALF,
                                              first=(lambda k: pe.wait_ge(m_parts.lo_ready, k // 2 + 1)) if n == 0 else None)
                    K.slab_done(last)
                for i in range(4):
                    pe.wait_ge(squared, i + 1)
                    if i == 2:
                        pe.wait_ge(z_ready, 6)
                    bank = K.bank[(4, 5, 2, 3)[i]]
                    pe.matmul(bank[:, :], K.c("ones"), sq[:, 2 * i:2 * i + 2, :].rearrange("p a t -> p (a t)"),
                              start=True, stop=True).then_inc(summed, 1)
                pe.wait_ge(normed, 8)
                att.pe(pe)
                pe.wait_ge(att.out_copied, 8)
                pe.wait_ge(o_parts.lo_ready, 4)
                for i in range(2):
                    w = split.next_view(pe, groups=4, cols=512)
                    for j in range(4):
                        bank = K.bank[2 * i + j // 2]
                        for k in range(4):
                            last = product3(pe, bank[:, (j % 2) * T:(j % 2 + 1) * T], [p[:, k, j * P:(j + 1) * P] for p in w],
                                            (o_parts.hi[:, k, :], o_parts.lo[:, k, :]), k == 0, k == 3)
                    K.slab_done(last)

            @block.scalar
            def _(act):
                for i in range(4):
                    act.wait_ge(mem_ready, 2 * i + 2)
                    m_parts.act(act, pair_of(i), hm[:, pair_of(i), :])
                norm.act(act, between=lambda: split.act(act, 3))
                for n in range(6):
                    split.act(act, n + 3)
                    K.wait_slabs(act, n0 + n + 1)
                    bank = K.bank[n % 4][:, :].rearrange("p (a t) -> p a t", a=2)
                    if n in (2, 3):
                        act.copy(v[:, :, (n - 2) * HALF:(n - 1) * HALF], bank).then_inc(z_ready, 1)
                    else:
                        t = 2 * n if n < 2 else 4 + 2 * (n - 4)
                        act.copy(qk[:, t:t + 2, :], bank).then_inc(z_ready, 1)
                        act.wait_ge(z_ready, n + 1)
                        act.activation(sq[:, t:t + 2, :], qk[:, t:t + 2, :], ACT.Square).then_inc(squared, 1)
                for i in range(4):
                    act.wait_ge(summed, i + 1)
                    last = act.activation(sq[:, 2 * i:2 * i + 2, :],
                                          K.bank[(4, 5, 2, 3)[i]][:, :].rearrange("p (a t) -> p a t", a=2),
                                          ACT.Ln, bias=K.c("eps"), scale=1.0 / P)
                K.act_own.after(act, last)
                act.activation(sq[:, :, :], sq[:, :, :], ACT.Exp, scale=-0.5).then_inc(rstd_ready, 1)
                att.act(act)
                for h in range(4):
                    act.wait_ge(att.out_copied, 2 * h + 2)
                    o_parts.act(act, slice(h, h + 1), o[:, h:h + 1, :])

            @block.vector
            def _(dve):
                own = K.dve_own
                for k in range(KD):
                    dve.tensor_scalar(hm[:, k, :], K.mem[:, k, :], K.col("xattn_mem_norm", KD)[:, k:k + 1], None, ALU.mult)\
                        .then_inc(mem_ready, 1)
                for i in range(4):
                    m_parts.dve(dve, pair_of(i), hm[:, pair_of(i), :])
                norm.dve(dve)
                own.after(dve, dve.tensor_scalar(gain[:, :], K.col("xq"), float(P) ** -0.5, None, ALU.mult))
                dve.wait_ge(rstd_ready, 1)
                for t in range(8):
                    g = K.col("xk") if t < 4 else gain[:, :]
                    dve.scalar_tensor_tensor(qk[:, t, :], qk[:, t, :], g, sq[:, t, :], ALU.mult, ALU.mult)\
                        .then_inc(normed, 1)
                att.dve(dve)
                for h in range(4):
                    dve.wait_ge(att.out_copied, 2 * h + 2)
                    o_parts.dve(dve, slice(h, h + 1), o[:, h:h + 1, :])
                for i in range(4):
                    if i % 2 == 0:
                        K.wait_slabs(dve, n0 + 7 + i // 2)
                    dve.tensor_tensor(K.x[:, 2 * i:2 * i + 2, :], K.bank[i][:, :].rearrange("p (a t) -> p a t", a=2),
                                      K.x[:, 2 * i:2 * i + 2, :], ALU.add).then_inc(x_updated, 1)



ROWS2 = {}


def _rows2():
    at = 0
    for name, n in (("c", 8), ("c_ctx", 8), ("b_mod", 48), ("q_norm", 1), ("k_norm", 1), ("gdn_norm", 1),
                    ("final", 8), ("a_log", 1), ("dt_bias", 1), ("conv", 72), ("ffn_b", 44), ("ffn_conv", 132)):
        ROWS2[name] = at
        at += n
    return at


N_ROWS2 = _rows2()
TILES2 = -(-N_ROWS2 // P)


def second_slabs(K):
    a = K.a
    w_in = a["w_in_2"]
    slabs = [whole(a["w_mod_2"], i * HALF) for i in range(24)]
    slabs += [whole(w_in, 0), whole(w_in, 256)] + [whole(w_in, CTX_COLS + i * HALF) for i in range(4)]
    slabs += [whole(w_in, 3584, 32)]
    slabs += [whole(w_in, 512 + 1024 + i * HALF) for i in range(8)]
    slabs += [whole(w_in, 512 + i * HALF) for i in range(4)]
    slabs += [whole(w_in, CTX_COLS + 1024 + i * HALF) for i in range(12)]
    for name in ("w_pa_2", "w_pd_2", "w_out_2"):
        slabs += [whole(a[name], i * HALF) for i in range(4)]
    slabs += ffn_slabs(a["w_up_2"], a["w_down_2"])
    return slabs


def modulation_stage(K):
    nc, a = K.nc, K.a
    n0 = K.eaten
    with ExitStack() as ctx:
        rows = K.sb("rows2", [P, TILES2, P], ctx=ctx)
        cs = K.sb("cs", [P, KD, 2], ctx=ctx)
        ctx_in = K.sb("ctx_in", [P, KD, T], ctx=ctx)
        gains = K.sb("gains2", [P, 2, KD], ctx=ctx)
        start, ctx_pe, ctx_act, ctx_copied = load_feature_major(K, ctx, "ctx", a["ctx_2"][0], ctx_in, (2, 3))
        mod = K.mod
        norm_x = Norm(K, ctx, "hx", K.x, K.h, gains[:, 0, :], K.bank[4], shift=mod[:, 0:KD, 0])
        norm_c = Norm(K, ctx, "hc", ctx_in, K.hc, gains[:, 1, :], K.bank[5], shift=mod[:, 0:KD, 1])
        cleared, arrived, turned = K.sem("rows2_cleared"), K.sem("rows2_arrived"), K.sem("rows2_turned")
        prm_ready, c_ready, consts_in = K.sem("prm2_ready"), K.sem("c_ready"), K.sem("consts2_in")
        pieces = []

        def put(name, src, width=P):
            r, at, n = ROWS2[name], 0, src.shape[0]
            while at < n:
                tile, row = divmod(r + at, P)
                m = min(n - at, P - row)
                pieces.append((rows[row:row + m, tile, 0:width], src[at:at + m, :]))
                at += m
        by_rows = lambda ap: ap.rearrange("a (r c) -> (a r) c", c=P)
        for name, key in (("c", "c_2"), ("c_ctx", "c_ctx_2"), ("b_mod", "b_mod_2"), ("q_norm", "q_norm_w_2"),
                          ("k_norm", "k_norm_w_2"), ("gdn_norm", "gdn_norm_w_2"), ("final", "final_norm_w_2"),
                          ("ffn_b", "ffn_conv_b_2")):
            put(name, by_rows(a[key]))
        put("a_log", a["a_log_2"].rearrange("a d h -> a (d h)"), 16)
        put("dt_bias", a["dt_bias_2"].rearrange("a d h -> a (d h)"), 16)
        put("conv", a["conv_qkv_w_2"].rearrange("a j (r c) -> (a j r) c", c=P))
        put("ffn_conv", a["ffn_conv_w_2"].rearrange("a j (r c) -> (a j r) c", c=P))
        with nc.Block(no_gpsimd_drain=True) as block:
            @block.sync
            def _(sync):
                sync.dma_start(K.consts[2][:, :], a["consts2"]).then_inc(consts_in, 16)
                start(sync)
                K.load_slabs(sync, n0 + RING)
                sync.wait_ge(cleared, 1)
                for dst, src in pieces:
                    sync.dma_start(dst, src).then_inc(arrived, 16)
                K.load_slabs(sync, n0 + 24 + RING)
                sync.wait_ge(consts_in, 16)

            @block.tensor
            def _(pe):
                pe.wait_ge(arrived, 16 * len(pieces))
                for i in range(TILES2):
                    last = pe.transpose(K.bank[7][:, i * P:(i + 1) * P], rows[:, i, :], K.c("ident"))
                last.then_inc(turned, 1)
                ctx_pe(pe)
                norm_x.pe(pe)
                norm_c.pe(pe)
                pe.wait_ge(c_ready, 1)
                for n in range(24):
                    w = view(K.next_slab(pe))
                    for j in range(2):
                        t = 2 * n + j
                        for k in range(KD):
                            last = pe.matmul(K.bank[0][:, 2 * t:2 * t + 2], w[:, k, j * P:(j + 1) * P], cs[:, k, :],
                                             start=(k == 0), stop=(k == KD - 1))
                    K.slab_done(last)

            @block.scalar
            def _(act):
                act.wait_ge(prm_ready, 1)
                for i, name in enumerate(("c", "c_ctx")):
                    last = act.activation(cs[:, :, i], K.col2(name, KD), ACT.Silu)
                last.then_inc(c_ready, 1)
                ctx_act(act)
                act.wait_ge(ctx_copied, 4)
                norm_x.act(act)
                norm_c.act(act)

            @block.vector
            def _(dve):
                own = K.dve_own
                dve.memset(rows[:, :, :], 0.0).then_inc(cleared, 1)
                dve.wait_ge(turned, 1)
                dve.tensor_copy(K.prm2[:, :], K.bank[7][:, 0:TILES2 * P]).then_inc(prm_ready, 1)
                dve.wait_ge(prm_ready, 1)
                K.wait_slabs(dve, n0 + 24)
                own.after(dve, dve.tensor_tensor(mod[:, :, :], K.bank[0][:, 0:96].rearrange("p (t c) -> p t c", c=2),
                                                 K.col2("b_mod", 48).unsqueeze(2).to_broadcast([P, 48, 2]), ALU.add))
                for i in range(2):
                    last = dve.tensor_scalar(gains[:, i, :], mod[:, KD:2 * KD, i], 1.0, None, ALU.add)
                own.after(dve, last)
                norm_x.dve(dve)
                norm_c.dve(dve)


def latent_attention_stage(K):
    nc = K.nc
    n0 = K.eaten
    with ExitStack() as ctx:
        a = K.sb("a2", [P, 12, T], ctx=ctx)
        sq = K.sb("a2sq", [P, 12, T], ctx=ctx)
        v = K.sb("v2", [P, 4, HALF], ctx=ctx)
        rot = K.sb("rot2", [P, 2, T], ctx=ctx)
        gain = K.sb("gain2", [P, 1], ctx=ctx)
        z_ready, squared, summed = K.sem("a2_z_ready"), K.sem("a2_squared"), K.sem("a2_summed")
        rstd_ready, normed = K.sem("a2_rstd"), K.sem("a2_normed")
        rotated, roped = K.sem("a2_rotated"), K.sem("a2_roped")
        units = []
        for h in range(8):
            g = h // 4
            for i in range(TT):
                units.append({"keys": 512, "rows": slice(0, P), "q": a[:, h, i * P:(i + 1) * P],
                              "k": [(a[:, 8 + 2 * g:10 + 2 * g, :].rearrange("p a t -> p (a t)"), slice(0, 512))],
                              "mask": K.c("nomask"), "v": [v[:, c, g * P:(g + 1) * P] for c in range(4)],
                              "out": K.attn[:, h, i * P:(i + 1) * P]})
        att = Attention(K, ctx, "a2", units, (0, 1, 2, 3, 4, 5), 512)
        pairs = [slice(2 * i, 2 * i + 2) for i in range(6)]
        roped_tiles = [slice(2 * i, 2 * i + 2) for i in range(4)] + [slice(8, 9), slice(10, 11)]
        with nc.Block(no_gpsimd_drain=True) as block:
            @block.sync
            def _(sync):
                K.load_slabs(sync, n0 + 6 + RING)

            @block.tensor
            def _(pe):
                w = view(K.next_slab(pe))
                for g in range(2):
                    for i, act in enumerate((K.h, K.hc)):
                        last = feature_major(K, pe, K.bank[g], w[:, :, g * P:(g + 1) * P], act, KD, P, at=i * T)
                K.slab_done(last)
                w = view(K.next_slab(pe))
                for i, act in enumerate((K.h, K.hc)):
                    last = token_major(K, pe, K.bank[2 + i], w, act, KD, HALF)
                K.slab_done(last)
                for n in range(4):
                    w = view(K.next_slab(pe))
                    pe.wait_ge(z_ready, (2, 2, 4, 4)[n])
                    K.slab_done(feature_major(K, pe, K.bank[n], w, K.h, KD, HALF))
                for i in range(6):
                    pe.wait_ge(squared, i + 1)
                    if i >= 2:
                        pe.wait_ge(rstd_ready, i - 1)
                    pe.matmul(K.bank[4 + i % 2][:, :], K.c("ones"), sq[:, pairs[i], :].rearrange("p a t -> p (a t)"),
                              start=True, stop=True).then_inc(summed, 1)
                pe.wait_ge(normed, 12)
                for i, t in enumerate(roped_tiles):
                    if i >= 2:
                        pe.wait_ge(roped, i - 1)
                    n = (t.stop - t.start) * T
                    pe.matmul(K.bank[6 + i % 2][:, 0:n], K.c("axial"), a[:, t, :].rearrange("p a t -> p (a t)"),
                              start=True, stop=True).then_inc(rotated, 1)
                pe.wait_ge(roped, 6)
                pe.wait_ge(z_ready, 8)
                att.pe(pe)

            @block.scalar
            def _(act):
                bank = lambda b: K.bank[b][:, :].rearrange("p (a t) -> p a t", a=2)
                K.wait_slabs(act, n0 + 1)
                for g in range(2):
                    act.copy(a[:, 8 + 2 * g:10 + 2 * g, :], bank(g)).then_inc(z_ready, 1)
                K.wait_slabs(act, n0 + 2)
                for i in range(2):
                    act.copy(v[:, 2 * i:2 * i + 2, :], bank(2 + i)).then_inc(z_ready, 1)
                for n in range(4):
                    K.wait_slabs(act, n0 + 3 + n)
                    act.copy(a[:, 2 * n:2 * n + 2, :], bank(n)).then_inc(z_ready, 1)
                act.wait_ge(z_ready, 8)
                for t in pairs:
                    act.activation(sq[:, t, :], a[:, t, :], ACT.Square).then_inc(squared, 1)
                for i, t in enumerate(pairs):
                    act.wait_ge(summed, i + 1)
                    act.activation(sq[:, t, :], bank(4 + i % 2), ACT.Ln, bias=K.c("eps"), scale=1.0 / P)\
                        .then_inc(rstd_ready, 1)
                act.wait_ge(rstd_ready, 6)
                act.activation(sq[:, :, :], sq[:, :, :], ACT.Exp, scale=-0.5).then_inc(rstd_ready, 1)
                att.act(act)

            @block.vector
            def _(dve):
                own = K.dve_own
                own.after(dve, dve.tensor_scalar(gain[:, :], K.col2("q_norm"), float(P) ** -0.5, None, ALU.mult))
                dve.wait_ge(rstd_ready, 7)
                for t in range(12):
                    g = gain[:, :] if t < 8 else K.col2("k_norm")
                    dve.scalar_tensor_tensor(a[:, t, :], a[:, t, :], g, sq[:, t, :], ALU.mult, ALU.mult)\
                        .then_inc(normed, 1)
                for i, t in enumerate(roped_tiles):
                    m = t.stop - t.start
                    cos = K.c("axcos").unsqueeze(1).to_broadcast([P, m, T])
                    sin = K.c("axsin").unsqueeze(1).to_broadcast([P, m, T])
                    dve.wait_ge(rotated, i + 1)
                    if i:
                        dve.wait_ge(roped, i)
                    own.after(dve, dve.tensor_tensor(rot[:, 0:m, :],
                                                     K.bank[6 + i % 2][:, 0:m * T].rearrange("p (a t) -> p a t", a=m),
                                                     sin, ALU.mult))
                    own.after(dve, dve.tensor_tensor(a[:, t, :], a[:, t, :], cos, ALU.mult))
                    dve.tensor_tensor(a[:, t, :], a[:, t, :], rot[:, 0:m, :], ALU.add).then_inc(roped, 1)
                att.dve(dve)


def gdn_prepare_stage(K):
    nc = K.nc
    n0 = K.eaten
    g = K.gdn
    with ExitStack() as ctx:
        raw = [K.sb(f"raw{i}", [P, 2, T + 2], ctx=ctx) for i in range(2)]
        con = [K.sb(f"conv{i}", [P, 2, T], ctx=ctx) for i in range(2)]
        gv = K.sb("gv", [P, 8, 2 * T], ctx=ctx)
        rstd = K.sb("gr", [P, 2, 2 * T], ctx=ctx)
        small = lambda n, w=512: K.sb(n, [16, w], ctx=ctx)
        beta, la, t1, t2, t3, gf, gb = (small(n) for n in ("beta", "la", "gt1", "gt2", "gt3", "gf", "gb"))
        e16, last16, lastd = small("ea", 1), small("glast", 4), small("glastd", 64)
        z_ready, conv_ready, silu_ready = K.sem("g_z_ready"), K.sem("g_conv_ready"), K.sem("g_silu_ready")
        squared, summed, rstd_ready, normed = K.sem("g_squared"), K.sem("g_summed"), K.sem("g_rstd"), K.sem("g_normed")
        turned, turn_copied = K.sem("g_turned"), K.sem("g_turn_copied")
        da_ready, exp_ready, gam_ready = K.sem("g_da"), K.sem("g_exp"), K.sem("g_gam")
        gamt_ready, gamt_read, scal_in, scal_ready = K.sem("g_gamt"), K.sem("g_gamt_read"), K.sem("g_scal_in"), K.sem("g_scal")
        flat = lambda x: x.rearrange("p a t -> p (a t)")
        tiles = [("k", h) for h in range(8)] + [("v", h) for h in range(8)] + [("q", h) for h in range(8)]
        dests = {"k": g["k"], "v": gv, "q": g["q"]}
        offset = {"q": 0, "k": 8, "v": 16}
        seg = lambda kind: 1 if kind == "q" else 2
        norms = [("k", h) for h in range(8)] + [("q", h) for h in range(0, 8, 2)]
        with nc.Block(no_gpsimd_drain=True) as block:
            @block.sync
            def _(sync):
                K.load_slabs(sync, n0 + 13 + RING)

            @block.tensor
            def _(pe):
                w = view(K.next_slab(pe), cols=32)
                for j in range(2):
                    for i, act in enumerate((K.h, K.hc)):
                        for k in range(KD):
                            last = pe.matmul(K.bank[4 + j][0:16, i * T:(i + 1) * T], w[:, k, 16 * j:16 * j + 16],
                                             act[:, k, :], start=(k == 0), stop=(k == KD - 1))
                K.slab_done(last)
                for n in range(12):
                    w = view(K.next_slab(pe))
                    for j in range(2):
                        i = 2 * n + j
                        if i >= 4:
                            pe.wait_ge(z_ready, i - 3)
                        for m, act in enumerate((K.h, K.hc)[0:seg(tiles[i][0])]):
                            last = feature_major(K, pe, K.bank[i % 4], w[:, :, j * P:(j + 1) * P], act, KD, P, at=m * T)
                    K.slab_done(last)
                pe.wait_ge(gam_ready, 1)
                for j in range(4):
                    pe.transpose(K.bank[4][:, j * 16:(j + 1) * 16], g["gam"][:, j * P:(j + 1) * P], K.c("ident", slice(0, 16), n=16))
                    last = pe.transpose(K.bank[4][:, 64 + j * 16:64 + (j + 1) * 16], g["beta"][:, j * P:(j + 1) * P],
                                        K.c("ident", slice(0, 16), n=16))
                last.then_inc(gamt_ready, 1)
                pe.matmul(K.bank[5][:, 0:64], K.c("ones", slice(0, 16)), lastd[:, :], start=True, stop=True)\
                    .then_inc(gamt_ready, 1)
                for i, (kind, h) in enumerate(norms):
                    pe.wait_ge(squared, i + 1)
                    if i >= 2:
                        pe.wait_ge(rstd_ready, i - 1)
                    pe.matmul(K.bank[6 + i % 2][:, :], K.c("ones"), con[i % 2][:, :, :].rearrange("p a t -> p (a t)"),
                              start=True, stop=True).then_inc(summed, 1)
                pe.wait_ge(z_ready, 24)
                pe.wait_ge(normed, 8)
                i = 0
                for src in (gv, g["k"]):
                    for j in range(4):
                        for hh in range(2):
                            if i >= 4:
                                pe.wait_ge(turn_copied, i - 3)
                            for q in range(4):
                                last = pe.transpose(K.bank[i % 4][:, q * P:(q + 1) * P],
                                                    src[:, 4 * hh + q, j * P:(j + 1) * P], K.c("ident"))
                            last.then_inc(turned, 1)
                            i += 1

            def rstd_of(act, i):
                act.wait_ge(summed, i + 1)
                if i >= 2:
                    act.wait_ge(normed, i - 1)
                K.act_own.after(act, act.activation(rstd[:, i % 2, :], K.bank[6 + i % 2][:, :], ACT.Ln, bias=K.c("eps")))
                act.activation(rstd[:, i % 2, :], rstd[:, i % 2, :], ACT.Exp, scale=-0.5).then_inc(rstd_ready, 1)

            @block.scalar
            def _(act):
                K.wait_slabs(act, n0 + 1)
                act.copy(t1[:, :], K.bank[4][0:16, :])
                act.copy(la[:, :], K.bank[5][0:16, :]).then_inc(da_ready, 1)
                for i in range(26):
                    if i < 24:
                        kind, h = tiles[i]
                        m = seg(kind)
                        K.wait_slabs(act, n0 + 2 + i // 2)
                        if i >= 2:
                            act.wait_ge(conv_ready, i - 1)
                        act.copy(raw[i % 2][:, 0:m, 1:T + 1], K.bank[i % 4][:, 0:m * T].rearrange("p (a t) -> p a t", a=m))\
                            .then_inc(z_ready, 1)
                    if i >= 1 and i - 1 < 24:
                        kind, h = tiles[i - 1]
                        m = seg(kind)
                        act.wait_ge(conv_ready, i)
                        act.activation(dests[kind][:, h, 0:m * T], flat(con[(i - 1) % 2][:, 0:m, :]), ACT.Silu)\
                            .then_inc(silu_ready, 1)
                act.wait_ge(da_ready, 1)
                act.activation(g["beta"][:, :], t1[:, :], ACT.Sigmoid).then_inc(exp_ready, 1)
                act.wait_ge(da_ready, 2)
                act.activation(e16[:, :], K.col2("a_log")[0:16, :], ACT.Exp)
                act.activation(t2[:, :], t2[:, :], ACT.Exp).then_inc(exp_ready, 1)
                act.wait_ge(silu_ready, 24)
                for i, (kind, h) in enumerate(norms):
                    src = g["k"][:, h, :] if kind == "k" else flat(g["q"][:, h:h + 2, :])
                    if i >= 2:
                        act.wait_ge(summed, i - 1)
                    act.activation(flat(con[i % 2][:, :, :]), src, ACT.Square).then_inc(squared, 1)
                    if i >= 1:
                        rstd_of(act, i - 1)
                rstd_of(act, len(norms) - 1)
                act.wait_ge(scal_in, 1)
                act.activation(g["glast"][:, :], K.bank[5][:, 0:64], ACT.Exp)
                act.activation(g["kdec"][:, :], g["kdec"][:, :], ACT.Exp)
                act.activation(g["bexp"][:, :], g["gamt"][:, :], ACT.Exp).then_inc(scal_ready, 1)
                for i in range(16):
                    act.wait_ge(turned, i + 1)
                    dst = g["vtok"] if i < 8 else g["ktok"]
                    j, hh = (i % 8) // 2, i % 2
                    act.copy(dst[:, j, hh * 512:(hh + 1) * 512], K.bank[i % 4][:, :]).then_inc(turn_copied, 1)

            @block.vector
            def _(dve):
                own = K.dve_own
                for i in range(2):
                    dve.memset(raw[i][:, :, 0:1], 0.0)
                    last = dve.memset(raw[i][:, :, T + 1:T + 2], 0.0)
                own.after(dve, last)
                for i, (kind, h) in enumerate(tiles):
                    m = seg(kind)
                    r, o = raw[i % 2], con[i % 2][:, 0:m, :]
                    tap = lambda j: K.col2("conv", 72)[:, j * 24 + offset[kind] + h:j * 24 + offset[kind] + h + 1]
                    dve.wait_ge(z_ready, i + 1)
                    if i >= 2:
                        dve.wait_ge(silu_ready, i - 1)
                    own.after(dve, dve.tensor_scalar(o, r[:, 0:m, 0:T], tap(0), None, ALU.mult))
                    own.after(dve, dve.scalar_tensor_tensor(o, r[:, 0:m, 1:T + 1], tap(1), o, ALU.mult, ALU.add))
                    dve.scalar_tensor_tensor(o, r[:, 0:m, 2:T + 2], tap(2), o, ALU.mult, ALU.add).then_inc(conv_ready, 1)
                dve.wait_ge(da_ready, 1)
                own.after(dve, dve.tensor_scalar(la[:, :], la[:, :], K.col2("dt_bias")[0:16, :], None, ALU.add))
                dve.scalar_tensor_tensor(t2[:, :], la[:, :], -1.0, la[:, :], ALU.mult, ALU.min).then_inc(da_ready, 1)
                dve.wait_ge(exp_ready, 2)
                own.after(dve, softplus_small(dve, own, t2[:, :], t3[:, :], gf[:, :], gb[:, :], t3[:, :]))
                own.after(dve, dve.scalar_tensor_tensor(la[:, :], la[:, :], 0.0, t3[:, :], ALU.max, ALU.add))
                own.after(dve, dve.tensor_scalar(la[:, :], la[:, :], e16[:, :], -1.0, ALU.mult, ALU.mult))
                zeros = K.c("nomask", slice(0, 16), n=P)
                for j in range(4):
                    c = slice(j * P, (j + 1) * P)
                    dve.tensor_tensor_scan(gf[:, c], la[:, c], zeros, 0.0, ALU.add, ALU.add)
                    last = dve.tensor_tensor_scan(gb[:, c][:, ::-1], la[:, c][:, ::-1], zeros, 0.0, ALU.add, ALU.add)
                own.after(dve, last)
                fwd, bwd = K.c("fwd", slice(0, 16)), K.c("bwd", slice(0, 16))
                own.after(dve, dve.tensor_scalar(t3[:, :], gb[:, :], bwd, None, ALU.mult))
                own.after(dve, dve.scalar_tensor_tensor(g["gam"][:, :], gf[:, :], fwd, t3[:, :], ALU.mult, ALU.add))
                tile4 = lambda x: x[:, :].rearrange("p (j t) -> p j t", j=4)
                own.after(dve, dve.tensor_scalar(last16[:, :], tile4(gb)[:, :, 0], bwd, None, ALU.mult))
                own.after(dve, dve.scalar_tensor_tensor(last16[:, :], tile4(gf)[:, :, P - 1], fwd, last16[:, :],
                                                        ALU.mult, ALU.add))
                dve.tensor_tensor(lastd[:, :].rearrange("p (j r) -> p j r", j=4),
                                  K.c("ident", slice(0, 16), n=16).unsqueeze(1).to_broadcast([16, 4, 16]),
                                  last16[:, :].unsqueeze(2).to_broadcast([16, 4, 16]), ALU.mult).then_inc(gam_ready, 1)
                dve.wait_ge(gamt_ready, 2)
                dve.tensor_copy(g["gamt"][:, :], K.bank[4][:, 0:64])
                own.after(dve, dve.tensor_copy(g["betat"][:, :], K.bank[4][:, 64:128]))
                dve.tensor_tensor(g["kdec"][:, :], K.bank[5][:, 0:64], g["gamt"][:, :], ALU.subtract).then_inc(scal_in, 1)
                for i, (kind, h) in enumerate(norms):
                    dve.wait_ge(rstd_ready, i + 1)
                    o = g["k"][:, h, :] if kind == "k" else flat(g["q"][:, h:h + 2, :])
                    scale = 1.0 if kind == "k" else float(P) ** -0.5
                    dve.scalar_tensor_tensor(o, o, scale, rstd[:, i % 2, :], ALU.mult, ALU.mult).then_inc(normed, 1)
                dve.wait_ge(scal_ready, 1)
                dve.tensor_tensor(g["bexp"][:, :], g["bexp"][:, :], g["betat"][:, :], ALU.mult)


def gdn_chunk_stage(K, d, half):
    nc, g = K.nc, K.gdn
    tag = f"g{d}{half}"
    heads = [4 * half + i for i in range(4)]
    order = (2, 3, 0, 1) if d == 0 else (3, 2, 1, 0)
    column = lambda j, h: 16 * j + 8 * d + h
    sem = K.sem
    with ExitStack() as ctx:
        four = lambda name: K.sb(name, [P, 4, 4, P], ctx=ctx)
        lt, xt, wt = four("glt"), four("gxt"), four("gwt")
        pt = K.sb("gpt", [P, 4, TT, P], ctx=ctx)
        qdec = K.sb("gqdec", [P, 4, T], ctx=ctx)
        u = lt
        dec_in, dec_ready, spread = sem("g_dec_in"), sem("g_dec_ready"), sem("g_spread")
        kb_ready, mats_ready, mats_read = sem("g_kb_ready"), sem("g_mats_ready"), sem("g_mats_read")
        spread_read = sem("g_spread_read")
        with ExitStack() as ictx:
            dec = [K.sb(f"gdec{i}", [P, 4, P], ctx=ictx) for i in range(2)]
            kb = [K.sb(f"gkb{i}", [P, 2 * T], ctx=ictx) for i in range(2)]
            eb = [K.sb(f"geb{i}", [P, T], ctx=ictx) for i in range(2)]
            inv = Inverse(K, ictx, "ginv", 4, LEVELS, "levels" if d == 0 else "levels_back",
                          lambda i: lt[:, i, :, :], lambda i: xt[:, i, :, :],
                          lambda eng, i: eng.wait_ge(mats_read, i + 1))
            flat = lambda x: x.rearrange("p a t -> p (a t)")
            with nc.Block(no_gpsimd_drain=True) as block:
                @block.tensor
                def _(pe):
                    for i in range(5):
                        if i < 4:
                            if i >= 1:
                                pe.wait_ge(spread_read, 2 * i)
                            row = K.c("ident", slice(0, 16), first=8 * d + heads[i], n=1).to_broadcast([16, P])
                            pe.matmul(K.bank[0][:, :], row, g["gam"][:, :], start=True, stop=True).then_inc(spread, 1)
                            pe.matmul(K.bank[1][:, :], row, g["beta"][:, :], start=True, stop=True).then_inc(spread, 1)
                        if i >= 1:
                            h = heads[i - 1]
                            pe.wait_ge(kb_ready, i)
                            if i >= 2:
                                pe.wait_ge(mats_read, i - 1)
                            for j in range(4):
                                c = slice(j * P, (j + 1) * P)
                                pe.matmul(K.bank[5][:, c], g["k"][:, h, c], kb[(i - 1) % 2][:, c], start=True, stop=True)
                            for j in range(TT):
                                c = slice(j * P, (j + 1) * P)
                                last = pe.matmul(K.bank[6][:, c], g["k"][:, h, c], g["q"][:, h, c], start=True, stop=True)
                            last.then_inc(mats_ready, 1)
                    pe.wait_ge(mats_read, 4)
                    inv.pe(pe)

                @block.vector
                def _(dve):
                    for i in range(5):
                        if i < 4:
                            h = heads[i]
                            dve.wait_ge(spread, 2 * i + 1)
                            if i >= 2:
                                dve.wait_ge(mats_read, i - 1)
                            for j in range(4):
                                last = dve.scalar_tensor_tensor(dec[i % 2][:, j, :], K.bank[0][:, j * P:(j + 1) * P],
                                                                g["gamt"][:, column(j, h):column(j, h) + 1],
                                                                K.c("future" if d == 0 else "past"), ALU.subtract, ALU.add)
                            last.then_inc(dec_in, 1)
                            dve.wait_ge(spread, 2 * i + 2)
                            dve.tensor_tensor(kb[i % 2][:, :], g["k"][:, h, :], K.bank[1][:, :], ALU.mult).then_inc(kb_ready, 1)
                            dve.wait_ge(kb_ready, i + 1)
                            dve.wait_ge(dec_ready, i + 1)
                            dve.tensor_tensor(qdec[:, i, :], g["q"][:, h, :], eb[i % 2][:, :], ALU.mult).then_inc(spread_read, 1)
                        if i >= 1:
                            dve.wait_ge(mats_ready, i)
                            dve.tensor_tensor(pt[:, i - 1, :, :], K.bank[6][:, 0:T].rearrange("p (a t) -> p a t", a=2),
                                              dec[(i - 1) % 2][:, 0:2, :], ALU.mult)
                            dve.tensor_tensor(flat(lt[:, i - 1, :, :]), K.bank[5][:, :], flat(dec[(i - 1) % 2][:, :, :]),
                                              ALU.mult).then_inc(mats_read, 1)
                    inv.dve(dve)

                @block.scalar
                def _(act):
                    for i in range(4):
                        act.wait_ge(dec_in, i + 1)
                        if i >= 2:
                            act.wait_ge(spread_read, 2 * (i - 1))
                        act.activation(eb[i % 2][:, :], K.bank[0][:, 0:T], ACT.Exp).then_inc(spread_read, 1)
                        act.activation(flat(dec[i % 2][:, :, :]), flat(dec[i % 2][:, :, :]), ACT.Exp).then_inc(dec_ready, 1)
                    inv.act(act)

                @block.gpsimd
                def _(pool):
                    inv.pool(pool)
        with ExitStack() as sctx:
            xb = [K.sb(f"gxb{i}", [P, 4, P], ctx=sctx) for i in range(2)]
            xe = [K.sb(f"gxe{i}", [P, 4, P], ctx=sctx) for i in range(2)]
            state = K.sb("gstate", [P, 4, P], ctx=sctx)
            delta = K.sb("gdelta", [P, 4, P], ctx=sctx)
            dk = K.sb("gdk", [P, 4, P], ctx=sctx)
            scaled, uw_ready, uw_copied = sem("g_scaled"), sem("g_uw_ready"), sem("g_uw_copied")
            s_ready, ws_ready, delta_ready = sem("g_s_ready"), sem("g_ws_ready"), sem("g_delta_ready")
            sn_ready, o_ready, o_copied = sem("g_sn_ready"), sem("g_o_ready"), sem("g_o_copied")
            bank4 = lambda b: K.bank[b][:, :].rearrange("p (a t) -> p a t", a=4)
            with nc.Block(no_gpsimd_drain=True) as block:
                @block.tensor
                def _(pe):
                    for i, h in enumerate(heads):
                        pe.wait_ge(scaled, i + 1)
                        if i >= 2:
                            pe.wait_ge(uw_copied, 2 * (i - 1))
                        ub, wb = K.bank[4 + 2 * (i % 2)], K.bank[5 + 2 * (i % 2)]
                        f = slice(h * P, (h + 1) * P)
                        for j in range(4):
                            pe.matmul(ub[:, j * P:(j + 1) * P], xb[i % 2][:, j, :], g["vtok"][:, j, f], start=True, stop=True)
                        for j in range(4):
                            last = pe.matmul(wb[:, j * P:(j + 1) * P], g["ktok"][:, j, f], xe[i % 2][:, j, :],
                                             start=True, stop=True)
                        last.then_inc(uw_ready, 1)
                    pe.wait_ge(uw_copied, 8)
                    for n, j in enumerate(order):
                        pe.wait_ge(s_ready, n + 1)
                        for i, h in enumerate(heads):
                            last = pe.matmul(K.bank[0][:, i * P:(i + 1) * P], wt[:, i, j, :], state[:, i, :],
                                             start=True, stop=True)
                        last.then_inc(ws_ready, 1)
                        pe.wait_ge(delta_ready, 2 * n + 2)
                        if n < 3:
                            for i, h in enumerate(heads):
                                last = pe.matmul(K.bank[1][:, i * P:(i + 1) * P], g["ktok"][:, j, h * P:(h + 1) * P],
                                                 dk[:, i, :], start=True, stop=True)
                            last.then_inc(sn_ready, 1)
                        if j < 2:
                            for i, h in enumerate(heads):
                                o = K.bank[2 + n % 2][:, i * P:(i + 1) * P]
                                pe.matmul(o, state[:, i, :], qdec[:, i, j * P:(j + 1) * P], start=True, stop=False)
                                last = pe.matmul(o, delta[:, i, :], pt[:, i, j, :], start=False, stop=True)
                            last.then_inc(o_ready, 1)

                @block.vector
                def _(dve):
                    own = K.dve_own
                    for i, h in enumerate(heads):
                        if i >= 2:
                            dve.wait_ge(uw_ready, i - 1)
                        for j in range(4):
                            c = slice(column(j, h), column(j, h) + 1)
                            dve.tensor_scalar(xb[i % 2][:, j, :], xt[:, i, j, :], g["betat"][:, c], None, ALU.mult)
                            last = dve.tensor_scalar(xe[i % 2][:, j, :], xt[:, i, j, :], g["bexp"][:, c], None, ALU.mult)
                        last.then_inc(scaled, 1)
                    dve.memset(state[:, :, :], 0.0).then_inc(s_ready, 1)
                    dve.wait_ge(uw_copied, 8)
                    for n, j in enumerate(order):
                        dve.wait_ge(ws_ready, n + 1)
                        if n == 3:
                            dve.wait_ge(o_ready, 1)
                        dve.tensor_tensor(delta[:, :, :], u[:, :, j, :], bank4(0), ALU.subtract).then_inc(delta_ready, 1)
                        dve.wait_ge(delta_ready, 2 * n + 1)
                        for i, h in enumerate(heads):
                            last = dve.tensor_scalar(dk[:, i, :], delta[:, i, :], g["kdec"][:, column(j, h):column(j, h) + 1],
                                                     None, ALU.mult)
                        last.then_inc(delta_ready, 1)
                        if n < 3:
                            dve.wait_ge(sn_ready, n + 1)
                            if j < 2:
                                dve.wait_ge(o_ready, 1)
                            for i, h in enumerate(heads):
                                last = dve.scalar_tensor_tensor(state[:, i, :], state[:, i, :],
                                                                g["glast"][:, column(j, h):column(j, h) + 1],
                                                                K.bank[1][:, i * P:(i + 1) * P], ALU.mult, ALU.add)
                            last.then_inc(s_ready, 1)
                    if d == 1:
                        for n in (2, 3):
                            j = order[n]
                            dve.wait_ge(o_ready, n - 1)
                            o = g["o"][:, 4 * half:4 * half + 4, j * P:(j + 1) * P]
                            dve.tensor_tensor(o, o, bank4(2 + n % 2), ALU.add).then_inc(o_copied, 1)

                @block.scalar
                def _(act):
                    for i in range(4):
                        act.wait_ge(uw_ready, i + 1)
                        act.copy(u[:, i, :, :], bank4(4 + 2 * (i % 2))).then_inc(uw_copied, 1)
                        act.copy(wt[:, i, :, :], bank4(5 + 2 * (i % 2))).then_inc(uw_copied, 1)
                    if d == 0:
                        for n in (2, 3):
                            j = order[n]
                            act.wait_ge(o_ready, n - 1)
                            act.copy(g["o"][:, 4 * half:4 * half + 4, j * P:(j + 1) * P], bank4(2 + n % 2)).then_inc(o_copied, 1)
    K.restart_stages()


def merge_stage(K):
    nc, g = K.nc, K.gdn
    n0 = K.eaten
    with ExitStack() as ctx:
        zs = K.sb("zsilu", [P, 8, T], ctx=ctx)
        gates = K.sb("gates", [P, 16, T], ctx=ctx)
        sq = K.sb("osq", [P, 8, T], ctx=ctx)
        y = K.sb("y2", [P, 8, T], ctx=ctx)
        tmp = K.sb("ytmp", [P, 2, T], ctx=ctx)
        h_parts, x_parts = Parts(K, ctx, "m_h", 8), Parts(K, ctx, "m_x", 8)
        split = Split(K, ctx, "m", n0, 24)
        o = g["o"]
        read, squared, summed, rstd_ready = K.sem("m_read"), K.sem("m_squared"), K.sem("m_summed"), K.sem("m_rstd")
        o_ready, y_ready, x_updated = K.sem("m_o_ready"), K.sem("m_y_ready"), K.sem("m_x_updated")
        pair = lambda b: K.bank[b][:, :].rearrange("p (a t) -> p a t", a=2)
        two = lambda i: slice(2 * i, 2 * i + 2)
        flat = lambda x: x.rearrange("p a t -> p (a t)")
        with nc.Block(no_gpsimd_drain=True) as block:
            @block.sync
            def _(sync):
                K.load_slabs(sync, n0 + 24 + RING)

            @block.gpsimd
            def _(pool):
                split.pool(pool)

            @block.tensor
            def _(pe):
                for i in range(4):
                    pe.wait_ge(squared, i + 1)
                    pe.matmul(K.bank[4 + i][:, :], K.c("ones"), flat(sq[:, two(i), :]), start=True, stop=True)\
                        .then_inc(summed, 1)
                for n in range(24):
                    w = split.next_view(pe)
                    if n >= 4:
                        pe.wait_ge(read, n - 3)
                    parts, ready = {0: (h_parts, 4), 12: (x_parts, 4), 16: (h_parts, 8), 20: (x_parts, 8)}.get(n, (parts if n else None, 0))
                    if ready:
                        pe.wait_ge(parts.lo_ready, ready)
                    K.slab_done(feature_major3(pe, K.bank[n % 4], w, (parts.hi, parts.lo), KD, HALF))

            @block.scalar
            def _(act):
                split.act(act, 1)
                for i in range(4):
                    h_parts.act(act, pair_of(i), K.h[:, pair_of(i), :])
                split.act(act, 3)
                for i in range(4):
                    x_parts.act(act, pair_of(i), K.attn[:, pair_of(i), :])
                for i in range(4):
                    act.activation(sq[:, two(i), :], o[:, two(i), :], ACT.Square).then_inc(squared, 1)
                for i in range(4):
                    act.wait_ge(summed, i + 1)
                    last = act.activation(sq[:, two(i), :], pair(4 + i), ACT.Ln, bias=K.c("eps"), scale=1.0 / P)
                K.act_own.after(act, last)
                act.activation(sq[:, :, :], sq[:, :, :], ACT.Exp, scale=-0.5).then_inc(rstd_ready, 1)
                for n in range(20):
                    split.act(act, n + 3)
                    K.wait_slabs(act, n0 + n + 1)
                    if n >= 12:
                        if n == 12:
                            for i in range(4):
                                act.wait_ge(o_ready, 2 * i + 2)
                                h_parts.act(act, pair_of(i), o[:, pair_of(i), :])
                        if n >= 16:
                            act.wait_ge(y_ready, 2 * (n - 16) + 2)
                            x_parts.act(act, pair_of(n - 16), y[:, pair_of(n - 16), :])
                        if n == 19:
                            split.act(act, 24)
                    elif n < 4:
                        act.activation(zs[:, two(n), :], pair(n % 4), ACT.Silu).then_inc(read, 1)
                    else:
                        act.activation(gates[:, two(n - 4), :], pair(n % 4), ACT.Sigmoid).then_inc(read, 1)

            @block.vector
            def _(dve):
                own = K.dve_own
                for i in range(4):
                    h_parts.dve(dve, pair_of(i), K.h[:, pair_of(i), :])
                for i in range(4):
                    x_parts.dve(dve, pair_of(i), K.attn[:, pair_of(i), :])
                dve.wait_ge(rstd_ready, 1)
                for h in range(8):
                    last = dve.scalar_tensor_tensor(o[:, h, :], o[:, h, :], K.col2("gdn_norm"), sq[:, h, :], ALU.mult, ALU.mult)
                own.after(dve, last)
                dve.wait_ge(read, 4)
                for h in range(8):
                    dve.tensor_tensor(o[:, h, :], o[:, h, :], zs[:, h, :], ALU.mult).then_inc(o_ready, 1)
                for n in range(12, 20):
                    K.wait_slabs(dve, n0 + n + 1)
                    i = n % 4
                    if n == 12:
                        for q in range(4):
                            h_parts.dve(dve, pair_of(q), o[:, pair_of(q), :])
                        dve.wait_ge(read, 12)
                    if n < 16:
                        dve.tensor_tensor(y[:, two(i), :], pair(i), gates[:, two(i), :], ALU.mult).then_inc(read, 1)
                    else:
                        if n > 16:
                            dve.wait_ge(y_ready, 2 * i)
                        dve.tensor_tensor(tmp[:, :, :], pair(i), gates[:, 8 + 2 * i:10 + 2 * i, :], ALU.mult).then_inc(read, 1)
                        dve.wait_ge(read, n + 1)
                        for k in range(2):
                            dve.tensor_tensor(y[:, 2 * i + k, :], y[:, 2 * i + k, :], tmp[:, k, :], ALU.add).then_inc(y_ready, 1)
                        x_parts.dve(dve, pair_of(i), y[:, pair_of(i), :])
                for i in range(4):
                    K.wait_slabs(dve, n0 + 21 + i)
                    for k in range(2):
                        t = 2 * i + k
                        dve.scalar_tensor_tensor(K.x[:, t, :], K.bank[i][:, k * T:(k + 1) * T], K.mod[:, 16 + t, 0:1],
                                                 K.x[:, t, :], ALU.mult, ALU.add).then_inc(x_updated, 1)


def conv_ffn_stage(K):
    nc = K.nc
    n0 = K.eaten
    with ExitStack() as ctx:
        hidden = Parts(K, ctx, "f_hidden", FK)
        whole_hidden = K.sb("hidden2", [P, 2, 2, T], ctx=ctx)
        raw = [K.sb(f"fraw{i}", [P, 4, T + 2], ctx=ctx) for i in range(2)]
        con = [K.sb(f"fcon{i}", [P, 4, T], ctx=ctx) for i in range(2)]
        gate = [K.sb(f"fgate{i}", [P, 2, T], ctx=ctx) for i in range(2)]
        gain = K.sb("fgain", [P, KD], ctx=ctx)
        gain_ready = K.sem("f_gain_ready")
        norm = Norm(K, ctx, "f", K.x, K.h, gain, K.bank[4], shift=K.mod[:, 24:32, 0],
                    parts=Parts(K, ctx, "fh", KD))
        split = Split(K, ctx, "f", n0, FK + 12)
        raw_ready, conv_ready, silu_ready = K.sem("f_raw_ready"), K.sem("f_conv_ready"), K.sem("f_silu_ready")
        hidden_ready, x_updated = K.sem("f_hidden_ready"), K.sem("f_x_updated")
        pair = lambda b: K.bank[b][:, :].rearrange("p (a t) -> p a t", a=2)
        N = FK // 2
        with nc.Block(no_gpsimd_drain=True) as block:
            @block.sync
            def _(sync):
                K.load_slabs(sync, n0 + FK + 12)

            @block.gpsimd
            def _(pool):
                split.pool(pool)

            @block.tensor
            def _(pe):
                norm.pe(pe)
                for i in range(N):
                    for part in range(2):
                        w = split.next_view(pe)
                        if i >= 2:
                            pe.wait_ge(raw_ready, 2 * (i - 2) + part + 1)
                        parts = norm.parts
                        K.slab_done(feature_major3(pe, K.bank[2 * (i % 2) + part], w, (parts.hi, parts.lo), KD, HALF,
                                                   first=(lambda k: pe.wait_ge(parts.lo_ready, k // 2 + 1))
                                                   if i == part == 0 else None))
                pe.wait_ge(raw_ready, 2 * N)
                ffn_out_pe(K, pe, split, hidden, x_updated)

            @block.scalar
            def _(act):
                norm.act(act, between=lambda: split.act(act, 2))
                for i in range(N + 2):
                    if i < N:
                        for part in range(2):
                            split.act(act, 2 * i + part + 3)
                            K.wait_slabs(act, n0 + 2 * i + part + 1)
                            if i >= 2:
                                act.wait_ge(conv_ready, i - 1)
                            act.copy(raw[i % 2][:, 2 * part:2 * part + 2, 1:T + 1], pair(2 * (i % 2) + part))\
                                .then_inc(raw_ready, 1)
                    else:
                        split.act(act, FK + 3)
                    if i >= 2:
                        act.wait_ge(hidden_ready, i - 1)
                        hidden.act(act, pair_of(i - 2), whole_hidden[:, i % 2, :, :])
                    if 1 <= i <= N:
                        act.wait_ge(conv_ready, i)
                        if i >= 3:
                            act.wait_ge(hidden_ready, i - 2)
                        act.activation(gate[(i - 1) % 2][:, :, :], con[(i - 1) % 2][:, 0:2, :], ACT.Silu).then_inc(silu_ready, 1)
                split.act(act, FK + 12)

            @block.vector
            def _(dve):
                own = K.dve_own
                for i in range(2):
                    dve.memset(raw[i][:, :, 0:1], 0.0)
                    dve.memset(raw[i][:, :, T + 1:T + 2], 0.0)
                own.after(dve, dve.tensor_scalar(gain[:, :], K.mod[:, 32:40, 0], 1.0, None, ALU.add))
                norm.dve(dve)
                for i in range(N + 2):
                    if i >= 2:
                        hidden.dve(dve, pair_of(i - 2), whole_hidden[:, i % 2, :, :])
                    if i < N:
                        r, o = raw[i % 2], con[i % 2]
                        dve.wait_ge(raw_ready, 2 * i + 2)
                        if i >= 2:
                            dve.wait_ge(silu_ready, i - 1)
                            dve.wait_ge(hidden_ready, i - 1)
                        for j in range(3):
                            for q in range(4):
                                t = (FK if q >= 2 else 0) + 2 * i + q % 2
                                tap = K.col2("ffn_conv", 132)[:, 44 * j + t:44 * j + t + 1]
                                if j == 0:
                                    last = dve.tensor_scalar(o[:, q, :], r[:, q, 0:T], tap, K.col2("ffn_b", 44)[:, t:t + 1],
                                                             ALU.mult, ALU.add)
                                else:
                                    last = dve.scalar_tensor_tensor(o[:, q, :], r[:, q, j:j + T], tap, o[:, q, :],
                                                                    ALU.mult, ALU.add)
                            if j < 2:
                                own.after(dve, last)
                        last.then_inc(conv_ready, 1)
                    if 1 <= i <= N:
                        dve.wait_ge(silu_ready, i)
                        if i >= 3:
                            dve.wait_ge(hidden.lo_ready, i - 2)
                        dve.tensor_tensor(whole_hidden[:, (i - 1) % 2, :, :], gate[(i - 1) % 2][:, :, :],
                                          con[(i - 1) % 2][:, 2:4, :], ALU.mult).then_inc(hidden_ready, 1)
                for jj in range(4):
                    K.wait_slabs(dve, n0 + FK + 3 * (jj + 1))
                    for j in range(2):
                        k = 2 * jj + j
                        dve.scalar_tensor_tensor(K.x[:, k, :], K.bank[2 * (jj % 2) + j][:, 0:T], K.mod[:, 40 + k, 0:1],
                                                 K.x[:, k, :], ALU.mult, ALU.add).then_inc(x_updated, 1)


def final_norm_stage(K):
    nc = K.nc
    with ExitStack() as ctx:
        norm = Norm(K, ctx, "final", K.x, K.h, K.col2("final", KD), K.bank[4])
        with nc.Block(no_gpsimd_drain=True) as block:
            @block.scalar
            def _(act):
                norm.act(act)

            @block.tensor
            def _(pe):
                norm.pe(pe)

            @block.vector
            def _(dve):
                norm.dve(dve)


def second_block(K):
    K.col2 = lambda name, n=1: K.prm2[:, ROWS2[name]:ROWS2[name] + n]
    K.plan(second_slabs(K))
    with ExitStack() as ctx:
        K.consts[2] = K.sb("const2", [P, CONSTS[2].shape[1]], ctx=ctx)
        K.prm2 = K.sb("prm2", [P, TILES2 * P], ctx=ctx)
        K.mod = K.sb("mod", [P, 48, 2], ctx=ctx)
        K.attn = K.sb("attn", [P, 8, T], ctx=ctx)
        g = K.gdn = {"o": K.sb("go", [P, 8, T], ctx=ctx)}
        with ExitStack() as gctx:
            for n, w in (("gam", 512), ("beta", 512)):
                g[n] = K.sb("g_" + n, [16, w], ctx=gctx)
            for n in ("gamt", "betat", "kdec", "glast", "bexp"):
                g[n] = K.sb("g_" + n, [P, 64], ctx=gctx)
            g["q"] = K.sb("g_q", [P, 8, T], ctx=gctx)
            g["k"] = K.sb("g_k", [P, 8, 2 * T], ctx=gctx)
            g["vtok"], g["ktok"] = K.sb("g_vtok", [P, 4, 1024], ctx=gctx), K.sb("g_ktok", [P, 4, 1024], ctx=gctx)
            with ExitStack() as hctx:
                K.hc = K.sb("hc", [P, KD, T], ctx=hctx)
                modulation_stage(K)
                latent_attention_stage(K)
                gdn_prepare_stage(K)
            for d in range(2):
                for half in range(2):
                    gdn_chunk_stage(K, d, half)
        merge_stage(K)
        conv_ffn_stage(K)
        final_norm_stage(K)


def build(nc, a, out):
    K = Kernel(nc, a, out)
    with K.ctx:
        K.open()
        K.first = ExitStack()
        prologue(K)
        K.restart()
        with nc.Fori(0, LAYERS) as l:
            K.plan(layer_slabs(K, l))
            load_params(K, l)
            K.col = lambda name, n=1: K.prm[:, PARAM_ROWS[name]:PARAM_ROWS[name] + n]
            ffn_stage(K, "ffn1", K.col("ffn1_norm", KD))
            mixer(K, l)
            xattn_stage(K, l)
            ffn_stage(K, "ffn2", K.col("ffn2_norm", KD))
            K.restart()
        K.first.close()
        K.forget()
        second_block(K)
        epilogue(K)


def kernel(**inputs):
    import concourse.bacc as bacc
    from concourse.bass_utils import run_bass_kernel_spmd

    nc = bacc.Bacc("TRN2", target_bir_lowering=False, num_devices=1)
    arrays, a = {}, {}
    for name, value in {**inputs, **{f"consts{i}": c for i, c in enumerate(CONSTS)}}.items():
        value = np.ascontiguousarray(value)
        if value.ndim == 1:
            value = value.reshape(1, -1)
        arrays["in_" + name] = value
        a[name] = nc.dram_tensor("in_" + name, value.shape, mybir.dt.from_np(value.dtype), kind="ExternalInput").ap()
    out = nc.dram_tensor("out", (1, T, D), F32, kind="ExternalOutput").ap()
    build(nc, a, out)
    r = run_bass_kernel_spmd(nc, [arrays], core_ids=[0])
    return r.results[0]["out"]
```

```python
import numpy as np
from contextlib import ExitStack
import concourse.bass as bass
from concourse import mybir

F32 = mybir.dt.float32
I32 = mybir.dt.int32
ALU = mybir.AluOpType
ACT = mybir.ActivationFunctionType
AX = mybir.AxisListType

P = 128
D = 1024
KD = D // P
T = 256
TT = T // P
LAYERS = 2
FFN = 2816
FK = FFN // P
HALF = 256
RING = 3
EPS = 1e-6
GN_EPS = 64e-5
DECAY = float(np.exp(-0.5))
CH = 64
NEG = -1.0e30
MOD_SLABS = 12
LEVELS = 7

FOX_IN = 3 * 256 + 4
MOBA_IN = 3 * 256
RW0 = FOX_IN + MOBA_IN
CTX_COLS = 512 + 3072 + 32


class Counted:

    def __init__(self, sem):
        self.sem = sem
        self.n = 0

    def on(self, ins, by=1):
        ins.then_inc(self.sem, by)
        self.n += by
        return self.n

    def after(self, eng, ins):
        self.on(ins)
        eng.wait_ge(self.sem, self.n)

    def hold(self, eng):
        if self.n:
            eng.wait_ge(self.sem, self.n)



FIRST_ONLY = ("headsum", "rot", "chunkmask", "gate", "causal", "freq", "gneps")
SECOND_ONLY = ("axial", "levels_back", "future", "past", "axcos", "axsin", "fwd", "bwd")


def constant_tables():
    i = np.arange(P)
    row, col = i[:, None], i[None, :]
    same = (row // CH) == (col // CH)
    parts = {}
    parts["ident"] = row == col
    parts["ones"] = np.ones((P, P))
    parts["headsum"] = same
    rot = np.zeros((P, P))
    for h in (0, 64):
        for j in range(8):
            rot[h + 8 + j, h + j] = -1.0
            rot[h + j, h + 8 + j] = 1.0
    parts["rot"] = rot
    axial = np.zeros((P, P))
    for a in (0, 64):
        for j in range(32):
            axial[a + 32 + j, a + j] = -1.0
            axial[a + j, a + 32 + j] = 1.0
    parts["axial"] = axial
    lev = []
    for l in range(LEVELS):
        join = (row >> (l + 1)) == (col >> (l + 1))
        lev.append(join & (((col >> l) & 1) == 1) & (((row >> l) & 1) == 0))
    parts["levels"] = np.concatenate(lev, 1)
    parts["levels_back"] = np.concatenate([m.T for m in lev], 1)
    strict, incl = same & (row < col), same & (row <= col)
    parts["chunkmask"] = np.concatenate([strict, incl], 1)
    gate = np.ones((P, 4 * T))
    gate[:, ::CH] = 0.0
    parts["gate"] = gate
    parts["nomask"] = np.zeros((P, 512))
    causal = np.where(row >= col, 0.0, NEG)
    parts["causal"] = np.concatenate([np.zeros((P, P)), causal], 1)
    parts["future"] = np.where(row <= col, 0.0, NEG)
    parts["past"] = np.where(row >= col, 0.0, NEG)
    rows, cols = np.arange(T) // 64, np.arange(T) % 64
    inv = (np.float32(10000.0) ** (-np.arange(0, 64, 2, dtype=np.float32) / np.float32(64))).astype(np.float32)
    ang = np.concatenate([rows[None, :].astype(np.float32) * inv[:, None]] * 2
                         + [cols[None, :].astype(np.float32) * inv[:, None]] * 2, 0).astype(np.float32)
    parts["axcos"], parts["axsin"] = np.cos(ang), np.sin(ang)
    inv1 = (np.float32(500000.0) ** (-np.arange(0, 16, 2, dtype=np.float32) / np.float32(16))).astype(np.float32)
    freq = np.zeros((P, 1), np.float32)
    for h in (0, 64):
        freq[h:h + 16, 0] = np.concatenate([inv1, inv1])
    parts["freq"] = freq
    parts["eps"] = np.full((P, 1), EPS)
    parts["gneps"] = np.full((P, 1), GN_EPS)
    parts["fwd"] = row < 8
    parts["bwd"] = row >= 8
    at, tiles = {}, []
    for part in range(3):
        columns, off = [], 0
        for name, a in parts.items():
            if part == (1 if name in FIRST_ONLY else 2 if name in SECOND_ONLY else 0):
                a = np.asarray(a, np.float32)
                at[name] = (part, off, a.shape[1])
                columns.append(a)
                off += a.shape[1]
        tiles.append(np.ascontiguousarray(np.concatenate(columns, 1)))
    return at, tiles


CONST_AT, CONSTS = constant_tables()

PARAM_ROWS = {}


def _rows():
    at = 0
    for name, n in (("ffn1_norm", 8), ("mix_norm", 8), ("xattn_norm", 8), ("xattn_mem_norm", 8),
                    ("ffn2_norm", 8), ("mu_rkv", 12), ("mu_wa", 1), ("mu_g", 2), ("w0", 4), ("a0", 4),
                    ("k_k", 4), ("k_a", 4), ("r_k", 4), ("ln_w", 4), ("ln_b", 4), ("fox_q", 1), ("fox_k", 1),
                    ("moba_q", 1), ("moba_k", 1), ("xq", 1), ("xk", 1), ("f_bias", 1)):
        PARAM_ROWS[name] = at
        at += n
    return at


N_PARAM_ROWS = _rows()


class Kernel:

    def __init__(self, nc, a, out):
        self.nc, self.a, self.out = nc, a, out
        self.ctx = ExitStack()
        self.names = 0

    def sb(self, name, shape, dt=F32, ctx=None):
        self.names += 1
        return (ctx or self.ctx).enter_context(self.nc.sbuf_tensor(f"{name}_{self.names}", shape, dt))

    def open(self):
        nc, ctx = self.nc, self.ctx
        self.sems = {}
        self.bank = [ctx.enter_context(nc.psum_tensor(f"bank{i}", [P, 512], F32)) for i in range(8)]
        self.consts = [self.sb("const", [P, CONSTS[0].shape[1]]), None, None]
        self.ring = [self.sb(f"ring{i}", [P, KD * HALF]) for i in range(RING)]
        self.x = self.sb("x", [P, KD, T])
        self.h = self.sb("h", [P, KD, T])
        self.prm = self.sb("prm", [P, P])
        self.prm2 = self.sb("prm2", [P, TILES2 * P])
        self.col2 = lambda name, n=1: self.prm2[:, ROWS2[name]:ROWS2[name] + n]
        self.cs = self.sb("cs", [P, KD, 2])
        self.mod = self.sb("mod", [P, 48, 2])
        self.sem_ctx = ctx
        self.loaded = [Counted(self.sem(f"slab_loaded{i}")) for i in range(RING)]
        self.done = Counted(self.sem("slab_done"))
        self.pe_own = Counted(self.sem("pe_own"))
        self.act_own = Counted(self.sem("act_own"))
        self.dve_own = Counted(self.sem("dve_own"))
        self.pool_own = Counted(self.sem("pool_own"))
        self.sem_ctx = ExitStack()

    def c(self, name, rows=slice(0, P), first=0, n=None):
        part, off, width = CONST_AT[name]
        return self.consts[part][rows, off + first:off + first + (width - first if n is None else n)]

    def sem(self, name):
        if name not in self.sems:
            self.sems[name] = self.sem_ctx.enter_context(self.nc.semaphore(name))
        return self.sems[name]

    def forget(self):
        keep = {s.sem.name: s.sem for s in self.lasting()}
        self.sem_ctx.close()
        self.sem_ctx = ExitStack()
        self.sems = keep

    def lasting(self):
        return self.loaded + [self.done, self.pe_own, self.act_own, self.dve_own, self.pool_own]

    def clear(self, keep=()):
        ids = sorted(s.num for s in self.sems.values() if s.num not in keep)
        runs = []
        for i in ids:
            if runs and runs[-1][1] == i:
                runs[-1][1] = i + 1
            else:
                runs.append([i, i + 1])
        with self.nc.Block(no_gpsimd_drain=True) as block:
            @block.sync
            def _(sync):
                for first, end in runs:
                    sync.sem_clear(range(first, end))

    def restart(self):
        self.clear()
        for s in self.lasting():
            s.n = 0

    def restart_stages(self):
        self.clear({s.sem.num for s in self.loaded + [self.done]})
        self.split_until = {}
        for s in (self.pe_own, self.act_own, self.dve_own, self.pool_own):
            s.n = 0

    def plan(self, slabs):
        self.slabs, self.issued, self.eaten = slabs, 0, 0
        self.split_until = {}
        self.landed = []
        total = [0] * RING
        for n, pieces in enumerate(slabs):
            total[n % RING] += 16 * len(pieces)
            self.landed.append(total[n % RING])

    def load_slabs(self, sync, upto):
        for n in range(self.issued, min(upto, len(self.slabs))):
            if n - RING in self.split_until:
                sync.wait_ge(*self.split_until[n - RING])
            elif n >= RING:
                sync.wait_ge(self.done.sem, n - RING + 1)
            for src, rows, start, groups, cols in self.slabs[n]:
                dst = self.ring[n % RING][0:rows, start:start + groups * cols]
                sync.dma_start(dst.rearrange("p (k n) -> p k n", k=groups), src)\
                    .then_inc(self.loaded[n % RING].sem, 16)
            self.issued = n + 1

    def next_slab(self, pe):
        n = self.eaten
        self.eaten += 1
        pe.wait_ge(self.loaded[n % RING].sem, self.landed[n])
        return self.ring[n % RING]

    def slab_done(self, last):
        last.then_inc(self.done.sem, 1)

    def wait_slabs(self, eng, n):
        eng.wait_ge(self.done.sem, n)



def groups_of(w, k0, groups, c0, cols):
    return w[:, k0 * P:(k0 + groups) * P, bass.ds(c0, cols)].rearrange("a (k p) n -> p (a k) n", p=P)


def whole(w, c0, cols=HALF):
    return [(groups_of(w, 0, KD, c0, cols), P, 0, KD, cols)]


def view(place, groups=KD, cols=HALF, start=0, rows=P):
    return place[0:rows, start:start + groups * cols].rearrange("p (k n) -> p k n", k=groups)


def feature_major(K, pe, bank, w, act, kd, cols, tokens=T, at=0):
    for j in range(0, cols, P):
        m = min(P, cols - j)
        for k in range(kd):
            last = pe.matmul(bank[0:m, at:at + tokens], w[:, k, j:j + m], act[:, k, 0:tokens],
                             start=(k == 0), stop=(k == kd - 1))
        at += tokens
    return last


def token_major(K, pe, bank, w, act, kd, cols, tiles=(0, 1)):
    for i, tt in enumerate(tiles):
        for k in range(kd):
            last = pe.matmul(bank[:, i * cols:(i + 1) * cols], act[:, k, tt * P:(tt + 1) * P],
                             w[:, k, 0:cols], start=(k == 0), stop=(k == kd - 1))
    return last


F32R = mybir.dt.float32r


class Split:

    def __init__(self, K, ctx, tag, n0, count, places=3):
        self.K, self.n0, self.count, self.issued, self.PLACES = K, n0, count, 0, places
        self.hi = [K.sb(f"slab_hi{i}", [P, KD * HALF], F32R, ctx=ctx) for i in range(self.PLACES)]
        self.lo = [K.sb(f"slab_lo{i}", [P, KD * HALF], F32R, ctx=ctx) for i in range(self.PLACES)]
        self.hi_ready, self.lo_ready = K.sem(tag + "_slab_hi"), K.sem(tag + "_slab_lo")
        for i in range(count):
            K.split_until[n0 + i] = (self.lo_ready, i + 1)

    def used(self, i):
        return sum(groups * cols for _, _, _, groups, cols in self.K.slabs[self.n0 + i])

    def act(self, act, upto):
        K = self.K
        for i in range(self.issued, min(upto, self.count)):
            n, w = self.n0 + i, self.used(i)
            act.wait_ge(K.loaded[n % RING].sem, K.landed[n])
            if i >= self.PLACES:
                K.wait_slabs(act, n - self.PLACES + 1)
            act.copy(self.hi[i % self.PLACES][:, 0:w], K.ring[n % RING][:, 0:w]).then_inc(self.hi_ready, 1)
            self.issued = i + 1

    def pool(self, pool):
        K = self.K
        for i in range(self.count):
            w, place = self.used(i), K.ring[(self.n0 + i) % RING]
            pool.wait_ge(self.hi_ready, i + 1)
            pool.tensor_tensor(self.lo[i % self.PLACES][:, 0:w], place[:, 0:w],
                               self.hi[i % self.PLACES][:, 0:w].bitcast(F32), ALU.subtract).then_inc(self.lo_ready, 1)

    def next_slab(self, pe):
        K = self.K
        i = K.eaten - self.n0
        K.eaten += 1
        pe.wait_ge(self.lo_ready, i + 1)
        return self.hi[i % self.PLACES], self.lo[i % self.PLACES]

    def next_view(self, pe, groups=KD, cols=HALF):
        return self.view(self.next_slab(pe), groups, cols)

    @staticmethod
    def view(places, groups=KD, cols=HALF, start=0):
        return [view(place, groups, cols, start) for place in places]


def product3(pe, out, w, act, start, stop):
    pe.matmul(out, w[0], act[0], start=start, stop=False)
    pe.matmul(out, w[0], act[1], start=False, stop=False)
    return pe.matmul(out, w[1], act[0], start=False, stop=stop)


def feature_major3(pe, bank, w, act, kd, cols, at=0, first=None):
    for j in range(0, cols, P):
        for k in range(kd):
            if first is not None and j == 0:
                first(k)
            last = product3(pe, bank[:, at:at + T], [p[:, k, j:j + P] for p in w], [p[:, k, :] for p in act],
                            k == 0, k == kd - 1)
        at += T
    return last


def token_major3(pe, bank, w, act, kd, cols, tiles=(0, 1)):
    for i, tt in enumerate(tiles):
        for k in range(kd):
            last = product3(pe, bank[:, i * cols:(i + 1) * cols], [p[:, k, tt * P:(tt + 1) * P] for p in act],
                            [p[:, k, 0:cols] for p in w], k == 0, k == kd - 1)
    return last


class Parts:

    def __init__(self, K, ctx, tag, groups):
        self.hi = K.sb(tag + "_hi", [P, groups, T], F32R, ctx=ctx)
        self.lo = K.sb(tag + "_lo", [P, groups, T], F32R, ctx=ctx)
        self.hi_ready, self.lo_ready = K.sem(tag + "_hi_ready"), K.sem(tag + "_lo_ready")
        self.splits = 0

    def act(self, act, t, source):
        act.copy(self.hi[:, t, :], source).then_inc(self.hi_ready, 1)

    def dve(self, dve, t, source):
        self.splits += 1
        dve.wait_ge(self.hi_ready, self.splits)
        dve.tensor_tensor(self.lo[:, t, :], source, self.hi[:, t, :].bitcast(F32), ALU.subtract)\
            .then_inc(self.lo_ready, 1)


def pair_of(i):
    return slice(2 * i, 2 * i + 2)


class Norm:

    def __init__(self, K, ctx, tag, x, h, gain, bank, shift=None, parts=None, sq=None):
        self.K, self.x, self.h, self.gain, self.bank = K, x, h, gain, bank
        self.shift, self.parts = shift, parts
        self.sq = h if sq is None else sq
        self.rstd = K.sb("rstd", [P, T], ctx=ctx)
        self.squared = K.sem(tag + "_squared")
        self.summed = K.sem(tag + "_summed")
        self.rstd_ready = K.sem(tag + "_rstd_ready")
        self.h_ready = K.sem(tag + "_h_ready")

    def act(self, act, between=None):
        K = self.K
        for i in range(4):
            act.activation(self.sq[:, 2 * i:2 * i + 2, :], self.x[:, 2 * i:2 * i + 2, :], ACT.Square)\
                .then_inc(self.squared, 1)
        if between is not None:
            between()
        act.wait_ge(self.summed, 1)
        K.act_own.after(act, act.activation(self.rstd[:, :], self.bank[:, 0:T], ACT.Ln,
                                            bias=K.c("eps"), scale=1.0 / D))
        act.activation(self.rstd[:, :], self.rstd[:, :], ACT.Exp, scale=-0.5).then_inc(self.rstd_ready, 1)
        if self.parts is not None:
            for i in range(KD // 2):
                act.wait_ge(self.h_ready, 2 * i + 2)
                self.parts.act(act, pair_of(i), self.h[:, pair_of(i), :])

    def pe(self, pe):
        for k in range(KD):
            if k % 2 == 0:
                pe.wait_ge(self.squared, k // 2 + 1)
            last = pe.matmul(self.bank[:, 0:T], self.K.c("ones"), self.sq[:, k, :], start=(k == 0), stop=(k == KD - 1))
        last.then_inc(self.summed, 1)

    def dve(self, dve):
        K = self.K
        dve.wait_ge(self.rstd_ready, 1)
        for k in range(KD):
            ins = dve.scalar_tensor_tensor(self.h[:, k, :], self.x[:, k, :], self.gain[:, k:k + 1], self.rstd[:, :],
                                           ALU.mult, ALU.mult)
            if self.shift is not None:
                K.dve_own.after(dve, ins)
                ins = dve.tensor_scalar(self.h[:, k, :], self.h[:, k, :], self.shift[:, k:k + 1], None, ALU.add)
            ins.then_inc(self.h_ready, 1)
        if self.parts is not None:
            for i in range(KD // 2):
                self.parts.dve(dve, pair_of(i), self.h[:, pair_of(i), :])


def ffn_out_pe(K, pe, split, hidden, x_updated):
    for jj in range(4):
        if jj >= 2:
            pe.wait_ge(x_updated, 2 * (jj - 1))
        for k0 in (0, 8, 16):
            g = min(KD, FK - k0)
            w = split.next_view(pe, groups=g)
            for j in range(2):
                for k in range(g):
                    if jj == j == 0:
                        pe.wait_ge(hidden.lo_ready, (k0 + k) // 2 + 1)
                    last = product3(pe, K.bank[2 * (jj % 2) + j][:, 0:T], [p[:, k, j * P:(j + 1) * P] for p in w],
                                    (hidden.hi[:, k0 + k, :], hidden.lo[:, k0 + k, :]), k0 + k == 0, k0 + k == FK - 1)
            K.slab_done(last)


def ffn_stage(K, tag, gain, l=None):
    nc = K.nc
    n0 = K.eaten
    N = FK // 2
    with ExitStack() as ctx:
        hidden = Parts(K, ctx, tag + "_hidden", FK)
        whole_hidden = K.sb("hidden", [P, 2, 2 * T], ctx=ctx)
        gate = K.sb("gate", [P, 2, 2 * T], ctx=ctx)
        parts = Parts(K, ctx, tag + "_h", KD)
        norm = Norm(K, ctx, tag, K.x, K.h, gain, K.bank[4], parts=parts)
        split = Split(K, ctx, tag, n0, FK + 12)
        params = None if l is None else LayerParams(K, ctx, l)
        silu_ready, product_ready = K.sem(tag + "_silu_ready"), K.sem(tag + "_product_ready")
        x_updated = K.sem(tag + "_x_updated")
        flat = lambda x: x.rearrange("p a t -> p (a t)")
        with nc.Block(no_gpsimd_drain=True) as block:
            @block.sync
            def _(sync):
                K.load_slabs(sync, n0 + RING)
                if params is not None:
                    params.sync(sync)
                K.load_slabs(sync, n0 + FK + 12 + RING)

            @block.gpsimd
            def _(pool):
                split.pool(pool)

            @block.scalar
            def _(act):
                norm.act(act, between=lambda: split.act(act, 2))
                for i in range(N):
                    split.act(act, 2 * i + 4)
                    K.wait_slabs(act, n0 + 2 * i + 1)
                    if i >= 2:
                        act.wait_ge(product_ready, i - 1)
                    act.activation(gate[:, i % 2, :], K.bank[2 * (i % 2)][:, :], ACT.Silu).then_inc(silu_ready, 1)
                    split.act(act, 2 * i + 5)
                    act.wait_ge(product_ready, i + 1)
                    act.copy(flat(hidden.hi[:, pair_of(i), :]), whole_hidden[:, i % 2, :]).then_inc(hidden.hi_ready, 1)
                split.act(act, FK + 12)

            @block.tensor
            def _(pe):
                norm.pe(pe)
                if params is not None:
                    params.pe_first(pe)
                for i in range(N):
                    if i == 2 and params is not None:
                        params.pe_rest(pe)
                    for part in range(2):
                        w = split.next_view(pe)
                        if i >= 2:
                            pe.wait_ge(product_ready, i - 1)
                        K.slab_done(feature_major3(pe, K.bank[2 * (i % 2) + part], w, (parts.hi, parts.lo), KD, HALF,
                                                   first=(lambda k: pe.wait_ge(parts.lo_ready, k // 2 + 1))
                                                   if i == part == 0 else None))
                pe.wait_ge(product_ready, N)
                ffn_out_pe(K, pe, split, hidden, x_updated)

            @block.vector
            def _(dve):
                if params is not None:
                    params.dve_first(dve)
                norm.dve(dve)
                for i in range(N + 1):
                    if i == 2 and params is not None:
                        params.dve_rest(dve)
                    if i < N:
                        dve.wait_ge(silu_ready, i + 1)
                        K.wait_slabs(dve, n0 + 2 * i + 2)
                        if i >= 2:
                            dve.wait_ge(hidden.lo_ready, i - 1)
                        dve.tensor_tensor(whole_hidden[:, i % 2, :], gate[:, i % 2, :],
                                          K.bank[2 * (i % 2) + 1][:, :], ALU.mult).then_inc(product_ready, 1)
                    if i >= 1:
                        hidden.dve(dve, pair_of(i - 1),
                                   whole_hidden[:, (i - 1) % 2, :].rearrange("p (a t) -> p a t", a=2))
                for jj in range(4):
                    K.wait_slabs(dve, n0 + FK + 3 * (jj + 1))
                    for j in range(2):
                        k = 2 * jj + j
                        dve.scalar_tensor_tensor(K.x[:, k, :], K.bank[2 * (jj % 2) + j][:, 0:T], 0.5, K.x[:, k, :],
                                                 ALU.mult, ALU.add).then_inc(x_updated, 1)


def ffn_slabs(w_in, w_out):
    slabs = []
    for i in range(FK // 2):
        slabs += [whole(w_in, i * HALF), whole(w_in, FFN + i * HALF)]
    for jj in range(4):
        for k0 in (0, 8, 16):
            g = min(KD, FK - k0)
            slabs.append([(groups_of(w_out, k0, g, jj * HALF, HALF), P, 0, g, HALF)])
    return slabs


def load_feature_major(K, block_ctx, tag, src, dst, banks, queue="sync"):
    rows = K.sb(tag + "_rows", [P, TT, D], ctx=block_ctx)
    arrived, turned, copied = K.sem(tag + "_arrived"), K.sem(tag + "_turned"), K.sem(tag + "_copied")

    def start(eng):
        eng.dma_start(rows[:, :, :], src.rearrange("(t p) d -> p t d", p=P)).then_inc(arrived, 16)

    def pe_part(pe):
        pe.wait_ge(arrived, 16)
        for i in range(4):
            bank = K.bank[banks[i % len(banks)]]
            if i >= len(banks):
                pe.wait_ge(copied, i - len(banks) + 1)
            for j in range(2):
                for tt in range(TT):
                    last = pe.transpose(bank[:, j * T + tt * P:j * T + (tt + 1) * P],
                                        rows[:, tt, (2 * i + j) * P:(2 * i + j + 1) * P], K.c("ident"))
            last.then_inc(turned, 1)

    def act_part(act):
        for i in range(4):
            act.wait_ge(turned, i + 1)
            act.copy(dst[:, 2 * i:2 * i + 2, :].rearrange("p a t -> p (a t)"), K.bank[banks[i % len(banks)]][:, :])\
                .then_inc(copied, 1)
    return start, pe_part, act_part, copied


class Rows2:

    def __init__(self, K, ctx):
        self.K, a = K, K.a
        rows = self.rows = K.sb("rows2", [P, TILES2, P], ctx=ctx)
        self.cleared, self.arrived, self.turned = K.sem("rows2_cleared"), K.sem("rows2_arrived"), K.sem("rows2_turned")
        self.prm_ready = K.sem("prm2_ready")
        pieces = []

        def put(name, src, width=P):
            r, at, n = ROWS2[name], 0, src.shape[0]
            while at < n:
                tile, row = divmod(r + at, P)
                m = min(n - at, P - row)
                pieces.append((rows[row:row + m, tile, 0:width], src[at:at + m, :]))
                at += m
        by_rows = lambda ap: ap.rearrange("a (r c) -> (a r) c", c=P)
        for name, key in (("c", "c_2"), ("c_ctx", "c_ctx_2"), ("b_mod", "b_mod_2"), ("q_norm", "q_norm_w_2"),
                          ("k_norm", "k_norm_w_2"), ("gdn_norm", "gdn_norm_w_2"), ("final", "final_norm_w_2"),
                          ("ffn_b", "ffn_conv_b_2")):
            put(name, by_rows(a[key]))
        put("a_log", a["a_log_2"].rearrange("a d h -> a (d h)"), 16)
        put("dt_bias", a["dt_bias_2"].rearrange("a d h -> a (d h)"), 16)
        put("conv", a["conv_qkv_w_2"].rearrange("a j (r c) -> (a j r) c", c=P))
        put("ffn_conv", a["ffn_conv_w_2"].rearrange("a j (r c) -> (a j r) c", c=P))
        self.pieces = pieces

    def sync(self, sync):
        sync.wait_ge(self.cleared, 1)
        for dst, src in self.pieces:
            sync.dma_start(dst, src).then_inc(self.arrived, 16)

    def pe(self, pe):
        pe.wait_ge(self.arrived, 16 * len(self.pieces))
        for i in range(TILES2):
            last = pe.transpose(self.K.bank[7][:, i * P:(i + 1) * P], self.rows[:, i, :], self.K.c("ident"))
        last.then_inc(self.turned, 1)

    def act(self, act):
        act.wait_ge(self.prm_ready, 1)
        for i, name in enumerate(("c", "c_ctx")):
            act.activation(self.K.cs[:, :, i], self.K.col2(name, KD), ACT.Silu)

    def dve_first(self, dve):
        dve.memset(self.rows[:, :, :], 0.0).then_inc(self.cleared, 1)
        dve.memset(self.K.mod[:, :, :], 0.0)

    def dve(self, dve):
        dve.wait_ge(self.turned, 1)
        dve.tensor_copy(self.K.prm2[:, :], self.K.bank[7][:, 0:TILES2 * P]).then_inc(self.prm_ready, 1)


def prologue(K):
    nc, a = K.nc, K.a
    first = K.first
    K.consts[1] = K.sb("const1", [P, CONSTS[1].shape[1]], ctx=first)
    K.mem = K.sb("mem", [P, KD, T], ctx=first)
    K.cos = K.sb("cos", [P, T], ctx=first)
    K.sin = K.sb("sin", [P, T], ctx=first)
    with ExitStack() as ctx:
        pos_i = K.sb("pos_i", [1, T], I32, ctx=ctx)
        pos = K.sb("pos", [1, T], ctx=ctx)
        ang = K.sb("ang", [P, T], ctx=ctx)
        turns = K.sb("turns", [P, T], ctx=ctx)
        quarter = K.sb("quarter", [P, T], ctx=ctx)
        over = K.sb("over", [P, T], ctx=ctx)
        consts_in, pos_in = K.sem("consts_in"), K.sem("pos_in")
        pos_ready, pos_spread, angles_ready = K.sem("pos_ready"), K.sem("pos_spread"), K.sem("angles_ready")
        x_start, x_pe, x_act, x_copied = load_feature_major(K, ctx, "x", a["x"][0], K.x, (0, 1))
        mem_in = K.sb("mem_in", [P, KD, T], ctx=ctx)
        m_start, m_pe, m_act, m_copied = load_feature_major(K, ctx, "mem", a["mem"][0], mem_in, (2, 3))
        rows2 = Rows2(K, ctx)
        norm = Norm(K, ctx, "mem", mem_in, K.mem, K.c("ones")[:, 0:KD], K.bank[4])
        with nc.Block(no_gpsimd_drain=True) as block:
            @block.sync
            def _(sync):
                for i in range(2):
                    sync.dma_start(K.consts[i][:, :], a[f"consts{i}"]).then_inc(consts_in, 16)
                x_start(sync)
                m_start(sync)
                sync.dma_start(pos_i[:, :], a["positions"]).then_inc(pos_in, 16)
                rows2.sync(sync)

            @block.scalar
            def _(act):
                act.wait_ge(consts_in, 32)
                x_act(act)
                m_act(act)
                act.wait_ge(m_copied, 4)
                norm.act(act)
                act.wait_ge(angles_ready, 1)
                act.activation(K.sin[:, :], ang[:, :], ACT.Sin)
                act.activation(K.cos[:, :], quarter[:, :], ACT.Sin)
                rows2.act(act)

            @block.tensor
            def _(pe):
                pe.wait_ge(consts_in, 32)
                x_pe(pe)
                m_pe(pe)
                norm.pe(pe)
                pe.wait_ge(pos_ready, 1)
                pe.matmul(K.bank[5][:, 0:T], K.c("ones", slice(0, 1)), pos[:, :], start=True, stop=True)\
                    .then_inc(pos_spread, 1)
                rows2.pe(pe)

            @block.vector
            def _(dve):
                own = K.dve_own
                rows2.dve_first(dve)
                dve.wait_ge(consts_in, 32)
                dve.wait_ge(pos_in, 16)
                dve.tensor_copy(pos[:, :], pos_i[:, :]).then_inc(pos_ready, 1)
                norm.dve(dve)
                dve.wait_ge(pos_spread, 1)
                own.after(dve, dve.tensor_scalar(ang[:, :], K.bank[5][:, 0:T], K.c("freq"), None, ALU.mult))
                own.after(dve, dve.tensor_scalar(turns[:, :], ang[:, :], float(1 / (2 * np.pi)), 12582912.0,
                                                 ALU.mult, ALU.add))
                own.after(dve, dve.tensor_scalar(turns[:, :], turns[:, :], 12582912.0, None, ALU.subtract))
                for part in (6.28125, 2029.0 / 2 ** 20, 2 * np.pi - 6.28125 - 2029.0 / 2 ** 20):
                    own.after(dve, dve.scalar_tensor_tensor(ang[:, :], turns[:, :], -float(part), ang[:, :],
                                                            ALU.mult, ALU.add))
                own.after(dve, dve.tensor_scalar(quarter[:, :], ang[:, :], float(np.pi / 2), None, ALU.add))
                own.after(dve, dve.tensor_scalar(over[:, :], quarter[:, :], float(np.pi), float(2 * np.pi),
                                                 ALU.is_gt, ALU.mult))
                own.after(dve, dve.tensor_tensor(quarter[:, :], quarter[:, :], over[:, :], ALU.subtract))
                own.after(dve, dve.tensor_scalar(quarter[:, :], quarter[:, :], 3.1415925, -3.1415925, ALU.min, ALU.max))
                dve.tensor_scalar(ang[:, :], ang[:, :], 3.1415925, -3.1415925, ALU.min, ALU.max)\
                    .then_inc(angles_ready, 1)
                rows2.dve(dve)


class LayerParams:

    FIRST = 8

    def __init__(self, K, ctx, l):
        self.K, a = K, K.a
        rows = self.rows = K.sb("param_rows", [P, P], ctx=ctx)
        self.cleared, self.arrived, self.turned = K.sem("prm_cleared"), K.sem("prm_arrived"), K.sem("prm_turned")
        self.first_in = K.sem("prm_first_in")

        def layer(name):
            return a[name][bass.ds(l, 1), :]
        pieces = []
        for name, key, n in (("ffn1_norm", "ffn1_norm", 8), ("mix_norm", "mix_norm", 8), ("xattn_norm", "xattn_norm", 8),
                             ("xattn_mem_norm", "xattn_mem_norm", 8), ("ffn2_norm", "ffn2_norm", 8),
                             ("w0", "rwkv_w0", 4), ("a0", "rwkv_a0", 4), ("k_k", "rwkv_k_k", 4), ("k_a", "rwkv_k_a", 4),
                             ("ln_w", "rwkv_ln_w", 4), ("ln_b", "rwkv_ln_b", 4), ("xq", "xattn_q_gain", 1),
                             ("xk", "xattn_k_gain", 1)):
            r = PARAM_ROWS[name]
            pieces.append((rows[r:r + n, :], layer(key).rearrange("a (r c) -> (a r) c", c=P)))
        r = PARAM_ROWS["mu_rkv"]
        pieces.append((rows[r:r + 12, :], layer("rwkv_mu")[:, 0:1536].rearrange("a (r c) -> (a r) c", c=P)))
        r = PARAM_ROWS["mu_wa"]
        pieces.append((rows[r:r + 2, :], layer("rwkv_mu")[:, 1536:1792].rearrange("a (r c) -> (a r) c", c=P)))
        pieces.append((rows[r + 2:r + 3, 0:32], layer("rwkv_mu")[:, 1792:1824]))
        r = PARAM_ROWS["r_k"]
        pieces.append((rows[r:r + 4, :], a["rwkv_r_k"][bass.ds(l, 1), :, :].rearrange("a (r h) d -> (a r) (h d)", h=2)))
        for name, key in (("fox_q", "fox_q_gain"), ("fox_k", "fox_k_gain"), ("moba_q", "moba_q_gain"),
                          ("moba_k", "moba_k_gain")):
            r = PARAM_ROWS[name]
            pieces += [(rows[r:r + 1, 0:64], layer(key)), (rows[r:r + 1, 64:128], layer(key))]
        r = PARAM_ROWS["f_bias"]
        pieces.append((rows[r:r + 1, 0:4], layer("fox_f_bias")))
        self.pieces = pieces

    def sync(self, sync):
        sync.wait_ge(self.cleared, 1)
        for i, (dst, src) in enumerate(self.pieces):
            sync.dma_start(dst, src).then_inc(self.first_in if i == 0 else self.arrived, 16)

    def pe_first(self, pe):
        pe.wait_ge(self.first_in, 16)
        n = self.FIRST
        pe.transpose(self.K.bank[7][:, 0:n], self.rows[0:n, :], self.K.c("ident", slice(0, n), n=n))\
            .then_inc(self.turned, 1)

    def pe_rest(self, pe):
        pe.wait_ge(self.arrived, 16 * (len(self.pieces) - 1))
        pe.transpose(self.K.bank[6][:, 0:P], self.rows[:, :], self.K.c("ident")).then_inc(self.turned, 1)

    def dve_first(self, dve):
        K = self.K
        dve.memset(self.rows[:, :], 0.0).then_inc(self.cleared, 1)
        dve.wait_ge(self.turned, 1)
        K.dve_own.after(dve, dve.tensor_copy(K.prm[:, 0:self.FIRST], K.bank[7][:, 0:self.FIRST]))

    def dve_rest(self, dve):
        dve.wait_ge(self.turned, 2)
        self.K.dve_own.on(dve.tensor_copy(self.K.prm[:, self.FIRST:], self.K.bank[6][:, self.FIRST:P]))


def epilogue(K, gain=None):
    nc = K.nc
    with ExitStack() as ctx:
        rows = K.sb("out_rows", [P, TT, D], ctx=ctx)
        turned, copied, stored = K.sem("out_turned"), K.sem("out_copied"), K.sem("out_stored")
        with nc.Block() as block:
            @block.tensor
            def _(pe):
                for i in range(4):
                    for j in range(4):
                        last = pe.transpose(K.bank[i][:, j * P:(j + 1) * P],
                                            K.h[:, 4 * (i % 2) + j, (i // 2) * P:(i // 2 + 1) * P], K.c("ident"))
                    last.then_inc(turned, 1)

            @block.scalar
            def _(act):
                for i in range(4):
                    act.wait_ge(turned, i + 1)
                    act.copy(rows[:, i // 2, (i % 2) * 512:(i % 2 + 1) * 512], K.bank[i][:, :]).then_inc(copied, 1)

            @block.sync
            def _(sync):
                for t in range(TT):
                    sync.wait_ge(copied, 2 * t + 2)
                    sync.dma_start(K.out[0, t * P:(t + 1) * P, :], rows[:, t, :]).then_inc(stored, 16)
                sync.wait_ge(stored, 16 * TT)


def layer_slabs(K, l):
    def w(name):
        return K.a[name][bass.ds(l, 1), :, :]
    mix = w("mix_w_in")
    slabs = ffn_slabs(w("ffn1_w_in"), w("ffn1_w_out"))
    slabs += mix_slabs(K, mix, l)
    slabs += [whole(K.a["w_mod_2"], l * (MOD_SLABS * HALF) + i * HALF) for i in range(MOD_SLABS)]
    slabs += [whole(w("mix_w_out"), i * HALF) for i in range(4)]
    slabs += xattn_slabs(K, l)
    slabs += ffn_slabs(w("ffn2_w_in"), w("ffn2_w_out"))
    return slabs



MIX_ORDER = ([("wa", RW0 + 1536, 128), ("g", RW0 + 1664, 160)]
             + [("k", RW0 + 512 + i * HALF, HALF) for i in range(2)]
             + [("r", RW0 + i * HALF, HALF) for i in range(2)]
             + [("v", RW0 + 1024 + i * HALF, HALF) for i in range(2)]
             + [("fox_q", 0, HALF), ("fox_k", 256, HALF), ("fox_v", 512, HALF)]
             + [("moba_q", FOX_IN, HALF), ("moba_k", FOX_IN + 256, HALF), ("moba_v", FOX_IN + 512, HALF)])


def mix_slabs(K, w, l):
    slabs = []
    for name, c0, cols in MIX_ORDER:
        pieces = [(groups_of(w, 0, KD, c0, cols), P, 0, KD, cols)]
        if name == "wa":
            pieces.append((groups_of(w, 0, KD, 768, 4), P, KD * 128, KD, 4))
        slabs.append(pieces)
    return slabs


def mixer(K, l):
    with ExitStack() as ctx:
        s = K.mx = {}
        s["y"] = K.h
        s["qk"] = K.sb("qk", [P, 8, T], ctx=ctx)
        s["v"] = K.sb("vtok", [P, TT, 512], ctx=ctx)
        s["f"] = K.sb("f", [4, T], ctx=ctx)
        with ExitStack() as rctx:
            s["ar"] = K.sb("ar", [P, 4, TT, 2, P], ctx=rctx)
            for n in ("kt", "bt", "bv", "g"):
                s[n] = K.sb(n, [P, 4, T], ctx=rctx)
            for n in ("ktok", "btok", "vtok_r"):
                s[n] = K.sb(n, [P, TT, 512], ctx=rctx)
            s["es"] = K.sb("es", [P, 4, 4], ctx=rctx)
            project_stage(K, l)
            rwkv_stage(K)
        mix_out_stage(K)


def project_stage(K, l):
    nc, s = K.nc, K.mx
    n0 = K.eaten
    n_slabs = len(MIX_ORDER)
    with ExitStack() as ctx:
        t3 = lambda name: K.sb(name, [P, 4, T], ctx=ctx)
        z = K.sb("z", [P, 12, T + 1], ctx=ctx)
        zs = K.sb("zs", [P, 3, T + 1], ctx=ctx)
        diff = K.sb("diff", [P, 2, T], ctx=ctx)
        kk, sq, lw, cum, dd = t3("kk"), t3("sq"), t3("lw"), t3("cum"), t3("dd")
        kp, rate = s["kt"], s["bt"]
        nrm, d3, e2 = sq, lw, cum
        e1, e3 = K.h[:, 0:4, :], K.h[:, 4:8, :]
        w2a2 = K.sb("w2a2", [P, 512], ctx=ctx)
        g2 = K.sb("g2", [P, 2, 512], ctx=ctx)
        om = K.sb("om", [P, 4], ctx=ctx)
        norm = Norm(K, ctx, "mix", K.x, K.h, K.col("mix_norm", KD), K.bank[4],
                    parts=Parts(K, ctx, "mix_h", KD))
        split = Split(K, ctx, "mix_in", n0 + 2, n_slabs - 2, places=2)
        lora_in, z_ready, mixed = K.sem("lora_in"), K.sem("z_ready"), K.sem("mixed")
        ranks_ready, lora_ready, lora_read = K.sem("ranks_ready"), K.sem("lora_ready"), K.sem("lora_read")
        kk_ready, kk_squared, kk_summed, kk_norm = K.sem("kk_ready"), K.sem("kk_squared"), K.sem("kk_summed"), K.sem("kk_norm")
        decay_diff, decays_ready = K.sem("decay_diff"), K.sem("decays_ready")
        bonus_in, bonus_summed, bonus_read = K.sem("bonus_in"), K.sem("bonus_summed"), K.sem("bonus_read")
        turn_in, turned, turn_copied = K.sem("turn_in"), K.sem("turned"), K.sem("turn_copied")
        z_cleared = K.sem("z_cleared")

        def bank4(b):
            return K.bank[b][:, :].rearrange("p (a t) -> p a t", a=2)

        with nc.Block(no_gpsimd_drain=True) as block:
            @block.sync
            def _(sync):
                sync.dma_start(w2a2[0:64, :], K.a["rwkv_w2"][bass.ds(l, 1), :, :].rearrange("a k n -> (a k) n"))\
                    .then_inc(lora_in, 16)
                sync.dma_start(w2a2[64:128, :], K.a["rwkv_a2"][bass.ds(l, 1), :, :].rearrange("a k n -> (a k) n"))\
                    .then_inc(lora_in, 16)
                sync.dma_start(g2[:, 0, :], K.a["rwkv_g2"][bass.ds(l, 1), 0:128, :].rearrange("a k n -> (a k) n"))\
                    .then_inc(lora_in, 16)
                sync.dma_start(g2[0:32, 1, :], K.a["rwkv_g2"][bass.ds(l, 1), 128:160, :].rearrange("a k n -> (a k) n"))\
                    .then_inc(lora_in, 16)
                K.load_slabs(sync, n0 + n_slabs + RING)

            def evacuate(act, n):
                name = MIX_ORDER[n][0]
                split.act(act, n + split.PLACES - 1)
                K.wait_slabs(act, n0 + n + 1)
                b = K.bank[n % 4]
                if name == "wa":
                    act.copy(s["f"][:, :], b[0:4, T:2 * T])
                    ins = act.copy(zs[:, 0, 1:], b[:, 0:T])
                elif name == "g":
                    act.copy(zs[:, 1, 1:], b[:, 0:T])
                    ins = act.copy(zs[0:32, 2, 1:], b[0:32, T:2 * T])
                elif name in ("r", "k", "v"):
                    i = {"k": 2, "r": 4, "v": 6}[name]
                    t = {"r": 0, "k": 4, "v": 8}[name] + 2 * (n - i)
                    ins = act.copy(z[:, t:t + 2, 1:], bank4(n % 4))
                elif name.endswith("_v"):
                    c = 0 if name == "fox_v" else HALF
                    ins = act.copy(s["v"][:, :, c:c + HALF], bank4(n % 4))
                else:
                    t = {"fox_q": 0, "fox_k": 2, "moba_q": 4, "moba_k": 6}[name]
                    ins = act.copy(s["qk"][:, t:t + 2, :], bank4(n % 4))
                ins.then_inc(z_ready, 1)

            @block.gpsimd
            def _(pool):
                split.pool(pool)

            @block.scalar
            def _(act):
                norm.act(act)
                for n in range(8):
                    evacuate(act, n)
                act.wait_ge(mixed, 2)
                act.activation(zs[0:64, 0, 1:], zs[0:64, 0, 1:], ACT.Tanh)
                act.activation(zs[:, 1, 1:], zs[:, 1, 1:], ACT.Sigmoid)
                act.activation(zs[0:32, 2, 1:], zs[0:32, 2, 1:], ACT.Sigmoid).then_inc(ranks_ready, 1)
                for n in range(8, 11):
                    evacuate(act, n)
                act.wait_ge(lora_ready, 1)
                for t in range(4):
                    act.activation(lw[:, t, :], K.bank[4 + t // 2][:, (t % 2) * T:(t % 2 + 1) * T], ACT.Sigmoid,
                                   bias=K.col("w0", 4)[:, t:t + 1])
                for t in range(4):
                    last = act.activation(rate[:, t, :], K.bank[6 + t // 2][:, (t % 2) * T:(t % 2 + 1) * T], ACT.Sigmoid,
                                          bias=K.col("a0", 4)[:, t:t + 1])
                last.then_inc(lora_read, 1)
                act.wait_ge(kk_ready, 1)
                act.activation(sq[:, :, :], kk[:, :, :], ACT.Square).then_inc(kk_squared, 1)
                for n in range(11, 14):
                    evacuate(act, n)
                act.wait_ge(lora_ready, 2)
                for i in range(2):
                    last = act.copy(s["g"][:, 2 * i:2 * i + 2, :], bank4(4 + i))
                last.then_inc(lora_read, 1)
                act.wait_ge(kk_summed, 1)
                for i in range(2):
                    last = act.activation(nrm[:, 2 * i:2 * i + 2, :], bank4(6 + i), ACT.Sqrt)
                last.then_inc(kk_norm, 1)
                act.wait_ge(decay_diff, 1)
                act.activation(e1[:, :, :], dd[:, :, :], ACT.Exp)
                act.activation(e2[:, :, :], dd[:, :, :], ACT.Exp, scale=-1.0)
                act.activation(e3[:, :, :], d3[:, :, :], ACT.Exp)
                act.activation(s["es"][:, :, 0:3], s["es"][:, :, 0:3], ACT.Exp).then_inc(decays_ready, 1)
                for i, dst in enumerate(("vtok_r", "vtok_r", "ktok", "ktok", "btok", "btok")):
                    act.wait_ge(turned, i + 1)
                    act.copy(s[dst][:, i % 2, :], K.bank[i % 4][:, :]).then_inc(turn_copied, 1)

            @block.tensor
            def _(pe):
                norm.pe(pe)
                pe.wait_ge(norm.h_ready, KD)

                def project(n):
                    name, _, cols = MIX_ORDER[n]
                    place = K.next_slab(pe) if n < 2 else split.next_slab(pe)
                    if n >= 4:
                        pe.wait_ge(z_ready, n - 3)
                    parts = (norm.parts.hi, norm.parts.lo)
                    if n == 2:
                        pe.wait_ge(norm.parts.lo_ready, 4)
                    if name.endswith("_v"):
                        last = token_major3(pe, K.bank[n % 4], split.view(place), parts, KD, HALF)
                    elif n >= 2:
                        last = feature_major3(pe, K.bank[n % 4], split.view(place), parts, KD, HALF)
                    else:
                        last = feature_major(K, pe, K.bank[n % 4], view(place, cols=cols), K.h, KD, cols)
                    if name == "wa":
                        last = feature_major(K, pe, K.bank[n % 4], view(place, cols=4, start=KD * 128), K.h, KD, 4, at=T)
                    K.slab_done(last)
                for n in range(11):
                    project(n)
                pe.wait_ge(lora_in, 64)
                pe.wait_ge(ranks_ready, 1)
                for half, banks in ((slice(0, 64), 4), (slice(64, 128), 6)):
                    for t in range(4):
                        last = pe.matmul(K.bank[banks + t // 2][:, (t % 2) * T:(t % 2 + 1) * T],
                                         w2a2[half, t * P:(t + 1) * P], zs[half, 0, 1:], start=True, stop=True)
                last.then_inc(lora_ready, 1)
                for n in range(11, 14):
                    project(n)
                pe.wait_ge(lora_read, 1)
                for t in range(4):
                    o = K.bank[4 + t // 2][:, (t % 2) * T:(t % 2 + 1) * T]
                    pe.matmul(o, g2[:, 0, t * P:(t + 1) * P], zs[:, 1, 1:], start=True, stop=False)
                    last = pe.matmul(o, g2[0:32, 1, t * P:(t + 1) * P], zs[0:32, 2, 1:], start=False, stop=True)
                last.then_inc(lora_ready, 1)
                pe.wait_ge(kk_squared, 1)
                for i in range(2):
                    last = pe.matmul(K.bank[6 + i][:, :], K.c("headsum"),
                                     sq[:, 2 * i:2 * i + 2, :].rearrange("p a t -> p (a t)"), start=True, stop=True)
                last.then_inc(kk_summed, 1)
                pe.wait_ge(lora_read, 2)
                pe.wait_ge(bonus_in, 1)
                for i in range(2):
                    last = pe.matmul(K.bank[4 + i][:, :], K.c("headsum"),
                                     dd[:, 2 * i:2 * i + 2, :].rearrange("p a t -> p (a t)"), start=True, stop=True)
                last.then_inc(bonus_summed, 1)
                pe.wait_ge(z_ready, 14)
                for i in range(6):
                    if i >= 4:
                        pe.wait_ge(turn_copied, i - 3)
                    pe.wait_ge(turn_in, i // 2)
                    for t in range(4):
                        tok = slice((i % 2) * P, (i % 2 + 1) * P)
                        src = (z[:, 8 + t, 1:][:, tok], s["kt"][:, t, tok], s["bt"][:, t, tok])[i // 2]
                        last = pe.transpose(K.bank[i % 4][:, t * P:(t + 1) * P], src, K.c("ident"))
                    last.then_inc(turned, 1)

            @block.vector
            def _(dve):
                own = K.dve_own
                dve.memset(z[:, :, 0:1], 0.0)
                own.after(dve, dve.memset(zs[:, :, 0:1], 0.0))
                norm.dve(dve)
                for n in range(8):
                    dve.wait_ge(z_ready, n + 1)
                    if n:
                        dve.wait_ge(mixed, n)
                    name = MIX_ORDER[n][0]
                    if name in ("wa", "g"):
                        tiles = [(zs, 0, P, K.col("mu_wa"))] if name == "wa" else \
                            [(zs, 1, P, K.col("mu_g")), (zs, 2, 32, K.prm[:, PARAM_ROWS["mu_g"] + 1:PARAM_ROWS["mu_g"] + 2])]
                    else:
                        t0 = {"r": 0, "k": 4, "v": 8}[name] + 2 * (n - {"k": 2, "r": 4, "v": 6}[name])
                        tiles = [(z, t0 + j, P, K.col("mu_rkv", 12)[:, t0 + j:t0 + j + 1]) for j in range(2)]
                    for j, (zz, t, m, mu) in enumerate(tiles):
                        last = dve.tensor_tensor(diff[0:m, j, :], zz[0:m, t, 0:T], zz[0:m, t, 1:T + 1], ALU.subtract)
                    own.after(dve, last)
                    for j, (zz, t, m, mu) in enumerate(tiles):
                        last = dve.scalar_tensor_tensor(zz[0:m, t, 1:], diff[0:m, j, :], mu[0:m, :], zz[0:m, t, 1:],
                                                        ALU.mult, ALU.add)
                    last.then_inc(mixed, 1)
                dve.wait_ge(mixed, 8)
                r, k, v = z[:, 0:4, 1:], z[:, 4:8, 1:], z[:, 8:12, 1:]
                for t in range(4):
                    last = dve.tensor_scalar(kk[:, t, :], k[:, t, :], K.col("k_k", 4)[:, t:t + 1], None, ALU.mult)
                last.then_inc(kk_ready, 1)
                own.after(dve, dve.tensor_scalar(om[:, :], K.col("k_a", 4), -1.0, 1.0, ALU.mult, ALU.add))
                dve.wait_ge(lora_read, 1)
                for t in range(4):
                    last = dve.tensor_scalar(kp[:, t, :], rate[:, t, :], K.col("k_a", 4)[:, t:t + 1], om[:, t:t + 1],
                                             ALU.mult, ALU.add)
                own.after(dve, last)
                own.after(dve, dve.tensor_tensor(kp[:, :, :], kp[:, :, :], k, ALU.mult))
                for t in range(4):
                    last = dve.scalar_tensor_tensor(dd[:, t, :], r[:, t, :], K.col("r_k", 4)[:, t:t + 1], kp[:, t, :],
                                                    ALU.mult, ALU.mult)
                last.then_inc(bonus_in, 1)
                flat = lambda x: x[:, :, :].rearrange("p a t -> p (a t)")
                own.after(dve, dve.tensor_scalar(flat(lw), flat(lw), -DECAY, None, ALU.mult))
                own.after(dve, dve.tensor_tensor_scan(flat(cum), K.c("gate"), flat(lw), 0.0, ALU.mult, ALU.add))
                chunks = lambda x: flat(x).rearrange("p (g c) -> p g c", c=CH)
                mid = chunks(cum)[:, :, CH // 2 - 1:CH // 2]
                c4 = cum[:, :, :].rearrange("p a (g c) -> p a g c", c=CH)
                end4, mid4 = c4[:, :, :, CH - 1], c4[:, :, :, CH // 2 - 1]
                own.after(dve, dve.tensor_tensor(s["es"][:, :, 0:3], end4[:, :, 0:3], mid4[:, :, 0:3], ALU.subtract))
                own.after(dve, dve.tensor_tensor(s["es"][:, :, 0:3], s["es"][:, :, 0:3], mid4[:, :, 1:4], ALU.add))
                dve.wait_ge(bonus_summed, 1)
                own.after(dve, dve.tensor_tensor(chunks(dd), chunks(cum), mid.to_broadcast([P, 16, CH]), ALU.subtract))
                dve.tensor_tensor(flat(d3), flat(dd), flat(lw), ALU.subtract).then_inc(decay_diff, 1)
                for i in range(2):
                    last = dve.tensor_tensor(s["bv"][:, 2 * i:2 * i + 2, :], bank4(4 + i), v[:, 2 * i:2 * i + 2, :],
                                             ALU.mult)
                dve.wait_ge(kk_norm, 1)
                own.after(dve, dve.tensor_scalar(flat(nrm), flat(nrm), 1e-12, None, ALU.max))
                own.after(dve, dve.reciprocal(flat(nrm), flat(nrm)))
                own.after(dve, dve.tensor_tensor(flat(kk), flat(kk), flat(nrm), ALU.mult))
                own.after(dve, dve.tensor_tensor(flat(rate), flat(rate), flat(kk), ALU.mult))
                dve.wait_ge(decays_ready, 1)
                dve.tensor_tensor(flat(s["kt"]), flat(kp), flat(e2), ALU.mult).then_inc(turn_in, 1)
                dve.tensor_tensor(flat(s["bt"]), flat(rate), flat(e2), ALU.mult).then_inc(turn_in, 1)
                for tt in range(TT):
                    tok = slice(tt * P, (tt + 1) * P)
                    dve.tensor_tensor(s["ar"][:, :, tt, 0, :], kk[:, :, tok], e3[:, :, tok], ALU.mult)
                    dve.tensor_tensor(s["ar"][:, :, tt, 1, :], r[:, :, tok], e1[:, :, tok], ALU.mult)


class Inverse:

    def __init__(self, K, ctx, tag, groups, levels, masks, lt, xt, before, bank=4):
        self.K, self.groups, self.levels, self.masks = K, groups, levels, masks
        self.lt, self.xt, self.before = lt, xt, before
        self.first_bank = lambda s: K.bank[bank + 2 * s]
        self.second_bank = lambda s: K.bank[bank + 1 + 2 * s]
        f = lambda name: [K.sb(f"{name}{i}", [P, 4, P], ctx=ctx) for i in range(2)]
        self.X, self.T1 = f("inv_x"), f("inv_t")
        self.mask = [[K.sb(f"inv_m{s}{j}", [P, 4, P], ctx=ctx) for j in range(2)] for s in range(2)]
        self.m_ready, self.t_ready = K.sem(tag + "_part_ready"), K.sem(tag + "_first_ready")
        self.t_copied, self.uv_ready = K.sem(tag + "_first_copied"), K.sem(tag + "_second_ready")
        self.x_ready = K.sem(tag + "_x_ready")
        self.steps = [(pair * 2 + s, l) for pair in range(groups // 2) for l in range(levels) for s in range(2)]
        self.index = {st: i for i, st in enumerate(self.steps)}
        self.update = {st: i for i, st in enumerate([st for st in self.steps if st[1] > 0])}

    def final(self, g):
        return self.update[(g, self.levels - 1)] + 1

    PAIRS = property(lambda self: len(self.steps) // 2)

    def pool(self, pool):
        K = self.K
        for i, (g, l) in enumerate(self.steps):
            s = g % 2
            m = self.mask[s][l % 2]
            if l == 0:
                self.before(pool, g)
            prev = [j for j in range(i) if self.steps[j][0] % 2 == s and self.steps[j][1] % 2 == l % 2]
            if prev:
                pool.wait_ge(self.t_ready, prev[-1] + 1)
            level = K.c(self.masks, first=l * P, n=P).unsqueeze(1).to_broadcast([P, 4, P])
            ins = pool.tensor_tensor(m[:, :, :], self.lt(g), level, ALU.mult)
            if l == 0:
                K.pool_own.after(pool, ins)
                ident = K.c("ident").unsqueeze(1).to_broadcast([P, 4, P])
                ins = pool.tensor_tensor(self.xt(g), ident, m[:, :, :], ALU.subtract)
            ins.then_inc(self.m_ready, 1)

    def pe(self, pe, between=lambda pair: None):
        K = self.K
        for i0 in range(0, len(self.steps), 2):
            between(i0 // 2)
            for i in (i0, i0 + 1):
                g, l = self.steps[i]
                s = g % 2
                bank = self.first_bank(s)
                pe.wait_ge(self.m_ready, i + 1)
                if l == 0:
                    for q in range(4):
                        last = pe.transpose(bank[:, q * P:(q + 1) * P], self.xt(g)[:, q, :], K.c("ident"))
                else:
                    if l == 1:
                        pe.wait_ge(self.t_copied, self.index[(g, 0)] + 1)
                    else:
                        pe.wait_ge(self.x_ready, self.update[(g, l - 1)] + 1)
                    for q in range(4):
                        last = pe.matmul(bank[:, q * P:(q + 1) * P], self.mask[s][l % 2][:, q, :], self.X[s][:, q, :],
                                         start=True, stop=True)
                last.then_inc(self.t_ready, 1)
            if self.steps[i0][1] == 0:
                continue
            for i in (i0, i0 + 1):
                g, l = self.steps[i]
                s = g % 2
                pe.wait_ge(self.t_copied, i + 1)
                if l == 1 and g >= 2:
                    pe.wait_ge(self.x_ready, self.final(g - 2))
                if l < self.levels - 1:
                    for q in range(4):
                        pe.matmul(self.first_bank(s)[:, q * P:(q + 1) * P], self.xt(g)[:, q, :], self.T1[s][:, q, :],
                                  start=True, stop=True)
                for q in range(4):
                    last = pe.matmul(self.second_bank(s)[:, q * P:(q + 1) * P], self.T1[s][:, q, :], self.xt(g)[:, q, :],
                                     start=True, stop=True)
                last.then_inc(self.uv_ready, 1)

    def act(self, act, between=lambda pair: None):
        for i, (g, l) in enumerate(self.steps):
            s = g % 2
            if i % 2 == 0:
                between(i // 2)
            act.wait_ge(self.t_ready, i + 1)
            dst = self.X[s] if l == 0 else self.T1[s]
            act.copy(dst[:, :, :].rearrange("p a t -> p (a t)"), self.first_bank(s)[:, :]).then_inc(self.t_copied, 1)

    def dve(self, dve, between=lambda pair: None):
        for i, (g, l) in enumerate(self.steps):
            if i % 2 == 0:
                between(i // 2)
            if l == 0:
                continue
            s = g % 2
            dve.wait_ge(self.uv_ready, self.update[(g, l)] + 1)
            if l < self.levels - 1:
                dve.tensor_tensor(self.X[s][:, :, :], self.X[s][:, :, :],
                                  self.first_bank(s)[:, :].rearrange("p (a t) -> p a t", a=4), ALU.subtract)
            dve.tensor_tensor(self.xt(g), self.xt(g), self.second_bank(s)[:, :].rearrange("p (a t) -> p a t", a=4),
                              ALU.subtract).then_inc(self.x_ready, 1)


def rwkv_stage(K):
    nc, s = K.nc, K.mx
    with ExitStack() as ctx:
        lt = K.sb("lt", [P, 16, 4, P], ctx=ctx)
        xt = K.sb("xt", [P, 16, P], ctx=ctx)
        unit = lambda t, tt, hh: 4 * t + 2 * tt + hh
        intra_ready, intra_read = K.sem("intra_ready"), K.sem("intra_read")
        with ExitStack() as ictx:
            inv = Inverse(K, ictx, "rinv", 4, 6, "levels", lambda g: lt[:, 4 * g:4 * g + 4, 0, :],
                          lambda g: xt[:, 4 * g:4 * g + 4, :], lambda eng, g: eng.wait_ge(intra_read, 4 * g + 4))
            with nc.Block(no_gpsimd_drain=True) as block:
                @block.tensor
                def _(pe):
                    for t in range(4):
                        for tt in range(TT):
                            for hh in range(2):
                                u = unit(t, tt, hh)
                                if u >= 2:
                                    pe.wait_ge(intra_read, u - 1)
                                half = slice(64 * hh, 64 * hh + 64)
                                rhs = s["ar"][half, t, tt, :, :].rearrange("p a t -> p (a t)")
                                for j, n in enumerate(("bt", "kt")):
                                    last = pe.matmul(K.bank[hh][:, j * T:(j + 1) * T],
                                                     s[n][half, t, tt * P:(tt + 1) * P], rhs, start=True, stop=True)
                                last.then_inc(intra_ready, 1)
                    inv.pe(pe)

                @block.vector
                def _(dve):
                    for u in range(16):
                        dve.wait_ge(intra_ready, u + 1)
                        dve.tensor_tensor(lt[:, u, :, :].rearrange("p (a b) t -> p a (b t)", a=2),
                                          K.bank[u % 2][:, :].rearrange("p (a t) -> p a t", a=2),
                                          K.c("chunkmask").unsqueeze(1).to_broadcast([P, 2, T]), ALU.mult).then_inc(intra_read, 1)
                    inv.dve(dve)

                @block.scalar
                def _(act):
                    inv.act(act)

                @block.gpsimd
                def _(pool):
                    inv.pool(pool)
        attention_stage(K, lt, xt, unit)


class RwkvScan:

    STEPS = 12
    MEAN, CENTRE, SQUARE, VARIANCE, ROOT, GATE = 13, 13, 14, 15, 15, 16
    WORK, OUT = 4, 5

    def __init__(self, K, ctx, lt, xt, unit, sq):
        self.K, self.lt, self.xt, self.unit, self.sq = K, lt, xt, unit, sq
        self.state = K.sb("state", [P, 4, P], ctx=ctx)
        self.tmp = K.sb("state_next", [P, 4, P], ctx=ctx)
        self.rhs = K.sb("rhs", [P, 512], ctx=ctx)
        self.sa = K.sb("sa", [P, TT, 512], ctx=ctx)
        self.y = K.sb("ysb", [P, 4, T], ctx=ctx)
        self.s_ready, self.rhs_ready, self.rhs_copied = K.sem("s_ready"), K.sem("rhs_ready"), K.sem("rhs_copied")
        self.sa_ready, self.sa_copied, self.st_ready = K.sem("sa_ready"), K.sem("sa_copied"), K.sem("st_ready")
        self.y_ready, self.y_copied, self.mean_ready = K.sem("y_ready"), K.sem("y_copied"), K.sem("mean_ready")
        self.centred, self.squared = K.sem("centred"), K.sem("y_squared")
        self.var_ready, self.rstd_ready = K.sem("var_ready"), K.sem("y_rstd")

    def pe(self, pe, step):
        if step == self.MEAN:
            self.pe_mean(pe)
        if step == self.VARIANCE:
            self.pe_variance(pe)
        if step >= self.STEPS:
            return
        K, s, unit = self.K, self.K.mx, self.unit
        c, part = divmod(step, 3)
        tt, p = divmod(c, 2)
        work, Y = K.bank[self.WORK], K.bank[self.OUT]
        rows, tok = slice(64 * p, 64 * p + 64), slice(64 * p, 64 * p + 64)
        head = lambda t, hh: slice(t * P + 64 * hh, t * P + 64 * hh + 64)
        heads = [(t, hh) for t in range(4) for hh in range(2)]
        if part == 0:
            if p == 0:
                if tt:
                    pe.wait_ge(self.y_copied, tt)
                for t, hh in heads:
                    pe.matmul(Y[64 * hh:64 * hh + 64, t * P:(t + 1) * P], s["vtok_r"][:, tt, head(t, hh)],
                              self.lt[:, unit(t, tt, hh), 3, :], start=(t == 0), stop=False, skip_group_check=True)
            pe.wait_ge(self.s_ready, c + 1)
            for t in range(4):
                pe.matmul(work[rows, t * P:(t + 1) * P], s["ar"][:, t, tt, 0, tok], self.state[:, t, :],
                          start=True, stop=False)
                for hh in range(2):
                    last = pe.matmul(work[rows, head(t, hh)], self.lt[rows, unit(t, tt, hh), 2, tok],
                                     s["vtok_r"][rows, tt, head(t, hh)], start=False, stop=(hh == 1))
            last.then_inc(self.rhs_ready, 1)
            for t in range(4):
                pe.matmul(Y[:, t * P + 64 * p:t * P + 64 * p + 64], self.state[:, t, :], s["ar"][:, t, tt, 1, tok],
                          start=False, stop=False, skip_group_check=True)
        elif part == 1:
            pe.wait_ge(self.rhs_copied, c + 1)
            for t, hh in heads:
                last = pe.matmul(work[rows, head(t, hh)], self.xt[rows, unit(t, tt, hh), tok],
                                 self.rhs[rows, head(t, hh)], start=True, stop=True)
            last.then_inc(self.sa_ready, 1)
        else:
            pe.wait_ge(self.sa_copied, c + 1)
            if c < 3:
                for t in range(4):
                    col = slice(t * P, (t + 1) * P)
                    pe.matmul(work[:, col], s["ktok"][rows, tt, col], s["vtok_r"][rows, tt, col], start=True, stop=False)
                    last = pe.matmul(work[:, col], s["btok"][rows, tt, col], self.sa[rows, tt, col],
                                     start=False, stop=True)
                last.then_inc(self.st_ready, 1)
            if p == 1:
                for t, hh in heads:
                    last = pe.matmul(Y[64 * hh:64 * hh + 64, t * P:(t + 1) * P], self.sa[:, tt, head(t, hh)],
                                     self.lt[:, unit(t, tt, hh), 1, :], start=False, stop=True, skip_group_check=True)
                last.then_inc(self.y_ready, 1)

    def dve(self, dve, step):
        if step == self.CENTRE:
            self.dve_centre(dve)
        if step >= self.GATE:
            self.dve_gate(dve, step - self.GATE)
        if step >= self.STEPS:
            return
        K, s = self.K, self.K.mx
        c, part = divmod(step, 3)
        tt, p = divmod(c, 2)
        rows, work = slice(64 * p, 64 * p + 64), K.bank[self.WORK]
        flat = lambda x: x[:, :, :].rearrange("p a t -> p (a t)")
        if part == 0:
            if c == 0:
                dve.memset(self.state[:, :, :], 0.0).then_inc(self.s_ready, 1)
            dve.wait_ge(self.rhs_ready, c + 1)
            dve.tensor_scalar(self.rhs[rows, :], work[rows, :], -1.0, None, ALU.mult).then_inc(self.rhs_copied, 1)
        elif part == 1:
            dve.wait_ge(self.sa_ready, c + 1)
            dve.tensor_copy(self.sa[rows, tt, :], work[rows, :]).then_inc(self.sa_copied, 1)
        elif c < 3:
            dve.wait_ge(self.st_ready, c + 1)
            K.dve_own.after(dve, dve.tensor_tensor(flat(self.tmp), work[:, :], flat(self.state), ALU.add))
            for t in range(4):
                last = dve.scalar_tensor_tensor(self.state[:, t, :], self.tmp[:, t, :], s["es"][:, t, c:c + 1],
                                                K.c("headsum"), ALU.mult, ALU.mult)
            last.then_inc(self.s_ready, 1)

    def act(self, act, step):
        if step in (5, 11):
            tt = step // 6
            act.wait_ge(self.y_ready, tt + 1)
            act.copy(self.y[:, :, tt * P:(tt + 1) * P], self.K.bank[self.OUT][:, :].rearrange("p (a t) -> p a t", a=4))\
                .then_inc(self.y_copied, 1)
        if step == self.SQUARE:
            act.wait_ge(self.centred, 1)
            act.activation(self.sq.rearrange("p a t -> p (a t)"), self.y[:, :, :].rearrange("p a t -> p (a t)"),
                           ACT.Square).then_inc(self.squared, 1)
        if step == self.ROOT:
            self.act_root(act)

    def pe_mean(self, pe):
        K = self.K
        flat = lambda x: x[:, :, :].rearrange("p a t -> p (a t)")
        pe.wait_ge(self.y_copied, 2)
        for i in range(2):
            last = pe.matmul(K.bank[4 + i][:, :], K.c("headsum"), flat(self.y)[:, i * 512:(i + 1) * 512], start=True, stop=True)
        last.then_inc(self.mean_ready, 1)

    def pe_variance(self, pe):
        K = self.K
        flat = lambda x: x[:, :, :].rearrange("p a t -> p (a t)")
        pe.wait_ge(self.squared, 1)
        for i in range(2):
            last = pe.matmul(K.bank[4 + i][:, :], K.c("headsum"), flat(self.sq)[:, i * 512:(i + 1) * 512],
                             start=True, stop=True)
        last.then_inc(self.var_ready, 1)

    def dve_centre(self, dve):
        K, y = self.K, self.y
        flat = lambda x: x[:, :, :].rearrange("p a t -> p (a t)")
        dve.wait_ge(self.mean_ready, 1)
        for i in range(2):
            last = dve.scalar_tensor_tensor(flat(y)[:, i * 512:(i + 1) * 512], K.bank[4 + i][:, :], -1.0 / 64,
                                            flat(y)[:, i * 512:(i + 1) * 512], ALU.mult, ALU.add)
        last.then_inc(self.centred, 1)

    def dve_gate(self, dve, part):
        K, s, y = self.K, self.K.mx, self.y
        own = K.dve_own
        flat = lambda x: x[:, :, :].rearrange("p a t -> p (a t)")
        if part == 0:
            dve.wait_ge(self.rstd_ready, 1)
            own.after(dve, dve.tensor_tensor(flat(y), flat(y), flat(self.sq), ALU.mult))
        elif part == 1:
            for t in range(4):
                last = dve.tensor_scalar(y[:, t, :], y[:, t, :], K.col("ln_w", 4)[:, t:t + 1],
                                         K.col("ln_b", 4)[:, t:t + 1], ALU.mult, ALU.add)
            own.after(dve, last)
        elif part == 2:
            own.after(dve, dve.tensor_tensor(flat(y), flat(y), flat(s["bv"]), ALU.add))
        elif part == 3:
            dve.tensor_tensor(s["y"][:, 2:6, :], y[:, :, :], s["g"][:, :, :], ALU.mult)

    def act_root(self, act):
        K = self.K
        flat = lambda x: x[:, :, :].rearrange("p a t -> p (a t)")
        act.wait_ge(self.var_ready, 1)
        for i in range(2):
            last = act.activation(self.sq[:, 2 * i:2 * i + 2, :], K.bank[4 + i][:, :].rearrange("p (a t) -> p a t", a=2),
                                  ACT.Ln, bias=K.c("gneps"), scale=1.0 / 64)
        K.act_own.after(act, last)
        act.activation(flat(self.sq), flat(self.sq), ACT.Exp, scale=-0.5).then_inc(self.rstd_ready, 1)



class Modulations:

    AT_A_CALL = 2
    BANKS = (6, 7)

    def __init__(self, K, ctx):
        self.K, self.n0, self.k, self.n, self.copies = K, K.eaten, 0, 0, 0
        self.rows = K.sb("mod_rows", [2, MOD_SLABS * HALF], ctx=ctx)
        self.copied, self.turned, self.kept = K.sem("mod_copied"), K.sem("mod_turned"), K.sem("mod_kept")

    def some(self, pe):
        K = self.K
        for _ in range(self.AT_A_CALL):
            if self.n == MOD_SLABS:
                return
            if self.k == 0:
                self.w = view(K.next_slab(pe))
                if self.n >= 2:
                    pe.wait_ge(self.copied, self.n - 1)
            last = pe.matmul(K.bank[self.BANKS[self.n % 2]][0:2, 0:HALF], K.cs[:, self.k, :], self.w[:, self.k, :],
                             start=(self.k == 0), stop=(self.k == KD - 1))
            self.k += 1
            if self.k == KD:
                K.slab_done(last)
                self.k, self.n = 0, self.n + 1

    def act(self, act, step, calls):
        K = self.K
        while self.copies < min(MOD_SLABS, step * calls * self.AT_A_CALL // KD):
            n = self.copies
            K.wait_slabs(act, self.n0 + n + 1)
            act.copy(self.rows[:, n * HALF:(n + 1) * HALF], K.bank[self.BANKS[n % 2]][0:2, 0:HALF]).then_inc(self.copied, 1)
            self.copies = n + 1

    def pe_end(self, pe):
        K = self.K
        while self.n < MOD_SLABS:
            self.some(pe)
        pe.wait_ge(self.copied, MOD_SLABS)
        for t in range(2 * MOD_SLABS):
            last = pe.transpose(K.bank[6][:, 2 * t:2 * t + 2], self.rows[:, t * P:(t + 1) * P], K.c("ident", slice(0, 2), n=2))
        last.then_inc(self.turned, 1)

    def dve(self, dve):
        K, m = self.K, 2 * MOD_SLABS
        dve.tensor_copy(K.mod[:, 0:m, :], K.mod[:, m:2 * m, :]).then_inc(self.kept, 1)
        dve.wait_ge(self.turned, 1)
        dve.wait_ge(self.kept, 1)
        dve.tensor_copy(K.mod[:, m:2 * m, :], K.bank[6][:, 0:2 * m].rearrange("p (t c) -> p t c", c=2))



class Attention:

    def __init__(self, K, ctx, tag, units, banks, keys, buffers=None):
        self.K, self.units = K, units
        self.score_banks, self.turn_banks, self.out_banks = banks
        two = lambda name, n: [K.sb(f"{name}{i}", [P, n], ctx=ctx) for i in range(2)]
        if buffers is None:
            buffers = [two(n, keys) for n in ("at_s", "at_p", "at_n", "at_t")]
        self.scores, self.probs, self.normed, self.turned = buffers
        self.top, self.sum = two("at_max", 2), two("at_sum", 2)
        self.scores_ready = K.sem(f"{tag}_scores_ready")
        self.top_ready = K.sem(f"{tag}_top_ready")
        self.exp_done = K.sem(f"{tag}_exp_done")
        self.probs_ready = K.sem(f"{tag}_probs_ready")
        self.turn_ready = K.sem(f"{tag}_turn_ready")
        self.turn_copied = K.sem(f"{tag}_turn_copied")
        self.out_ready = K.sem(f"{tag}_out_ready")
        self.out_copied = K.sem(f"{tag}_out_copied")

    CALLS = 3

    def pe(self, pe, between=lambda: None, mid_step=lambda i: None):
        U, K = self.units, self.K
        for i in range(len(U) + 2):
            if i < len(U):
                u, bank = U[i], K.bank[self.score_banks[i % 2]]
                if i >= 2:
                    pe.wait_ge(self.top_ready, i - 1)
                n = u["keys"]
                prods = [(u["q"], k, c) for k, c in u["k"]] + [(a, b, slice(0, n)) for a, b in u.get("bias", ())]
                regions = len(u["k"])
                for j, (a, b, c) in enumerate(prods):
                    last = pe.matmul(bank[:, c], a, b, start=(j < regions), stop=(j == len(prods) - 1 or len(prods) == regions))
                last.then_inc(self.scores_ready, 1)
            between()
            mid_step(i)
            j = i - 1
            if 0 <= j < len(U):
                bank = K.bank[self.turn_banks[j % len(self.turn_banks)]]
                pe.wait_ge(self.probs_ready, j + 1)
                if j >= len(self.turn_banks):
                    pe.wait_ge(self.turn_copied, j - len(self.turn_banks) + 1)
                for c in range(U[j]["keys"] // P):
                    last = pe.transpose(bank[:, c * P:(c + 1) * P], self.normed[j % 2][:, c * P:(c + 1) * P], K.c("ident"))
                last.then_inc(self.turn_ready, 1)
            between()
            m = i - 2
            if m >= 0:
                u, bank = U[m], K.bank[self.out_banks[m % len(self.out_banks)]]
                pe.wait_ge(self.turn_copied, m + 1)
                if m >= len(self.out_banks):
                    pe.wait_ge(self.out_copied, m - len(self.out_banks) + 1)
                rows = u["rows"]
                nk = u["keys"] // P
                for c in range(nk):
                    last = pe.matmul(bank[rows, 0:P], u["v"][c], self.turned[m % 2][:, c * P:(c + 1) * P],
                                     start=(c == 0), stop=(c == nk - 1))
                last.then_inc(self.out_ready, 1)
            between()

    def dve(self, dve, at_step=lambda i: None):
        U, K = self.units, self.K
        for i in range(len(U) + 1):
            at_step(i)
            if i < len(U):
                n = U[i]["keys"]
                s, top = self.scores[i % 2][:, 0:n], self.top[i % 2]
                dve.wait_ge(self.scores_ready, i + 1)
                if i >= 2:
                    dve.wait_ge(self.exp_done, i - 1)
                K.dve_own.after(dve, dve.tensor_tensor_reduce(
                    out=s, in0=K.bank[self.score_banks[i % 2]][:, 0:n], in1=U[i]["mask"], scale=1.0, scalar=-3.0e38,
                    op0=ALU.add, op1=ALU.max, accum_out=top[:, 0:1]))
                dve.tensor_scalar(top[:, 1:2], top[:, 0:1], -1.0, None, ALU.mult).then_inc(self.top_ready, 1)
            j = i - 1
            if j >= 0:
                n = U[j]["keys"]
                dve.wait_ge(self.exp_done, j + 1)
                K.dve_own.after(dve, dve.reciprocal(self.sum[j % 2][:, 1:2], self.sum[j % 2][:, 0:1]))
                if j >= 2:
                    dve.wait_ge(self.turn_ready, j - 1)
                dve.tensor_scalar(self.normed[j % 2][:, 0:n], self.probs[j % 2][:, 0:n], self.sum[j % 2][:, 1:2],
                                  None, ALU.mult).then_inc(self.probs_ready, 1)

    def act(self, act, at_step=lambda i: None):
        U, K = self.units, self.K
        for i in range(len(U) + 2):
            at_step(i)
            if i < len(U):
                n = U[i]["keys"]
                act.wait_ge(self.top_ready, i + 1)
                if i >= 2:
                    act.wait_ge(self.probs_ready, i - 1)
                act.activation(self.probs[i % 2][:, 0:n], self.scores[i % 2][:, 0:n], ACT.Exp,
                               bias=self.top[i % 2][:, 1:2], accum_out=self.sum[i % 2][:, 0:1]).then_inc(self.exp_done, 1)
            j = i - 1
            if 0 <= j < len(U):
                n = U[j]["keys"]
                act.wait_ge(self.turn_ready, j + 1)
                if j >= 2:
                    act.wait_ge(self.out_ready, j - 1)
                act.copy(self.turned[j % 2][:, 0:n], K.bank[self.turn_banks[j % len(self.turn_banks)]][:, 0:n]).then_inc(self.turn_copied, 1)
            m = i - 2
            if m >= 0:
                act.wait_ge(self.out_ready, m + 1)
                act.copy(U[m]["out"], K.bank[self.out_banks[m % len(self.out_banks)]][U[m]["rows"], 0:P]).then_inc(self.out_copied, 1)


LOG1P = [1.0 / (2 * k + 1) for k in range(9)]


def softplus_small(dve, own, e, s, s2, q, out):
    own.after(dve, dve.tensor_scalar(s2, e, 2.0, None, ALU.add))
    own.after(dve, dve.reciprocal(s2, s2))
    own.after(dve, dve.tensor_tensor(s, e, s2, ALU.mult))
    own.after(dve, dve.tensor_tensor(s2, s, s, ALU.mult))
    own.after(dve, dve.tensor_scalar(q, s2, LOG1P[8], None, ALU.mult))
    for c in LOG1P[7:0:-1]:
        own.after(dve, dve.scalar_tensor_tensor(q, q, c, s2, ALU.add, ALU.mult))
    own.after(dve, dve.scalar_tensor_tensor(q, q, 1.0, s, ALU.add, ALU.mult))
    return dve.tensor_scalar(out, q, 2.0, None, ALU.mult)


def attention_stage(K, lt, xt, unit):
    nc, s = K.nc, K.mx
    qk, v, f, y = s["qk"], s["v"], s["f"], s["y"]
    with ExitStack() as ctx:
        sq = K.sb("qksq", [P, 8, T], ctx=ctx)
        gains = K.sb("gains", [P, 2], ctx=ctx)
        rot = K.sb("rotd", [P, 2, T], ctx=ctx)
        fx, fs, fs2, fq, fc, fneg, fe = (K.sb(n, [4, T], ctx=ctx) for n in ("fx", "fs", "fs2", "fq", "fc", "fneg", "fe"))
        squared, summed, rstd_ready = K.sem("qk_squared"), K.sem("qk_summed"), K.sem("qk_rstd")
        normed, rotated, roped = K.sem("qk_normed"), K.sem("qk_rotated"), K.sem("qk_roped")
        fabs_ready, fexp_ready, fsum_ready = K.sem("f_abs"), K.sem("f_exp"), K.sem("f_sum")
        units = []
        for kind in range(2):
            for h in range(4):
                rows = slice(64 * (h % 2), 64 * (h % 2) + 64)
                for i in range(TT):
                    n = P * (i + 1)
                    u = {"keys": n, "rows": rows,
                         "q": qk[rows, 4 * kind + h // 2, i * P:(i + 1) * P],
                         "k": [(qk[rows, 4 * kind + 2 + h // 2, 0:n], slice(0, n))],
                         "mask": K.c("causal")[:, P - i * P:2 * P],
                         "v": [v[:, c, 256 * kind + 64 * h:256 * kind + 64 * h + 64] for c in range(i + 1)],
                         "out": y[rows, 6 * kind + h // 2, i * P:(i + 1) * P]}
                    if kind == 0:
                        one = K.c("ident", slice(0, 4), first=h, n=1)
                        u["bias"] = [(fc[:, i * P:(i + 1) * P], one.to_broadcast([4, n])),
                                     (one.to_broadcast([4, P]), fneg[:, 0:n])]
                    units.append(u)
        att = Attention(K, ctx, "mix_at", units, ((0, 1), (2,), (3,)), T)
        scan = RwkvScan(K, ctx, lt, xt, unit, sq[:, 0:4, :])
        mod = Modulations(K, ctx)
        n0 = K.eaten
        EARLY = 4
        with nc.Block(no_gpsimd_drain=True) as block:
            @block.sync
            def _(sync):
                K.load_slabs(sync, n0 + MOD_SLABS + RING)

            @block.tensor
            def _(pe):
                scan.pe(pe, 0)
                for i in range(4):
                    pe.wait_ge(squared, i + 1)
                    pe.matmul(K.bank[i][:, :], K.c("headsum"), sq[:, 2 * i:2 * i + 2, :].rearrange("p a t -> p (a t)"),
                              start=True, stop=True).then_inc(summed, 1)
                scan.pe(pe, 1)
                for i in range(2):
                    pe.wait_ge(normed, 8)
                    pe.matmul(K.bank[6 + i][:, :], K.c("rot"),
                              qk[:, 4 + 2 * i:6 + 2 * i, :].rearrange("p a t -> p (a t)"), start=True, stop=True)\
                        .then_inc(rotated, 1)
                    scan.pe(pe, 2 + i)
                pe.wait_ge(fsum_ready, 1)
                pe.wait_ge(roped, 2)
                att.pe(pe, between=lambda: mod.some(pe), mid_step=lambda i: scan.pe(pe, i + EARLY))
                mod.pe_end(pe)

            @block.scalar
            def _(act):
                for i in range(4):
                    act.activation(sq[:, 2 * i:2 * i + 2, :], qk[:, 2 * i:2 * i + 2, :], ACT.Square).then_inc(squared, 1)
                act.wait_ge(fabs_ready, 1)
                act.activation(fe[:, :], fe[:, :], ACT.Exp).then_inc(fexp_ready, 1)
                for i in range(4):
                    act.wait_ge(summed, i + 1)
                    last = act.activation(sq[:, 2 * i:2 * i + 2, :], K.bank[i][:, :].rearrange("p (a t) -> p a t", a=2),
                                          ACT.Ln, bias=K.c("eps"), scale=1.0 / 64)
                K.act_own.after(act, last)
                act.activation(sq[:, :, :], sq[:, :, :], ACT.Exp, scale=-0.5).then_inc(rstd_ready, 1)
                att.act(act, at_step=lambda i: (mod.act(act, i, att.CALLS), scan.act(act, i + EARLY - 1)))
                mod.act(act, KD * MOD_SLABS, 1)

            @block.vector
            def _(dve):
                own = K.dve_own
                dve.tensor_scalar(gains[:, 0:1], K.col("fox_q"), 0.125, None, ALU.mult)
                own.after(dve, dve.tensor_scalar(gains[:, 1:2], K.col("moba_q"), 0.125, None, ALU.mult))
                own.after(dve, dve.tensor_scalar(fx[:, :], f[:, :], K.col("f_bias")[0:4, :], None, ALU.add))
                dve.scalar_tensor_tensor(fe[:, :], fx[:, :], -1.0, fx[:, :], ALU.mult, ALU.min).then_inc(fabs_ready, 1)
                scan.dve(dve, 0)
                dve.wait_ge(fexp_ready, 1)
                own.after(dve, softplus_small(dve, own, fe[:, :], fs[:, :], fs2[:, :], fq[:, :], fs[:, :]))
                own.after(dve, dve.scalar_tensor_tensor(fx[:, :], fx[:, :], 0.0, fs[:, :], ALU.min, ALU.subtract))
                own.after(dve, dve.tensor_tensor_scan(fc[:, :], fx[:, :], K.c("nomask")[0:4, 0:T], 0.0, ALU.add, ALU.add))
                dve.tensor_scalar(fneg[:, :], fc[:, :], -1.0, None, ALU.mult).then_inc(fsum_ready, 1)
                scan.dve(dve, 1)
                dve.wait_ge(rstd_ready, 1)
                for t in range(8):
                    gain = (gains[:, 0:1], K.col("fox_k"), gains[:, 1:2], K.col("moba_k"))[t // 2]
                    dve.scalar_tensor_tensor(qk[:, t, :], qk[:, t, :], gain, sq[:, t, :], ALU.mult, ALU.mult)\
                        .then_inc(normed, 1)
                cos = K.cos[:, :].unsqueeze(1).to_broadcast([P, 2, T])
                sin = K.sin[:, :].unsqueeze(1).to_broadcast([P, 2, T])
                scan.dve(dve, 2)
                for i in range(2):
                    t = slice(4 + 2 * i, 6 + 2 * i)
                    dve.wait_ge(rotated, i + 1)
                    if i:
                        dve.wait_ge(roped, i)
                    own.after(dve, dve.tensor_tensor(rot[:, :, :], K.bank[6 + i][:, :].rearrange("p (a t) -> p a t", a=2),
                                                     sin, ALU.mult))
                    own.after(dve, dve.tensor_tensor(qk[:, t, :], qk[:, t, :], cos, ALU.mult))
                    dve.tensor_tensor(qk[:, t, :], qk[:, t, :], rot[:, :, :], ALU.add).then_inc(roped, 1)
                att.dve(dve, at_step=lambda i: scan.dve(dve, i + EARLY - 1))
                mod.dve(dve)


def mix_out_stage(K):
    nc, y = K.nc, K.mx["y"]
    n0 = K.eaten
    x_updated = K.sem("mix_x_updated")
    with ExitStack() as ctx:
        parts = Parts(K, ctx, "mix_y", KD)
        split = Split(K, ctx, "mix", n0, 4)
        with nc.Block(no_gpsimd_drain=True) as block:
            @block.sync
            def _(sync):
                K.load_slabs(sync, n0 + 4 + RING)

            @block.gpsimd
            def _(pool):
                split.pool(pool)

            @block.scalar
            def _(act):
                split.act(act, 1)
                for i in range(4):
                    parts.act(act, pair_of(i), y[:, pair_of(i), :])
                split.act(act, 4)

            @block.tensor
            def _(pe):
                for i in range(4):
                    w = split.next_view(pe)
                    K.slab_done(feature_major3(pe, K.bank[i], w, (parts.hi, parts.lo), KD, HALF,
                                               first=(lambda k: pe.wait_ge(parts.lo_ready, k // 2 + 1)) if i == 0 else None))

            @block.vector
            def _(dve):
                for i in range(4):
                    parts.dve(dve, pair_of(i), y[:, pair_of(i), :])
                for i in range(4):
                    K.wait_slabs(dve, n0 + i + 1)
                    dve.tensor_tensor(K.x[:, 2 * i:2 * i + 2, :], K.bank[i][:, :].rearrange("p (a t) -> p a t", a=2),
                                      K.x[:, 2 * i:2 * i + 2, :], ALU.add).then_inc(x_updated, 1)


def xattn_slabs(K, l):
    w = lambda n: K.a[n][bass.ds(l, 1), :, :]
    slabs = [whole(w("xattn_w_kv"), i * HALF) for i in range(4)]
    slabs += [whole(w("xattn_w_q"), i * HALF) for i in range(2)]
    slabs += [[(groups_of(w("xattn_w_out"), 0, 4, i * 512, 512), P, 0, 4, 512)] for i in range(2)]
    return slabs


def xattn_stage(K, l):
    nc = K.nc
    n0 = K.eaten
    with ExitStack() as ctx:
        hm = K.sb("hm", [P, KD, T], ctx=ctx)
        qk = K.sb("xqk", [P, 8, T], ctx=ctx)
        v = K.sb("xv", [P, TT, 512], ctx=ctx)
        o = K.sb("xo", [P, 4, T], ctx=ctx)
        sq = K.sb("xsq", [P, 8, T], ctx=ctx)
        gain = K.sb("xgain", [P, 1], ctx=ctx)
        norm = Norm(K, ctx, "xat", K.x, K.h, K.col("xattn_norm", KD), K.bank[6],
                    parts=Parts(K, ctx, "xh", KD))
        m_parts, o_parts = Parts(K, ctx, "xm", KD), Parts(K, ctx, "xo", 4)
        split = Split(K, ctx, "xat", n0, 8)
        mem_ready, z_ready, squared = K.sem("mem_ready"), K.sem("xz_ready"), K.sem("xqk_squared")
        summed, rstd_ready, normed = K.sem("xqk_summed"), K.sem("xqk_rstd"), K.sem("xqk_normed")
        x_updated = K.sem("xat_x_updated")
        units = []
        for h in range(4):
            for i in range(TT):
                units.append({"keys": T, "rows": slice(0, P), "q": qk[:, 4 + h, i * P:(i + 1) * P],
                              "k": [(qk[:, h, :], slice(0, T))], "mask": K.c("nomask")[:, 0:T],
                              "v": [v[:, c, h * P:(h + 1) * P] for c in range(TT)],
                              "out": o[:, h, i * P:(i + 1) * P]})
        att = Attention(K, ctx, "xat", units, ((0, 1), (2, 3), (4, 5)), T)
        with nc.Block(no_gpsimd_drain=True) as block:
            @block.sync
            def _(sync):
                K.load_slabs(sync, n0 + 8 + RING)

            @block.gpsimd
            def _(pool):
                split.pool(pool)

            @block.tensor
            def _(pe):
                norm.pe(pe)
                m, h = ((p.hi, p.lo) for p in (m_parts, norm.parts))
                for n in range(6):
                    w = split.next_view(pe)
                    if n == 4:
                        pe.wait_ge(norm.parts.lo_ready, 4)
                    if n >= 4:
                        pe.wait_ge(z_ready, n - 3)
                    if n in (2, 3):
                        last = token_major3(pe, K.bank[n % 4], w, m, KD, HALF)
                    else:
                        last = feature_major3(pe, K.bank[n % 4], w, m if n < 4 else h, KD, HALF,
                                              first=(lambda k: pe.wait_ge(m_parts.lo_ready, k // 2 + 1)) if n == 0 else None)
                    K.slab_done(last)
                for i in range(4):
                    pe.wait_ge(squared, i + 1)
                    if i == 2:
                        pe.wait_ge(z_ready, 6)
                    bank = K.bank[(4, 5, 2, 3)[i]]
                    pe.matmul(bank[:, :], K.c("ones"), sq[:, 2 * i:2 * i + 2, :].rearrange("p a t -> p (a t)"),
                              start=True, stop=True).then_inc(summed, 1)
                pe.wait_ge(normed, 8)
                att.pe(pe)
                pe.wait_ge(att.out_copied, 8)
                pe.wait_ge(o_parts.lo_ready, 4)
                for i in range(2):
                    w = split.next_view(pe, groups=4, cols=512)
                    for j in range(4):
                        bank = K.bank[2 * i + j // 2]
                        for k in range(4):
                            last = product3(pe, bank[:, (j % 2) * T:(j % 2 + 1) * T], [p[:, k, j * P:(j + 1) * P] for p in w],
                                            (o_parts.hi[:, k, :], o_parts.lo[:, k, :]), k == 0, k == 3)
                    K.slab_done(last)

            @block.scalar
            def _(act):
                for i in range(4):
                    act.wait_ge(mem_ready, 2 * i + 2)
                    m_parts.act(act, pair_of(i), hm[:, pair_of(i), :])
                norm.act(act, between=lambda: split.act(act, 3))
                for n in range(6):
                    split.act(act, n + 3)
                    K.wait_slabs(act, n0 + n + 1)
                    bank = K.bank[n % 4][:, :].rearrange("p (a t) -> p a t", a=2)
                    if n in (2, 3):
                        act.copy(v[:, :, (n - 2) * HALF:(n - 1) * HALF], bank).then_inc(z_ready, 1)
                    else:
                        t = 2 * n if n < 2 else 4 + 2 * (n - 4)
                        act.copy(qk[:, t:t + 2, :], bank).then_inc(z_ready, 1)
                        act.wait_ge(z_ready, n + 1)
                        act.activation(sq[:, t:t + 2, :], qk[:, t:t + 2, :], ACT.Square).then_inc(squared, 1)
                for i in range(4):
                    act.wait_ge(summed, i + 1)
                    last = act.activation(sq[:, 2 * i:2 * i + 2, :],
                                          K.bank[(4, 5, 2, 3)[i]][:, :].rearrange("p (a t) -> p a t", a=2),
                                          ACT.Ln, bias=K.c("eps"), scale=1.0 / P)
                K.act_own.after(act, last)
                act.activation(sq[:, :, :], sq[:, :, :], ACT.Exp, scale=-0.5).then_inc(rstd_ready, 1)
                att.act(act)
                for h in range(4):
                    act.wait_ge(att.out_copied, 2 * h + 2)
                    o_parts.act(act, slice(h, h + 1), o[:, h:h + 1, :])

            @block.vector
            def _(dve):
                own = K.dve_own
                for k in range(KD):
                    dve.tensor_scalar(hm[:, k, :], K.mem[:, k, :], K.col("xattn_mem_norm", KD)[:, k:k + 1], None, ALU.mult)\
                        .then_inc(mem_ready, 1)
                for i in range(4):
                    m_parts.dve(dve, pair_of(i), hm[:, pair_of(i), :])
                norm.dve(dve)
                own.after(dve, dve.tensor_scalar(gain[:, :], K.col("xq"), float(P) ** -0.5, None, ALU.mult))
                dve.wait_ge(rstd_ready, 1)
                for t in range(8):
                    g = K.col("xk") if t < 4 else gain[:, :]
                    dve.scalar_tensor_tensor(qk[:, t, :], qk[:, t, :], g, sq[:, t, :], ALU.mult, ALU.mult)\
                        .then_inc(normed, 1)
                att.dve(dve)
                for h in range(4):
                    dve.wait_ge(att.out_copied, 2 * h + 2)
                    o_parts.dve(dve, slice(h, h + 1), o[:, h:h + 1, :])
                for i in range(4):
                    if i % 2 == 0:
                        K.wait_slabs(dve, n0 + 7 + i // 2)
                    dve.tensor_tensor(K.x[:, 2 * i:2 * i + 2, :], K.bank[i][:, :].rearrange("p (a t) -> p a t", a=2),
                                      K.x[:, 2 * i:2 * i + 2, :], ALU.add).then_inc(x_updated, 1)



ROWS2 = {}


def _rows2():
    at = 0
    for name, n in (("c", 8), ("c_ctx", 8), ("b_mod", 48), ("q_norm", 1), ("k_norm", 1), ("gdn_norm", 1),
                    ("final", 8), ("a_log", 1), ("dt_bias", 1), ("conv", 72), ("ffn_b", 44), ("ffn_conv", 132)):
        ROWS2[name] = at
        at += n
    return at


N_ROWS2 = _rows2()
TILES2 = -(-N_ROWS2 // P)


def second_slabs(K):
    a = K.a
    w_in = a["w_in_2"]
    slabs = [whole(w_in, 3584, 32)]
    slabs += [whole(w_in, 0), whole(w_in, 256)] + [whole(w_in, CTX_COLS + i * HALF) for i in range(4)]
    slabs += [whole(w_in, 512 + 1024 + i * HALF) for i in range(8)]
    slabs += [whole(w_in, 512 + i * HALF) for i in range(4)]
    slabs += [whole(w_in, CTX_COLS + 1024 + i * HALF) for i in range(12)]
    for name in ("w_pa_2", "w_pd_2", "w_out_2"):
        slabs += [whole(a[name], i * HALF) for i in range(4)]
    slabs += ffn_slabs(a["w_up_2"], a["w_down_2"])
    return slabs


def inputs_stage(K):
    nc, a = K.nc, K.a
    with ExitStack() as ctx:
        ctx_in = K.sb("ctx_in", [P, KD, T], ctx=ctx)
        gains = K.sb("gains2", [P, 2, KD], ctx=ctx)
        start, ctx_pe, ctx_act, ctx_copied = load_feature_major(K, ctx, "ctx", a["ctx_2"][0], ctx_in, (2, 3))
        mod = K.mod
        norm_x = Norm(K, ctx, "hx", K.x, K.h, gains[:, 0, :], K.bank[4], shift=mod[:, 0:KD, 0])
        norm_c = Norm(K, ctx, "hc", ctx_in, K.hc, gains[:, 1, :], K.bank[5], shift=mod[:, 0:KD, 1])
        consts_in = K.sem("consts2_in")
        with nc.Block(no_gpsimd_drain=True) as block:
            @block.sync
            def _(sync):
                sync.dma_start(K.consts[2][:, :], a["consts2"]).then_inc(consts_in, 16)
                start(sync)
                K.load_slabs(sync, RING)
                sync.wait_ge(consts_in, 16)

            @block.tensor
            def _(pe):
                ctx_pe(pe)
                norm_x.pe(pe)
                norm_c.pe(pe)

            @block.scalar
            def _(act):
                ctx_act(act)
                act.wait_ge(ctx_copied, 4)
                norm_x.act(act)
                norm_c.act(act)

            @block.vector
            def _(dve):
                own = K.dve_own
                own.after(dve, dve.tensor_tensor(mod[:, :, :], mod[:, :, :],
                                                 K.col2("b_mod", 48).unsqueeze(2).to_broadcast([P, 48, 2]), ALU.add))
                for i in range(2):
                    last = dve.tensor_scalar(gains[:, i, :], mod[:, KD:2 * KD, i], 1.0, None, ALU.add)
                own.after(dve, last)
                norm_x.dve(dve)
                norm_c.dve(dve)


def gdn_prepare(K, ctx, n0):
    g = K.gdn
    raw = [K.sb(f"raw{i}", [P, 2, T + 2], ctx=ctx) for i in range(2)]
    con = [K.sb(f"conv{i}", [P, 2, T], ctx=ctx) for i in range(2)]
    gv = K.sb("gv", [P, 8, 2 * T], ctx=ctx)
    more = K.sb("gr", [P, 4, 2 * T], ctx=ctx)
    log_ready = K.sem("g_log")
    small = lambda n, w=512: K.sb(n, [16, w], ctx=ctx)
    beta, la, t1, t2, t3, gf, gb = (small(n) for n in ("beta", "la", "gt1", "gt2", "gt3", "gf", "gb"))
    e16, last16, lastd = small("ea", 1), small("glast", 4), small("glastd", 64)
    z_ready, conv_ready, silu_ready = K.sem("g_z_ready"), K.sem("g_conv_ready"), K.sem("g_silu_ready")
    squared, summed, rstd_ready, normed = K.sem("g_squared"), K.sem("g_summed"), K.sem("g_rstd"), K.sem("g_normed")
    turned, turn_copied = K.sem("g_turned"), K.sem("g_turn_copied")
    da_ready, exp_ready, gam_ready = K.sem("g_da"), K.sem("g_exp"), K.sem("g_gam")
    gamt_ready, gamt_read, scal_in, scal_ready = K.sem("g_gamt"), K.sem("g_gamt_read"), K.sem("g_scal_in"), K.sem("g_scal")
    flat = lambda x: x.rearrange("p a t -> p (a t)")
    tiles = [("k", h) for h in range(8)] + [("v", h) for h in range(8)] + [("q", h) for h in range(8)]
    dests = {"k": g["k"], "v": gv, "q": g["q"]}
    offset = {"q": 0, "k": 8, "v": 16}
    seg = lambda kind: 1 if kind == "q" else 2
    TILES = len(tiles)
    norms = [("k", h) for h in range(8)] + [("q", h) for h in range(0, 8, 2)]
    own = K.dve_own

    def pe_first(pe):
        w = view(K.next_slab(pe), cols=32)
        for j in range(2):
            for i, act in enumerate((K.h, K.hc)):
                for k in range(KD):
                    last = pe.matmul(K.bank[4 + j][0:16, i * T:(i + 1) * T], w[:, k, 16 * j:16 * j + 16],
                                     act[:, k, :], start=(k == 0), stop=(k == KD - 1))
        K.slab_done(last)

    def pe_decay(pe):
        pe.wait_ge(gam_ready, 1)
        for j in range(4):
            pe.transpose(K.bank[4][:, j * 16:(j + 1) * 16], g["gam"][:, j * P:(j + 1) * P], K.c("ident", slice(0, 16), n=16))
            last = pe.transpose(K.bank[4][:, 64 + j * 16:64 + (j + 1) * 16], g["beta"][:, j * P:(j + 1) * P],
                                K.c("ident", slice(0, 16), n=16))
        last.then_inc(gamt_ready, 1)
        pe.matmul(K.bank[5][:, 0:64], K.c("ones", slice(0, 16)), lastd[:, :], start=True, stop=True)\
            .then_inc(gamt_ready, 1)

    slab, first_ready = {}, K.sem("g_first_ready")

    def pe_tile(pe, i):
        if i % 2 == 0:
            slab["w"] = view(K.next_slab(pe))
        if i == 0:
            pe.wait_ge(scal_ready, 1)
        if i >= 4:
            pe.wait_ge(z_ready, i - 3)
        j = i % 2
        for m, act in enumerate((K.h, K.hc)[0:seg(tiles[i][0])]):
            last = feature_major(K, pe, K.bank[4 + i % 4], slab["w"][:, :, j * P:(j + 1) * P], act, KD, P, at=m * T)
        if j:
            K.slab_done(last)
        else:
            last.then_inc(first_ready, 1)

    def pe_tail(pe):
        for i, (kind, h) in enumerate(norms):
            pe.wait_ge(squared, i + 1)
            if i >= 2:
                pe.wait_ge(log_ready, i - 1)
            pe.matmul(K.bank[6 + i % 2][:, :], K.c("ones"), con[i % 2][:, :, :].rearrange("p a t -> p (a t)"),
                      start=True, stop=True).then_inc(summed, 1)
        pe.wait_ge(z_ready, 24)
        i = 0
        for src in (gv, g["k"]):
            if src is not gv:
                pe.wait_ge(normed, 8)
            for j in range(4):
                for hh in range(2):
                    if i >= 4:
                        pe.wait_ge(turn_copied, i - 3)
                    for q in range(4):
                        last = pe.transpose(K.bank[i % 4][:, q * P:(q + 1) * P],
                                            src[:, 4 * hh + q, j * P:(j + 1) * P], K.c("ident"))
                    last.then_inc(turned, 1)
                    i += 1


    def rstd(i):
        return g["ktok"][:, i // 2, 512 * (i % 2):512 * (i % 2 + 1)] if i < 8 else more[:, i - 8, :]

    def log_of(act, i):
        act.wait_ge(summed, i + 1)
        act.activation(rstd(i), K.bank[6 + i % 2][:, :], ACT.Ln, bias=K.c("eps")).then_inc(log_ready, 1)

    def act_first(act):
        K.wait_slabs(act, n0 + 1)
        act.copy(t1[:, :], K.bank[4][0:16, :])
        act.copy(la[:, :], K.bank[5][0:16, :]).then_inc(da_ready, 1)

        act.wait_ge(da_ready, 1)
        act.activation(g["beta"][:, :], t1[:, :], ACT.Sigmoid).then_inc(exp_ready, 1)
        act.wait_ge(da_ready, 2)
        act.activation(e16[:, :], K.col2("a_log")[0:16, :], ACT.Exp)
        act.activation(t2[:, :], t2[:, :], ACT.Exp).then_inc(exp_ready, 1)

    def act_decay(act):
        act.wait_ge(scal_in, 1)
        act.activation(g["glast"][:, :], K.bank[5][:, 0:64], ACT.Exp)
        act.activation(g["kdec"][:, :], g["kdec"][:, :], ACT.Exp)
        act.activation(g["bexp"][:, :], g["gamt"][:, :], ACT.Exp).then_inc(scal_ready, 1)

    def act_tile(act, i):
        if i >= TILES + 1:
            return
        if i < TILES:
            kind, h = tiles[i]
            m = seg(kind)
            if i % 2:
                K.wait_slabs(act, n0 + 8 + i // 2)
            else:
                act.wait_ge(first_ready, i // 2 + 1)
            if i >= 2:
                act.wait_ge(conv_ready, i - 1)
            act.copy(raw[i % 2][:, 0:m, 1:T + 1], K.bank[4 + i % 4][:, 0:m * T].rearrange("p (a t) -> p a t", a=m))\
                .then_inc(z_ready, 1)
        if i >= 1 and i - 1 < TILES:
            kind, h = tiles[i - 1]
            m = seg(kind)
            act.wait_ge(conv_ready, i)
            act.activation(dests[kind][:, h, 0:m * T], flat(con[(i - 1) % 2][:, 0:m, :]), ACT.Silu)\
                .then_inc(silu_ready, 1)

    def act_tail(act):
        act.wait_ge(silu_ready, 24)
        for i, (kind, h) in enumerate(norms):
            src = g["k"][:, h, :] if kind == "k" else flat(g["q"][:, h:h + 2, :])
            if i >= 2:
                act.wait_ge(summed, i - 1)
            act.activation(flat(con[i % 2][:, :, :]), src, ACT.Square).then_inc(squared, 1)
            if i >= 1:
                log_of(act, i - 1)
        log_of(act, len(norms) - 1)
        for i in range(len(norms)):
            act.wait_ge(log_ready, i + 1)
            act.activation(rstd(i), rstd(i), ACT.Exp, scale=-0.5).then_inc(rstd_ready, 1)
        for i in range(16):
            act.wait_ge(turned, i + 1)
            dst = g["vtok"] if i < 8 else g["ktok"]
            j, hh = (i % 8) // 2, i % 2
            act.copy(dst[:, j, hh * 512:(hh + 1) * 512], K.bank[i % 4][:, :]).then_inc(turn_copied, 1)

    def dve_first(dve):
        for i in range(2):
            dve.memset(raw[i][:, :, 0:1], 0.0)
            last = dve.memset(raw[i][:, :, T + 1:T + 2], 0.0)
        own.after(dve, last)

        dve.wait_ge(da_ready, 1)
        own.after(dve, dve.tensor_scalar(la[:, :], la[:, :], K.col2("dt_bias")[0:16, :], None, ALU.add))
        dve.scalar_tensor_tensor(t2[:, :], la[:, :], -1.0, la[:, :], ALU.mult, ALU.min).then_inc(da_ready, 1)
        dve.wait_ge(exp_ready, 2)
        own.after(dve, softplus_small(dve, own, t2[:, :], t3[:, :], gf[:, :], gb[:, :], t3[:, :]))
        own.after(dve, dve.scalar_tensor_tensor(la[:, :], la[:, :], 0.0, t3[:, :], ALU.max, ALU.add))
        own.after(dve, dve.tensor_scalar(la[:, :], la[:, :], e16[:, :], -1.0, ALU.mult, ALU.mult))
        zeros = K.c("nomask", slice(0, 16), n=P)
        for j in range(4):
            c = slice(j * P, (j + 1) * P)
            dve.tensor_tensor_scan(gf[:, c], la[:, c], zeros, 0.0, ALU.add, ALU.add)
            last = dve.tensor_tensor_scan(gb[:, c][:, ::-1], la[:, c][:, ::-1], zeros, 0.0, ALU.add, ALU.add)
        own.after(dve, last)
        fwd, bwd = K.c("fwd", slice(0, 16)), K.c("bwd", slice(0, 16))
        own.after(dve, dve.tensor_scalar(t3[:, :], gb[:, :], bwd, None, ALU.mult))
        own.after(dve, dve.scalar_tensor_tensor(g["gam"][:, :], gf[:, :], fwd, t3[:, :], ALU.mult, ALU.add))
        tile4 = lambda x: x[:, :].rearrange("p (j t) -> p j t", j=4)
        own.after(dve, dve.tensor_scalar(last16[:, :], tile4(gb)[:, :, 0], bwd, None, ALU.mult))
        own.after(dve, dve.scalar_tensor_tensor(last16[:, :], tile4(gf)[:, :, P - 1], fwd, last16[:, :],
                                                ALU.mult, ALU.add))
        dve.tensor_tensor(lastd[:, :].rearrange("p (j r) -> p j r", j=4),
                          K.c("ident", slice(0, 16), n=16).unsqueeze(1).to_broadcast([16, 4, 16]),
                          last16[:, :].unsqueeze(2).to_broadcast([16, 4, 16]), ALU.mult).then_inc(gam_ready, 1)

    def dve_decay(dve):
        dve.wait_ge(gamt_ready, 2)
        dve.tensor_copy(g["gamt"][:, :], K.bank[4][:, 0:64])
        own.after(dve, dve.tensor_copy(g["betat"][:, :], K.bank[4][:, 64:128]))
        dve.tensor_tensor(g["kdec"][:, :], K.bank[5][:, 0:64], g["gamt"][:, :], ALU.subtract).then_inc(scal_in, 1)

    def dve_tile(dve, i):
        kind, h = tiles[i]
        m = seg(kind)
        r, o = raw[i % 2], con[i % 2][:, 0:m, :]
        tap = lambda j: K.col2("conv", 72)[:, j * 24 + offset[kind] + h:j * 24 + offset[kind] + h + 1]
        dve.wait_ge(z_ready, i + 1)
        if i >= 2:
            dve.wait_ge(silu_ready, i - 1)
        own.after(dve, dve.tensor_scalar(o, r[:, 0:m, 0:T], tap(0), None, ALU.mult))
        own.after(dve, dve.scalar_tensor_tensor(o, r[:, 0:m, 1:T + 1], tap(1), o, ALU.mult, ALU.add))
        dve.scalar_tensor_tensor(o, r[:, 0:m, 2:T + 2], tap(2), o, ALU.mult, ALU.add).then_inc(conv_ready, 1)

    def dve_tail(dve):
        for i, (kind, h) in enumerate(norms):
            dve.wait_ge(rstd_ready, i + 1)
            o = g["k"][:, h, :] if kind == "k" else flat(g["q"][:, h:h + 2, :])
            scale = 1.0 if kind == "k" else float(P) ** -0.5
            dve.scalar_tensor_tensor(o, o, scale, rstd(i), ALU.mult, ALU.mult).then_inc(normed, 1)
        dve.wait_ge(scal_ready, 1)
        dve.tensor_tensor(g["bexp"][:, :], g["bexp"][:, :], g["betat"][:, :], ALU.mult)

    return ((pe_first, pe_decay, pe_tile, pe_tail), (act_first, act_decay, act_tile, act_tail),
            (dve_first, dve_decay, dve_tile, dve_tail), gv)


def latent_attention_stage(K):
    nc = K.nc
    n0 = K.eaten
    da_ready = K.sem("g_da")
    with ExitStack() as ctx:
        g = K.gdn
        ((pe_first, pe_decay, pe_tile, pe_tail), (act_first, act_decay, act_tile, act_tail),
         (dve_first, dve_decay, dve_tile, dve_tail), gv) = gdn_prepare(K, ctx, n0)
        spare = g["vtok"][:, :, :].rearrange("p j (a t) -> p (j a) t", t=T)
        a = spare[:, 0:12, :]
        v = spare[:, 12:16, :]
        buffers = [[g["ktok"][:, i, 512 * j:512 * (j + 1)] for j in range(2)] for i in range(4)]
        sq = gv[:, 0:6, :].rearrange("p h (a t) -> p (h a) t", t=T)
        rot = K.sb("rot2", [P, 2, T], ctx=ctx)
        gain = K.sb("gain2", [P, 1], ctx=ctx)
        z_ready, squared, summed = K.sem("a2_z_ready"), K.sem("a2_squared"), K.sem("a2_summed")
        rstd_ready, normed = K.sem("a2_rstd"), K.sem("a2_normed")
        rotated, roped = K.sem("a2_rotated"), K.sem("a2_roped")
        units = []
        for h in range(8):
            g = h // 4
            for i in range(TT):
                units.append({"keys": 512, "rows": slice(0, P), "q": a[:, h, i * P:(i + 1) * P],
                              "k": [(a[:, 8 + 2 * g:10 + 2 * g, :].rearrange("p a t -> p (a t)"), slice(0, 512))],
                              "mask": K.c("nomask"), "v": [v[:, c, g * P:(g + 1) * P] for c in range(4)],
                              "out": K.attn[:, h, i * P:(i + 1) * P]})
        att = Attention(K, ctx, "a2", units, ((0, 1), (2,), (3,)), 512, buffers)
        STEPS = len(units) + 2
        pairs = [slice(2 * i, 2 * i + 2) for i in range(6)]
        roped_tiles = [slice(2 * i, 2 * i + 2) for i in range(4)] + [slice(8, 9), slice(10, 11)]
        with nc.Block(no_gpsimd_drain=True) as block:
            @block.sync
            def _(sync):
                K.load_slabs(sync, n0 + 6 + 13)

            @block.tensor
            def _(pe):
                pe_first(pe)
                w = view(K.next_slab(pe))
                for g in range(2):
                    for i, act in enumerate((K.h, K.hc)):
                        last = feature_major(K, pe, K.bank[g], w[:, :, g * P:(g + 1) * P], act, KD, P, at=i * T)
                K.slab_done(last)
                w = view(K.next_slab(pe))
                for i, act in enumerate((K.h, K.hc)):
                    last = token_major(K, pe, K.bank[2 + i], w, act, KD, HALF)
                K.slab_done(last)
                for n in range(4):
                    w = view(K.next_slab(pe))
                    pe.wait_ge(z_ready, (2, 2, 4, 4)[n])
                    K.slab_done(feature_major(K, pe, K.bank[n], w, K.h, KD, HALF))
                for i in range(6):
                    pe.wait_ge(squared, i + 1)
                    if i == 0:
                        pe.wait_ge(da_ready, 1)
                    if i >= 2:
                        pe.wait_ge(rstd_ready, i - 1)
                    pe.matmul(K.bank[4 + i % 2][:, :], K.c("ones"), sq[:, pairs[i], :].rearrange("p a t -> p (a t)"),
                              start=True, stop=True).then_inc(summed, 1)
                pe.wait_ge(rstd_ready, 6)
                pe_decay(pe)
                pe.wait_ge(normed, 12)
                for i, t in enumerate(roped_tiles):
                    if i >= 2:
                        pe.wait_ge(roped, i - 1)
                    n = (t.stop - t.start) * T
                    pe.matmul(K.bank[6 + i % 2][:, 0:n], K.c("axial"), a[:, t, :].rearrange("p a t -> p (a t)"),
                              start=True, stop=True).then_inc(rotated, 1)
                pe.wait_ge(roped, 6)
                pe.wait_ge(z_ready, 8)
                att.pe(pe, mid_step=lambda i: pe_tile(pe, i))
                for i in range(STEPS, 24):
                    pe_tile(pe, i)
                pe.wait_ge(att.out_copied, len(units))
                pe_tail(pe)

            @block.scalar
            def _(act):
                bank = lambda b: K.bank[b][:, :].rearrange("p (a t) -> p a t", a=2)
                act_first(act)
                K.wait_slabs(act, n0 + 2)
                for g in range(2):
                    act.copy(a[:, 8 + 2 * g:10 + 2 * g, :], bank(g)).then_inc(z_ready, 1)
                K.wait_slabs(act, n0 + 3)
                for i in range(2):
                    act.copy(v[:, 2 * i:2 * i + 2, :], bank(2 + i)).then_inc(z_ready, 1)
                for n in range(4):
                    K.wait_slabs(act, n0 + 4 + n)
                    act.copy(a[:, 2 * n:2 * n + 2, :], bank(n)).then_inc(z_ready, 1)
                act.wait_ge(z_ready, 8)
                for t in pairs:
                    act.activation(sq[:, t, :], a[:, t, :], ACT.Square).then_inc(squared, 1)
                for i, t in enumerate(pairs):
                    act.wait_ge(summed, i + 1)
                    act.activation(sq[:, t, :], bank(4 + i % 2), ACT.Ln, bias=K.c("eps"), scale=1.0 / P)\
                        .then_inc(rstd_ready, 1)
                act.wait_ge(rstd_ready, 6)
                act.activation(sq[:, :, :], sq[:, :, :], ACT.Exp, scale=-0.5).then_inc(rstd_ready, 1)
                act_decay(act)
                att.act(act, at_step=lambda i: act_tile(act, i - 1) if i else None)
                for i in range(STEPS - 1, 25):
                    act_tile(act, i)
                act_tail(act)

            @block.vector
            def _(dve):
                own = K.dve_own
                dve_first(dve)
                own.after(dve, dve.tensor_scalar(gain[:, :], K.col2("q_norm"), float(P) ** -0.5, None, ALU.mult))
                dve_decay(dve)
                dve.wait_ge(rstd_ready, 7)
                for t in range(12):
                    g = gain[:, :] if t < 8 else K.col2("k_norm")
                    dve.scalar_tensor_tensor(a[:, t, :], a[:, t, :], g, sq[:, t, :], ALU.mult, ALU.mult)\
                        .then_inc(normed, 1)
                for i, t in enumerate(roped_tiles):
                    m = t.stop - t.start
                    cos = K.c("axcos").unsqueeze(1).to_broadcast([P, m, T])
                    sin = K.c("axsin").unsqueeze(1).to_broadcast([P, m, T])
                    dve.wait_ge(rotated, i + 1)
                    if i:
                        dve.wait_ge(roped, i)
                    own.after(dve, dve.tensor_tensor(rot[:, 0:m, :],
                                                     K.bank[6 + i % 2][:, 0:m * T].rearrange("p (a t) -> p a t", a=m),
                                                     sin, ALU.mult))
                    own.after(dve, dve.tensor_tensor(a[:, t, :], a[:, t, :], cos, ALU.mult))
                    dve.tensor_tensor(a[:, t, :], a[:, t, :], rot[:, 0:m, :], ALU.add).then_inc(roped, 1)
                att.dve(dve, at_step=lambda i: dve_tile(dve, i - 2) if i >= 2 else None)
                for i in range(STEPS - 3, 24):
                    dve_tile(dve, i)
                dve_tail(dve)


def column(d, j, h):
    return slice(16 * j + 8 * d + h, 16 * j + 8 * d + h + 1)


class GdnMatrices:

    STEPS = 5

    def __init__(self, K, ctx, d, half, buffers):
        self.K, self.d, self.heads = K, d, [4 * half + i for i in range(4)]
        self.lt, self.xt, self.pt, self.qdec = buffers
        sem = K.sem
        self.dec_in, self.dec_ready, self.spread = sem("g_dec_in"), sem("g_dec_ready"), sem("g_spread")
        self.kb_ready, self.mats_ready, self.mats_read = sem("g_kb_ready"), sem("g_mats_ready"), sem("g_mats_read")
        self.spread_read = sem("g_spread_read")
        self.dec = [K.sb(f"gdec{i}", [P, 4, P], ctx=ctx) for i in range(2)]
        self.kb = [K.sb(f"gkb{i}", [P, 2 * T], ctx=ctx) for i in range(2)]
        self.eb = [K.sb(f"geb{i}", [P, T], ctx=ctx) for i in range(2)]
        self.inv = Inverse(K, ctx, "ginv", 4, LEVELS, "levels" if d == 0 else "levels_back",
                           lambda i: self.lt[:, i, :, :], lambda i: self.xt[:, i, :, :],
                           lambda eng, i: eng.wait_ge(self.mats_read, i + 1))

    def pe(self, pe, i):
        K, g = self.K, self.K.gdn
        if i < 4:
            if i >= 1:
                pe.wait_ge(self.spread_read, 2 * i)
                pe.wait_ge(self.kb_ready, i)
            row = K.c("ident", slice(0, 16), first=8 * self.d + self.heads[i], n=1).to_broadcast([16, P])
            pe.matmul(K.bank[4][:, :], row, g["gam"][:, :], start=True, stop=True).then_inc(self.spread, 1)
            pe.matmul(K.bank[5][:, :], row, g["beta"][:, :], start=True, stop=True).then_inc(self.spread, 1)
        if i >= 1:
            h = self.heads[i - 1]
            pe.wait_ge(self.kb_ready, i)
            if i >= 2:
                pe.wait_ge(self.mats_read, i - 1)
            for j in range(4):
                c = slice(j * P, (j + 1) * P)
                pe.matmul(K.bank[6][:, c], g["k"][:, h, c], self.kb[(i - 1) % 2][:, c], start=True, stop=True)
            for j in range(TT):
                c = slice(j * P, (j + 1) * P)
                last = pe.matmul(K.bank[7][:, c], g["k"][:, h, c], g["q"][:, h, c], start=True, stop=True)
            last.then_inc(self.mats_ready, 1)
        if i == 4:
            pe.wait_ge(self.mats_read, 4)

    def dve(self, dve, i):
        K, g, dec = self.K, self.K.gdn, self.dec
        flat = lambda x: x.rearrange("p a t -> p (a t)")
        if i < 4:
            h = self.heads[i]
            dve.wait_ge(self.spread, 2 * i + 1)
            if i >= 2:
                dve.wait_ge(self.mats_read, i - 1)
            for j in range(4):
                last = dve.scalar_tensor_tensor(dec[i % 2][:, j, :], K.bank[4][:, j * P:(j + 1) * P],
                                                g["gamt"][:, column(self.d, j, h)],
                                                K.c("future" if self.d == 0 else "past"), ALU.subtract, ALU.add)
            last.then_inc(self.dec_in, 1)
            dve.wait_ge(self.spread, 2 * i + 2)
            dve.tensor_tensor(self.kb[i % 2][:, :], g["k"][:, h, :], K.bank[5][:, :], ALU.mult).then_inc(self.kb_ready, 1)
            dve.wait_ge(self.dec_ready, i + 1)
            dve.tensor_tensor(self.qdec[:, i, :], g["q"][:, h, :], self.eb[i % 2][:, :], ALU.mult)\
                .then_inc(self.spread_read, 1)
        if i >= 1:
            dve.wait_ge(self.mats_ready, i)
            dve.tensor_tensor(self.pt[:, i - 1, :, :], K.bank[7][:, 0:T].rearrange("p (a t) -> p a t", a=2),
                              dec[(i - 1) % 2][:, 0:2, :], ALU.mult)
            dve.tensor_tensor(flat(self.lt[:, i - 1, :, :]), K.bank[6][:, :], flat(dec[(i - 1) % 2][:, :, :]),
                              ALU.mult).then_inc(self.mats_read, 1)

    def act(self, act, i):
        K, dec = self.K, self.dec[i % 2]
        flat = dec[:, :, :].rearrange("p a t -> p (a t)")
        act.wait_ge(self.dec_in, i + 1)
        if i >= 2:
            act.wait_ge(self.spread_read, 2 * (i - 1))
        act.activation(self.eb[i % 2][:, :], K.bank[4][:, 0:T], ACT.Exp).then_inc(self.spread_read, 1)
        act.activation(flat, flat, ACT.Exp).then_inc(self.dec_ready, 1)


class GdnScan:

    STEPS = 12

    def __init__(self, K, ctx, d, half, buffers):
        self.K, self.d, self.half, self.heads = K, d, half, [4 * half + i for i in range(4)]
        self.order = (2, 3, 0, 1) if d == 0 else (3, 2, 1, 0)
        self.lt, self.xt, self.pt, self.qdec = buffers
        self.u, self.wt = self.lt, self.xt
        self.xb = [K.sb(f"gxb{i}", [P, 4, P], ctx=ctx) for i in range(2)]
        self.xe = [K.sb(f"gxe{i}", [P, 4, P], ctx=ctx) for i in range(2)]
        self.state, self.delta, self.dk = (K.sb(n, [P, 4, P], ctx=ctx) for n in ("gstate", "gdelta", "gdk"))
        sem = K.sem
        self.scaled, self.uw_ready, self.uw_copied = sem("g_scaled"), sem("g_uw_ready"), sem("g_uw_copied")
        self.s_ready, self.ws_ready, self.delta_ready = sem("g_s_ready"), sem("g_ws_ready"), sem("g_delta_ready")
        self.sn_ready, self.o_ready, self.o_copied = sem("g_sn_ready"), sem("g_o_ready"), sem("g_o_copied")
        self.bank4 = lambda b: K.bank[b][:, :].rearrange("p (a t) -> p a t", a=4)

    def pe(self, pe, step):
        K, g = self.K, self.K.gdn
        if step < 4:
            i, h = step, self.heads[step]
            pe.wait_ge(self.scaled, i + 1)
            if i >= 2:
                pe.wait_ge(self.uw_copied, 2 * (i - 1))
            ub, wb = K.bank[2 * (i % 2)], K.bank[1 + 2 * (i % 2)]
            f = slice(h * P, (h + 1) * P)
            for j in range(4):
                pe.matmul(ub[:, j * P:(j + 1) * P], self.xb[i % 2][:, j, :], g["vtok"][:, j, f], start=True, stop=True)
            for j in range(4):
                last = pe.matmul(wb[:, j * P:(j + 1) * P], g["ktok"][:, j, f], self.xe[i % 2][:, j, :],
                                 start=True, stop=True)
            last.then_inc(self.uw_ready, 1)
        elif step < self.STEPS:
            n, second = divmod(step - 4, 2)
            j = self.order[n]
            if not second:
                if n == 0:
                    pe.wait_ge(self.uw_copied, 8)
                pe.wait_ge(self.s_ready, n + 1)
                for i in range(4):
                    last = pe.matmul(K.bank[0][:, i * P:(i + 1) * P], self.wt[:, i, j, :], self.state[:, i, :],
                                     start=True, stop=True)
                last.then_inc(self.ws_ready, 1)
                return
            pe.wait_ge(self.delta_ready, 2 * n + 2)
            if n < 3:
                for i, h in enumerate(self.heads):
                    last = pe.matmul(K.bank[1][:, i * P:(i + 1) * P], g["ktok"][:, j, h * P:(h + 1) * P],
                                     self.dk[:, i, :], start=True, stop=True)
                last.then_inc(self.sn_ready, 1)
            if j < 2:
                for i in range(4):
                    o = K.bank[2 + n % 2][:, i * P:(i + 1) * P]
                    pe.matmul(o, self.state[:, i, :], self.qdec[:, i, j * P:(j + 1) * P], start=True, stop=False)
                    last = pe.matmul(o, self.delta[:, i, :], self.pt[:, i, j, :], start=False, stop=True)
                last.then_inc(self.o_ready, 1)

    def dve(self, dve, step):
        K, g = self.K, self.K.gdn
        if step < 4:
            i, h = step, self.heads[step]
            if i >= 2:
                dve.wait_ge(self.uw_ready, i - 1)
            for j in range(4):
                dve.tensor_scalar(self.xb[i % 2][:, j, :], self.xt[:, i, j, :], g["betat"][:, column(self.d, j, h)],
                                  None, ALU.mult)
                last = dve.tensor_scalar(self.xe[i % 2][:, j, :], self.xt[:, i, j, :], g["bexp"][:, column(self.d, j, h)],
                                         None, ALU.mult)
            last.then_inc(self.scaled, 1)
            if i == 3:
                dve.memset(self.state[:, :, :], 0.0).then_inc(self.s_ready, 1)
        elif step < self.STEPS:
            n, second = divmod(step - 4, 2)
            j = self.order[n]
            if not second:
                dve.wait_ge(self.ws_ready, n + 1)
                if n == 3:
                    dve.wait_ge(self.o_ready, 1)
                dve.tensor_tensor(self.delta[:, :, :], self.u[:, :, j, :], self.bank4(0), ALU.subtract)\
                    .then_inc(self.delta_ready, 1)
                dve.wait_ge(self.delta_ready, 2 * n + 1)
                for i, h in enumerate(self.heads):
                    last = dve.tensor_scalar(self.dk[:, i, :], self.delta[:, i, :], g["kdec"][:, column(self.d, j, h)],
                                             None, ALU.mult)
                last.then_inc(self.delta_ready, 1)
                return
            if n < 3:
                dve.wait_ge(self.sn_ready, n + 1)
                if j < 2:
                    dve.wait_ge(self.o_ready, 1)
                for i, h in enumerate(self.heads):
                    last = dve.scalar_tensor_tensor(self.state[:, i, :], self.state[:, i, :],
                                                    g["glast"][:, column(self.d, j, h)],
                                                    K.bank[1][:, i * P:(i + 1) * P], ALU.mult, ALU.add)
                last.then_inc(self.s_ready, 1)
            if self.d == 1 and n >= 2:
                dve.wait_ge(self.o_ready, n - 1)
                o = g["o"][:, 4 * self.half:4 * self.half + 4, j * P:(j + 1) * P]
                dve.tensor_tensor(o, o, self.bank4(2 + n % 2), ALU.add).then_inc(self.o_copied, 1)

    def act(self, act, step):
        g = self.K.gdn
        if step < 4:
            i = step
            act.wait_ge(self.uw_ready, i + 1)
            act.copy(self.u[:, i, :, :], self.bank4(2 * (i % 2))).then_inc(self.uw_copied, 1)
            act.copy(self.wt[:, i, :, :], self.bank4(1 + 2 * (i % 2))).then_inc(self.uw_copied, 1)
        elif step < self.STEPS and self.d == 0:
            n, second = divmod(step - 4, 2)
            if second and n >= 2:
                act.wait_ge(self.o_ready, n - 1)
                j = self.order[n]
                act.copy(g["o"][:, 4 * self.half:4 * self.half + 4, j * P:(j + 1) * P], self.bank4(2 + n % 2))\
                    .then_inc(self.o_copied, 1)


def gdn_stages(K):
    nc = K.nc
    quarters = [(d, half) for d in range(2) for half in range(2)]
    with ExitStack() as ctx:
        four = [r[:, :].rearrange("p (a b t) -> p a b t", a=4, b=4) for r in K.ring]
        four.append(K.sb("gxt", [P, 4, 4, P], ctx=ctx)[:, :, :, :])
        buffers = []
        for i in range(2):
            pt = K.sb(f"gpt{i}", [P, 4, TT, P], ctx=ctx)
            qdec = K.sb(f"gqdec{i}", [P, 4, T], ctx=ctx)
            buffers.append((four[2 * i], four[2 * i + 1], pt, qdec))
        for q in range(5):
            with ExitStack() as qctx:
                mats = GdnMatrices(K, qctx, *quarters[q], buffers[q % 2]) if q < 4 else None
                scan = GdnScan(K, qctx, *quarters[q - 1], buffers[(q - 1) % 2]) if q else None

                def program(eng, name):
                    def scan_step(step):
                        if scan is not None:
                            {"pe": scan.pe, "dve": scan.dve, "act": scan.act}[name](eng, step)
                    if mats is None:
                        for step in range(GdnScan.STEPS):
                            scan_step(step)
                        return
                    for i in range(GdnMatrices.STEPS):
                        if i < 4:
                            scan_step(i)
                        if name == "pe":
                            mats.pe(eng, i)
                        elif name == "dve":
                            mats.dve(eng, i)
                        elif i < 4:
                            mats.act(eng, i)
                    inverse = {"pe": mats.inv.pe, "dve": mats.inv.dve, "act": mats.inv.act}[name]
                    inverse(eng, between=lambda pair: scan_step(4 + pair))
                with nc.Block(no_gpsimd_drain=True) as block:
                    @block.tensor
                    def _(pe):
                        program(pe, "pe")

                    @block.vector
                    def _(dve):
                        program(dve, "dve")

                    @block.scalar
                    def _(act):
                        program(act, "act")

                    if mats is not None:
                        @block.gpsimd
                        def _(pool):
                            mats.inv.pool(pool)
            K.restart_stages()


def merge_stage(K):
    nc, g = K.nc, K.gdn
    n0 = K.eaten
    with ExitStack() as ctx:
        zs = K.sb("zsilu", [P, 8, T], ctx=ctx)
        gates = K.sb("gates", [P, 16, T], ctx=ctx)
        sq = K.sb("osq", [P, 8, T], ctx=ctx)
        y = K.sb("y2", [P, 8, T], ctx=ctx)
        tmp = K.sb("ytmp", [P, 2, T], ctx=ctx)
        h_parts, x_parts = Parts(K, ctx, "m_h", 8), Parts(K, ctx, "m_x", 8)
        split = Split(K, ctx, "m", n0, 24)
        o = g["o"]
        read, squared, summed, rstd_ready = K.sem("m_read"), K.sem("m_squared"), K.sem("m_summed"), K.sem("m_rstd")
        o_ready, y_ready, x_updated = K.sem("m_o_ready"), K.sem("m_y_ready"), K.sem("m_x_updated")
        pair = lambda b: K.bank[b][:, :].rearrange("p (a t) -> p a t", a=2)
        two = lambda i: slice(2 * i, 2 * i + 2)
        flat = lambda x: x.rearrange("p a t -> p (a t)")
        with nc.Block(no_gpsimd_drain=True) as block:
            @block.sync
            def _(sync):
                K.load_slabs(sync, n0 + 24 + RING)

            @block.gpsimd
            def _(pool):
                split.pool(pool)

            @block.tensor
            def _(pe):
                for i in range(4):
                    pe.wait_ge(squared, i + 1)
                    pe.matmul(K.bank[4 + i][:, :], K.c("ones"), flat(sq[:, two(i), :]), start=True, stop=True)\
                        .then_inc(summed, 1)
                for n in range(24):
                    w = split.next_view(pe)
                    if n >= 4:
                        pe.wait_ge(read, n - 3)
                    parts, ready = {0: (h_parts, 4), 12: (x_parts, 4), 16: (h_parts, 8), 20: (x_parts, 8)}.get(n, (parts if n else None, 0))
                    if ready:
                        pe.wait_ge(parts.lo_ready, ready)
                    K.slab_done(feature_major3(pe, K.bank[n % 4], w, (parts.hi, parts.lo), KD, HALF))

            @block.scalar
            def _(act):
                split.act(act, 1)
                for i in range(4):
                    h_parts.act(act, pair_of(i), K.h[:, pair_of(i), :])
                split.act(act, 3)
                for i in range(4):
                    x_parts.act(act, pair_of(i), K.attn[:, pair_of(i), :])
                for i in range(4):
                    act.activation(sq[:, two(i), :], o[:, two(i), :], ACT.Square).then_inc(squared, 1)
                for i in range(4):
                    act.wait_ge(summed, i + 1)
                    last = act.activation(sq[:, two(i), :], pair(4 + i), ACT.Ln, bias=K.c("eps"), scale=1.0 / P)
                K.act_own.after(act, last)
                act.activation(sq[:, :, :], sq[:, :, :], ACT.Exp, scale=-0.5).then_inc(rstd_ready, 1)
                for n in range(20):
                    split.act(act, n + 3)
                    K.wait_slabs(act, n0 + n + 1)
                    if n >= 12:
                        if n == 12:
                            for i in range(4):
                                act.wait_ge(o_ready, 2 * i + 2)
                                h_parts.act(act, pair_of(i), o[:, pair_of(i), :])
                        if n >= 16:
                            act.wait_ge(y_ready, 2 * (n - 16) + 2)
                            x_parts.act(act, pair_of(n - 16), y[:, pair_of(n - 16), :])
                        if n == 19:
                            split.act(act, 24)
                    elif n < 4:
                        act.activation(zs[:, two(n), :], pair(n % 4), ACT.Silu).then_inc(read, 1)
                    else:
                        act.activation(gates[:, two(n - 4), :], pair(n % 4), ACT.Sigmoid).then_inc(read, 1)

            @block.vector
            def _(dve):
                own = K.dve_own
                for i in range(4):
                    h_parts.dve(dve, pair_of(i), K.h[:, pair_of(i), :])
                for i in range(4):
                    x_parts.dve(dve, pair_of(i), K.attn[:, pair_of(i), :])
                dve.wait_ge(rstd_ready, 1)
                for h in range(8):
                    last = dve.scalar_tensor_tensor(o[:, h, :], o[:, h, :], K.col2("gdn_norm"), sq[:, h, :], ALU.mult, ALU.mult)
                own.after(dve, last)
                dve.wait_ge(read, 4)
                for h in range(8):
                    dve.tensor_tensor(o[:, h, :], o[:, h, :], zs[:, h, :], ALU.mult).then_inc(o_ready, 1)
                for n in range(12, 20):
                    K.wait_slabs(dve, n0 + n + 1)
                    i = n % 4
                    if n == 12:
                        for q in range(4):
                            h_parts.dve(dve, pair_of(q), o[:, pair_of(q), :])
                        dve.wait_ge(read, 12)
                    if n < 16:
                        dve.tensor_tensor(y[:, two(i), :], pair(i), gates[:, two(i), :], ALU.mult).then_inc(read, 1)
                    else:
                        if n > 16:
                            dve.wait_ge(y_ready, 2 * i)
                        dve.tensor_tensor(tmp[:, :, :], pair(i), gates[:, 8 + 2 * i:10 + 2 * i, :], ALU.mult).then_inc(read, 1)
                        dve.wait_ge(read, n + 1)
                        for k in range(2):
                            dve.tensor_tensor(y[:, 2 * i + k, :], y[:, 2 * i + k, :], tmp[:, k, :], ALU.add).then_inc(y_ready, 1)
                        x_parts.dve(dve, pair_of(i), y[:, pair_of(i), :])
                for i in range(4):
                    K.wait_slabs(dve, n0 + 21 + i)
                    for k in range(2):
                        t = 2 * i + k
                        dve.scalar_tensor_tensor(K.x[:, t, :], K.bank[i][:, k * T:(k + 1) * T], K.mod[:, 16 + t, 0:1],
                                                 K.x[:, t, :], ALU.mult, ALU.add).then_inc(x_updated, 1)


def conv_ffn_stage(K):
    nc = K.nc
    n0 = K.eaten
    with ExitStack() as ctx:
        hidden = Parts(K, ctx, "f_hidden", FK)
        whole_hidden = K.sb("hidden2", [P, 2, 2, T], ctx=ctx)
        raw = [K.sb(f"fraw{i}", [P, 4, T + 2], ctx=ctx) for i in range(2)]
        con = [K.sb(f"fcon{i}", [P, 4, T], ctx=ctx) for i in range(2)]
        gate = [K.sb(f"fgate{i}", [P, 2, T], ctx=ctx) for i in range(2)]
        gain = K.sb("fgain", [P, KD], ctx=ctx)
        gain_ready = K.sem("f_gain_ready")
        norm = Norm(K, ctx, "f", K.x, K.h, gain, K.bank[4], shift=K.mod[:, 24:32, 0],
                    parts=Parts(K, ctx, "fh", KD))
        split = Split(K, ctx, "f", n0, FK + 12)
        raw_ready, conv_ready, silu_ready = K.sem("f_raw_ready"), K.sem("f_conv_ready"), K.sem("f_silu_ready")
        hidden_ready, x_updated = K.sem("f_hidden_ready"), K.sem("f_x_updated")
        pair = lambda b: K.bank[b][:, :].rearrange("p (a t) -> p a t", a=2)
        N = FK // 2
        with nc.Block(no_gpsimd_drain=True) as block:
            @block.sync
            def _(sync):
                K.load_slabs(sync, n0 + FK + 12)

            @block.gpsimd
            def _(pool):
                split.pool(pool)

            @block.tensor
            def _(pe):
                norm.pe(pe)
                for i in range(N):
                    for part in range(2):
                        w = split.next_view(pe)
                        if i >= 2:
                            pe.wait_ge(raw_ready, 2 * (i - 2) + part + 1)
                        parts = norm.parts
                        K.slab_done(feature_major3(pe, K.bank[2 * (i % 2) + part], w, (parts.hi, parts.lo), KD, HALF,
                                                   first=(lambda k: pe.wait_ge(parts.lo_ready, k // 2 + 1))
                                                   if i == part == 0 else None))
                pe.wait_ge(raw_ready, 2 * N)
                ffn_out_pe(K, pe, split, hidden, x_updated)

            @block.scalar
            def _(act):
                norm.act(act, between=lambda: split.act(act, 2))
                for i in range(N + 2):
                    if i < N:
                        for part in range(2):
                            split.act(act, 2 * i + part + 3)
                            K.wait_slabs(act, n0 + 2 * i + part + 1)
                            if i >= 2:
                                act.wait_ge(conv_ready, i - 1)
                            act.copy(raw[i % 2][:, 2 * part:2 * part + 2, 1:T + 1], pair(2 * (i % 2) + part))\
                                .then_inc(raw_ready, 1)
                    else:
                        split.act(act, FK + 3)
                    if i >= 2:
                        act.wait_ge(hidden_ready, i - 1)
                        hidden.act(act, pair_of(i - 2), whole_hidden[:, i % 2, :, :])
                    if 1 <= i <= N:
                        act.wait_ge(conv_ready, i)
                        if i >= 3:
                            act.wait_ge(hidden_ready, i - 2)
                        act.activation(gate[(i - 1) % 2][:, :, :], con[(i - 1) % 2][:, 0:2, :], ACT.Silu).then_inc(silu_ready, 1)
                split.act(act, FK + 12)

            @block.vector
            def _(dve):
                own = K.dve_own
                for i in range(2):
                    dve.memset(raw[i][:, :, 0:1], 0.0)
                    dve.memset(raw[i][:, :, T + 1:T + 2], 0.0)
                own.after(dve, dve.tensor_scalar(gain[:, :], K.mod[:, 32:40, 0], 1.0, None, ALU.add))
                norm.dve(dve)
                for i in range(N + 2):
                    if i >= 2:
                        hidden.dve(dve, pair_of(i - 2), whole_hidden[:, i % 2, :, :])
                    if i < N:
                        r, o = raw[i % 2], con[i % 2]
                        dve.wait_ge(raw_ready, 2 * i + 2)
                        if i >= 2:
                            dve.wait_ge(silu_ready, i - 1)
                            dve.wait_ge(hidden_ready, i - 1)
                        for j in range(3):
                            for q in range(4):
                                t = (FK if q >= 2 else 0) + 2 * i + q % 2
                                tap = K.col2("ffn_conv", 132)[:, 44 * j + t:44 * j + t + 1]
                                if j == 0:
                                    last = dve.tensor_scalar(o[:, q, :], r[:, q, 0:T], tap, K.col2("ffn_b", 44)[:, t:t + 1],
                                                             ALU.mult, ALU.add)
                                else:
                                    last = dve.scalar_tensor_tensor(o[:, q, :], r[:, q, j:j + T], tap, o[:, q, :],
                                                                    ALU.mult, ALU.add)
                            if j < 2:
                                own.after(dve, last)
                        last.then_inc(conv_ready, 1)
                    if 1 <= i <= N:
                        dve.wait_ge(silu_ready, i)
                        if i >= 3:
                            dve.wait_ge(hidden.lo_ready, i - 2)
                        dve.tensor_tensor(whole_hidden[:, (i - 1) % 2, :, :], gate[(i - 1) % 2][:, :, :],
                                          con[(i - 1) % 2][:, 2:4, :], ALU.mult).then_inc(hidden_ready, 1)
                for jj in range(4):
                    K.wait_slabs(dve, n0 + FK + 3 * (jj + 1))
                    for j in range(2):
                        k = 2 * jj + j
                        dve.scalar_tensor_tensor(K.x[:, k, :], K.bank[2 * (jj % 2) + j][:, 0:T], K.mod[:, 40 + k, 0:1],
                                                 K.x[:, k, :], ALU.mult, ALU.add).then_inc(x_updated, 1)


def final_norm_stage(K):
    nc = K.nc
    with ExitStack() as ctx:
        norm = Norm(K, ctx, "final", K.x, K.h, K.col2("final", KD), K.bank[4])
        with nc.Block(no_gpsimd_drain=True) as block:
            @block.scalar
            def _(act):
                norm.act(act)

            @block.tensor
            def _(pe):
                norm.pe(pe)

            @block.vector
            def _(dve):
                norm.dve(dve)


def second_block(K):
    K.plan(second_slabs(K))
    with ExitStack() as ctx:
        K.consts[2] = K.sb("const2", [P, CONSTS[2].shape[1]], ctx=ctx)
        K.attn = K.sb("attn", [P, 8, T], ctx=ctx)
        g = K.gdn = {"o": K.sb("go", [P, 8, T], ctx=ctx)}
        with ExitStack() as gctx:
            for n, w in (("gam", 512), ("beta", 512)):
                g[n] = K.sb("g_" + n, [16, w], ctx=gctx)
            for n in ("gamt", "betat", "kdec", "glast", "bexp"):
                g[n] = K.sb("g_" + n, [P, 64], ctx=gctx)
            g["q"] = K.sb("g_q", [P, 8, T], ctx=gctx)
            g["k"] = K.sb("g_k", [P, 8, 2 * T], ctx=gctx)
            g["vtok"], g["ktok"] = K.sb("g_vtok", [P, 4, 1024], ctx=gctx), K.sb("g_ktok", [P, 4, 1024], ctx=gctx)
            with ExitStack() as hctx:
                K.hc = K.sb("hc", [P, KD, T], ctx=hctx)
                inputs_stage(K)
                latent_attention_stage(K)
            gdn_stages(K)
        merge_stage(K)
        conv_ffn_stage(K)
        final_norm_stage(K)


def build(nc, a, out):
    K = Kernel(nc, a, out)
    with K.ctx:
        K.open()
        K.first = ExitStack()
        prologue(K)
        K.restart()
        with nc.Fori(0, LAYERS) as l:
            K.plan(layer_slabs(K, l))
            K.col = lambda name, n=1: K.prm[:, PARAM_ROWS[name]:PARAM_ROWS[name] + n]
            ffn_stage(K, "ffn1", K.col("ffn1_norm", KD), l)
            mixer(K, l)
            xattn_stage(K, l)
            ffn_stage(K, "ffn2", K.col("ffn2_norm", KD))
            K.restart()
        K.first.close()
        K.forget()
        second_block(K)
        epilogue(K)


def kernel(**inputs):
    import concourse.bacc as bacc
    from concourse.bass_utils import run_bass_kernel_spmd

    nc = bacc.Bacc("TRN2", target_bir_lowering=False, num_devices=1)
    arrays, a = {}, {}
    for name, value in {**inputs, **{f"consts{i}": c for i, c in enumerate(CONSTS)}}.items():
        value = np.ascontiguousarray(value)
        if value.ndim == 1:
            value = value.reshape(1, -1)
        arrays["in_" + name] = value
        a[name] = nc.dram_tensor("in_" + name, value.shape, mybir.dt.from_np(value.dtype), kind="ExternalInput").ap()
    out = nc.dram_tensor("out", (1, T, D), F32, kind="ExternalOutput").ap()
    build(nc, a, out)
    r = run_bass_kernel_spmd(nc, [arrays], core_ids=[0])
    return r.results[0]["out"]
```
